# Optimizing a Trainium2 kernel written in Bass

```python
import jax, jax.numpy as jnp
from jax import lax
import numpy as np

D_MODEL = 1024
BATCH = 1
SEQ = 512
DEPTH = 2

GROUP_WIDTH = D_MODEL // 4
N_GROUP_HEADS = 4
HEAD_DIM = GROUP_WIDTH // N_GROUP_HEADS
SC_KERNEL = 3
CF_KERNEL = 31
FFN_KERNEL = 3
MOBA_BLOCK = 256
MOBA_TOPK = 3
QUERY_BLOCK = 128
ROPE_THETA = 500000.0
ROPE_DIM = HEAD_DIM // 4
MLA_Q_RANK = 3 * GROUP_WIDTH // 2
MLA_KV_RANK = GROUP_WIDTH // 2
MLA_NOPE_DIM = HEAD_DIM
MLA_ROPE_DIM = HEAD_DIM // 2
MLA_V_DIM = HEAD_DIM
D_FF = ((8 * D_MODEL // 3 + 127) // 128) * 128
EPS = 1e-6
NEG = -1e30

SC_COLS = 3 * GROUP_WIDTH
CF_COLS = 2 * GROUP_WIDTH
MOBA_COLS = 3 * GROUP_WIDTH
MLA_COLS = MLA_Q_RANK + MLA_KV_RANK + MLA_ROPE_DIM
IN_COLS = SC_COLS + CF_COLS + MOBA_COLS + MLA_COLS
SPLITS = (SC_COLS, SC_COLS + CF_COLS, SC_COLS + CF_COLS + MOBA_COLS)
MIX_WIDTH = 4 * GROUP_WIDTH

kernel_name = "hybrid_parallel_conv_moba_mla_block"

def rmsnorm(x, g):
    xf = x.astype(jnp.float32)
    y = xf * lax.rsqrt(jnp.mean(xf * xf, axis=-1, keepdims=True) + EPS)
    return (y * g.astype(jnp.float32)).astype(x.dtype)

def layernorm(x, g, b):
    xf = x.astype(jnp.float32)
    mu = jnp.mean(xf, axis=-1, keepdims=True)
    xc = xf - mu
    y = xc * lax.rsqrt(jnp.mean(xc * xc, axis=-1, keepdims=True) + EPS)
    return (y * g.astype(jnp.float32) + b.astype(jnp.float32)).astype(x.dtype)

def causal_dwconv(x, w):
    k, c = w.shape
    xp = jnp.pad(x, ((0, 0), (k - 1, 0), (0, 0)))
    return lax.conv_general_dilated(xp, w.astype(x.dtype)[:, None, :], (1,), 'VALID',
                                    dimension_numbers=('NWC', 'WIO', 'NWC'),
                                    feature_group_count=c)

def rope_tables(seq, dim):
    inv = 1.0 / (ROPE_THETA ** (jnp.arange(0, dim, 2, dtype=jnp.float32) / dim))
    ang = jnp.arange(seq, dtype=jnp.float32)[:, None] * inv[None, :]
    return jnp.cos(ang), jnp.sin(ang)

def apply_rope(x, cos, sin):
    half = x.shape[-1] // 2
    x1, x2 = x[..., :half], x[..., half:]
    c = cos.astype(x.dtype)
    s = sin.astype(x.dtype)
    return jnp.concatenate([x1 * c - x2 * s, x2 * c + x1 * s], axis=-1)

def merge_chunks(outs):
    nq, b, h, qb, dh = outs.shape
    return jnp.transpose(outs, (1, 0, 3, 2, 4)).reshape(b, nq * qb, h * dh)

def short_conv_mixer(z, w_conv):
    h, b_gate, c_gate = jnp.split(z, 3, axis=-1)
    return b_gate * causal_dwconv(c_gate * h, w_conv)

def conformer_conv_mixer(z, w_conv, b_conv, ln_g, ln_b):
    a, g = jnp.split(z, 2, axis=-1)
    u = a * jax.nn.sigmoid(g)
    u = causal_dwconv(u, w_conv) + b_conv.astype(u.dtype)
    return jax.nn.silu(layernorm(u, ln_g, ln_b))

def moba_attention(z, cos, sin):
    b, s, _ = z.shape
    h, dh = N_GROUP_HEADS, HEAD_DIM
    q, k, v = [t.reshape(b, s, h, dh).transpose(0, 2, 1, 3) for t in jnp.split(z, 3, axis=-1)]
    q = jnp.concatenate([apply_rope(q[..., :ROPE_DIM], cos, sin), q[..., ROPE_DIM:]], axis=-1)
    k = jnp.concatenate([apply_rope(k[..., :ROPE_DIM], cos, sin), k[..., ROPE_DIM:]], axis=-1)
    nb = -(-s // MOBA_BLOCK)
    pad = nb * MOBA_BLOCK - s
    kp = jnp.pad(k, ((0, 0), (0, 0), (0, pad), (0, 0)))
    vp = jnp.pad(v, ((0, 0), (0, 0), (0, pad), (0, 0)))
    kb = kp.reshape(b, h, nb, MOBA_BLOCK, dh)
    vb = vp.reshape(b, h, nb, MOBA_BLOCK, dh)
    kmean = jnp.mean(kb.astype(jnp.float32), axis=3)
    n_sel = min(MOBA_TOPK, nb)
    scale = dh ** -0.5
    bi = jnp.arange(b)[:, None, None, None]
    hi = jnp.arange(h)[None, :, None, None]
    blk_ids = jnp.arange(nb)

    def chunk(c):
        q0 = c * QUERY_BLOCK
        qc = lax.dynamic_slice_in_dim(q, q0, QUERY_BLOCK, axis=2)
        own = q0 // MOBA_BLOCK
        gate = jnp.einsum('bhqd,bhnd->bhqn', qc.astype(jnp.float32), kmean)
        gate = jnp.where(blk_ids < own, gate, -jnp.inf)
        _, idx = lax.top_k(gate, n_sel)
        valid = idx < own
        kg = kb[bi, hi, idx]
        vg = vb[bi, hi, idx]
        s_sel = jnp.einsum('bhqd,bhqnkd->bhqnk', qc, kg).astype(jnp.float32) * scale
        s_sel = jnp.where(valid[..., None], s_sel, NEG)
        k_own = lax.dynamic_slice_in_dim(kp, own * MOBA_BLOCK, MOBA_BLOCK, axis=2)
        v_own = lax.dynamic_slice_in_dim(vp, own * MOBA_BLOCK, MOBA_BLOCK, axis=2)
        s_own = jnp.einsum('bhqd,bhkd->bhqk', qc, k_own).astype(jnp.float32) * scale
        qpos = q0 + jnp.arange(QUERY_BLOCK)
        kpos = own * MOBA_BLOCK + jnp.arange(MOBA_BLOCK)
        s_own = jnp.where(kpos[None, :] <= qpos[:, None], s_own, NEG)
        sc = jnp.concatenate([s_sel.reshape(b, h, QUERY_BLOCK, n_sel * MOBA_BLOCK), s_own], axis=-1)
        p = jax.nn.softmax(sc, axis=-1).astype(v.dtype)
        p_sel = p[..., :n_sel * MOBA_BLOCK].reshape(b, h, QUERY_BLOCK, n_sel, MOBA_BLOCK)
        p_own = p[..., n_sel * MOBA_BLOCK:]
        return (jnp.einsum('bhqnk,bhqnkd->bhqd', p_sel, vg)
                + jnp.einsum('bhqk,bhkd->bhqd', p_own, v_own))

    return merge_chunks(lax.map(chunk, jnp.arange(s // QUERY_BLOCK)))

def mla_attention(z, g_q, g_kv, w_uq, w_ukv, cos, sin):
    b, s, _ = z.shape
    h = N_GROUP_HEADS
    cq, ckv, kr = jnp.split(z, (MLA_Q_RANK, MLA_Q_RANK + MLA_KV_RANK), axis=-1)
    q = (rmsnorm(cq, g_q) @ w_uq).reshape(b, s, h, MLA_NOPE_DIM + MLA_ROPE_DIM).transpose(0, 2, 1, 3)
    q_nope = q[..., :MLA_NOPE_DIM]
    q_rope = apply_rope(q[..., MLA_NOPE_DIM:], cos, sin)
    kv = (rmsnorm(ckv, g_kv) @ w_ukv).reshape(b, s, h, MLA_NOPE_DIM + MLA_V_DIM).transpose(0, 2, 1, 3)
    k_nope = kv[..., :MLA_NOPE_DIM]
    v = kv[..., MLA_NOPE_DIM:]
    k_rope = apply_rope(kr, cos, sin)
    scale = (MLA_NOPE_DIM + MLA_ROPE_DIM) ** -0.5
    kpos = jnp.arange(s)

    def chunk(c):
        q0 = c * QUERY_BLOCK
        qn = lax.dynamic_slice_in_dim(q_nope, q0, QUERY_BLOCK, axis=2)
        qr = lax.dynamic_slice_in_dim(q_rope, q0, QUERY_BLOCK, axis=2)
        sc = (jnp.einsum('bhqd,bhkd->bhqk', qn, k_nope)
              + jnp.einsum('bhqd,bkd->bhqk', qr, k_rope)).astype(jnp.float32) * scale
        qpos = q0 + jnp.arange(QUERY_BLOCK)
        sc = jnp.where(kpos[None, :] <= qpos[:, None], sc, NEG)
        p = jax.nn.softmax(sc, axis=-1).astype(v.dtype)
        return jnp.einsum('bhqk,bhkd->bhqd', p, v)

    return merge_chunks(lax.map(chunk, jnp.arange(s // QUERY_BLOCK)))

def conv_ffn_block(h, w_up, w_conv, w_down):
    u = causal_dwconv(h @ w_up, w_conv)
    g, v = jnp.split(u, 2, axis=-1)
    return (jax.nn.silu(g) * v) @ w_down

def setup_inputs(seed: int = 0) -> dict:
    key = jax.random.key(seed)
    ks = jax.random.split(key, 20)
    f32 = jnp.float32

    def nrm(k, shape, scale):
        return jax.random.normal(k, shape, f32) * scale

    def gain(k, shape):
        return 1.0 + 0.02 * jax.random.normal(k, shape, f32)

    L = DEPTH
    return {
        "x": jax.random.normal(ks[0], (BATCH, SEQ, D_MODEL), f32),
        "norm_mix_pre": gain(ks[1], (L, D_MODEL)),
        "norm_mix_post": gain(ks[2], (L, D_MODEL)),
        "norm_ffn_pre": gain(ks[3], (L, D_MODEL)),
        "norm_ffn_post": gain(ks[4], (L, D_MODEL)),
        "w_in": nrm(ks[5], (L, D_MODEL, IN_COLS), D_MODEL ** -0.5),
        "conv_a": nrm(ks[6], (L, SC_KERNEL, GROUP_WIDTH), SC_KERNEL ** -0.5),
        "conv_b": nrm(ks[7], (L, CF_KERNEL, GROUP_WIDTH), CF_KERNEL ** -0.5),
        "conv_b_bias": nrm(ks[8], (L, GROUP_WIDTH), 0.01),
        "ln_b_gain": gain(ks[9], (L, GROUP_WIDTH)),
        "ln_b_bias": nrm(ks[10], (L, GROUP_WIDTH), 0.01),
        "mla_q_norm": gain(ks[11], (L, MLA_Q_RANK)),
        "mla_kv_norm": gain(ks[12], (L, MLA_KV_RANK)),
        "w_uq": nrm(ks[13], (L, MLA_Q_RANK, N_GROUP_HEADS * (MLA_NOPE_DIM + MLA_ROPE_DIM)), MLA_Q_RANK ** -0.5),
        "w_ukv": nrm(ks[14], (L, MLA_KV_RANK, N_GROUP_HEADS * (MLA_NOPE_DIM + MLA_V_DIM)), MLA_KV_RANK ** -0.5),
        "w_out": nrm(ks[15], (L, MIX_WIDTH, D_MODEL), MIX_WIDTH ** -0.5),
        "w_ffn_up": nrm(ks[16], (L, D_MODEL, 2 * D_FF), D_MODEL ** -0.5),
        "conv_ffn": nrm(ks[17], (L, FFN_KERNEL, 2 * D_FF), FFN_KERNEL ** -0.5),
        "w_ffn_down": nrm(ks[18], (L, D_FF, D_MODEL), D_FF ** -0.5),
    }

def reference(x, norm_mix_pre, norm_mix_post, norm_ffn_pre, norm_ffn_post, w_in,
              conv_a, conv_b, conv_b_bias, ln_b_gain, ln_b_bias, mla_q_norm, mla_kv_norm,
              w_uq, w_ukv, w_out, w_ffn_up, conv_ffn, w_ffn_down):
    seq = x.shape[1]
    cos_c, sin_c = rope_tables(seq, ROPE_DIM)
    cos_d, sin_d = rope_tables(seq, MLA_ROPE_DIM)
    for l in range(DEPTH):
        h = rmsnorm(x, norm_mix_pre[l])
        z = h @ w_in[l]
        z_sc, z_cf, z_moba, z_mla = jnp.split(z, SPLITS, axis=-1)
        y_a = short_conv_mixer(z_sc, conv_a[l])
        y_b = conformer_conv_mixer(z_cf, conv_b[l], conv_b_bias[l], ln_b_gain[l], ln_b_bias[l])
        y_c = moba_attention(z_moba, cos_c, sin_c)
        y_d = mla_attention(z_mla, mla_q_norm[l], mla_kv_norm[l], w_uq[l], w_ukv[l], cos_d, sin_d)
        y = jnp.concatenate([y_a, y_b, y_c, y_d], axis=-1) @ w_out[l]
        x = x + rmsnorm(y, norm_mix_post[l])
        f = conv_ffn_block(rmsnorm(x, norm_ffn_pre[l]), w_ffn_up[l], conv_ffn[l], w_ffn_down[l])
        x = x + rmsnorm(f, norm_ffn_post[l])
    return x


_drawn_inputs = setup_inputs


def setup_inputs(seed=0):
    import zlib

    import numpy as np

    out = dict(_drawn_inputs(seed))
    spreads = {}
    factors = {'norm_ffn_post': 3.274,
     'conv_b_bias': 4.33,
     'ln_b_gain': 10.462,
     'ln_b_bias': 35.045,
     'mla_q_norm': 8.0,
     'mla_kv_norm': 8.0}
    for name, (base, spread) in spreads.items():
        noise = np.random.default_rng([zlib.crc32(name.encode()), seed]).standard_normal(out[name].shape)
        drawn = base * np.exp(spread * noise) if base else spread * noise
        out[name] = __import__('jax').numpy.asarray(drawn.astype(out[name].dtype))
    for name, factor in factors.items():
        out[name] = (out[name] * factor).astype(out[name].dtype)
    return out
```

```python
import concourse.bass as bass
from concourse import mybir
from contextlib import ExitStack

P = 128
T = 512
TC = T // P
D = 1024
KD = D // P
DEPTH = 2
GW = 256
HEADS = 4
DH = 64
MLA_ROPE = 32
MLA_QK = DH + MLA_ROPE
Q_RANK, KV_RANK = 384, 128
D_FF = 2816
NF = D_FF // P
EPS = 1e-6
MASKED = -1e30
MOBA_SCALE = DH ** -0.5
MLA_SCALE = MLA_QK ** -0.5
CF_TAPS, SC_TAPS, FFN_TAPS = 31, 3, 3

SC0 = 0
CF0 = 3 * GW
MB0 = CF0 + 2 * GW
ML0 = MB0 + 3 * GW
KR0 = ML0 + Q_RANK + KV_RANK
IN_COLS = KR0 + MLA_ROPE

SMALL = []
_at = 0
for _name, _rows in (("norm_mix_pre", KD), ("norm_mix_post", KD), ("norm_ffn_pre", KD), ("norm_ffn_post", KD),
                     ("conv_a", SC_TAPS * 2), ("conv_b", CF_TAPS * 2), ("conv_b_bias", 2), ("ln_b_gain", 2),
                     ("ln_b_bias", 2), ("mla_q_norm", 3), ("mla_kv_norm", 1)):
    SMALL.append((_name, _at, _rows))
    _at += _rows
NSMALL = _at
VC = {n: a for n, a, _ in SMALL}
VC["conv_ffn"] = NSMALL
NTAPROWS = FFN_TAPS * 2 * NF
HALFROWS = NTAPROWS // 2
NVEC = NSMALL + NTAPROWS

W_IN_COLS = ([CF0 + GW, CF0, CF0 + GW + P, CF0 + P]
             + [MB0, MB0 + GW, MB0 + P, MB0 + GW + P]
             + [None, None]
             + [ML0 + Q_RANK, KR0 - DH]
             + [ML0, ML0 + P, ML0 + 2 * P]
             + [SC0 + 2 * GW, SC0, SC0 + GW, SC0 + 2 * GW + P, SC0 + P, SC0 + GW + P])
U_VAL = 8
U_KR = 11
U_UQ, U_UKV = 21, 23
U_OUT = 24
U_UP = U_OUT + KD
U_DOWN = U_UP + 2 * NF
DOWN_PARTS = ((0, 8), (8, 8), (16, 6))
NU = U_DOWN + 3 * KD
RAW, SPLIT = 2, 4
LEAD = 3

G_CF, G_QK, G_V, G_CKV, G_KR, G_CQ, G_SC = 0, 4, 8, 10, 11, 12, 15
G_MQ, G_MK, G_MV, G_PV = 21, 25, 29, 31
G_OUT = 39
G_UP = G_OUT + KD
G_DOWN = G_UP + 2 * NF
NG = G_DOWN + KD

STAT, SCORE0, PT_BANKS = 4, 5, (3, 7)


def bank_of(g):
    if G_MQ <= g < G_OUT:
        return (g - G_MQ) % 3
    return {0: g, 1: g - G_OUT, 2: g - G_UP, 3: g - G_DOWN}[(g >= G_OUT) + (g >= G_UP) + (g >= G_DOWN)] % 4


EVENTS = ["pre_mix", "ln", "ckv", "cq", "post_mix", "pre_ffn", "post_ffn"]
SQUARES = dict(pre_mix=KD, ln=2, ckv=1, cq=3, post_mix=KD, pre_ffn=KD, post_ffn=KD)
WIDTH = dict(pre_mix=D, ln=GW, ckv=KV_RANK, cq=Q_RANK, post_mix=D, pre_ffn=D, post_ffn=D)
NEV = len(EVENTS)
NSQ = sum(SQUARES.values())
NADD = sum(n - 1 for n in SQUARES.values())


def squares_before(ev):
    return sum(SQUARES[e] for e in EVENTS[:EVENTS.index(ev)])


def adds_before(ev):
    return sum(SQUARES[e] - 1 for e in EVENTS[:EVENTS.index(ev)])


N_EVAC = G_OUT + 2 * NF
N_YEVAC = 2 * KD
N_XH = 2 * KD
CF_SHARE = {3: 1, 4: 1, 5: 1, 6: 1, 7: 1, 8: 5, 9: 4, 10: 4, 11: 3, 12: 4, 13: 6}
assert sum(CF_SHARE.values()) == CF_TAPS
N_ATT = 2 * HEADS * TC
V_STEPS = 2 + 1 + (CF_TAPS - 1) + (4 + 1 + 2 + HEADS) + 2 * (1 + SC_TAPS) + 2 + N_ATT + 2 * KD + NF * (2 * FFN_TAPS)
ATT_TAIL = 4


def hybrid_trunk_kernel(nc, inp, rope_tables, out):
    f32 = mybir.dt.float32
    f32r = mybir.dt.float32r
    ALU = mybir.AluOpType
    ACT = mybir.ActivationFunctionType

    def fp(ap):
        return ap.bitcast(f32)

    with ExitStack() as ctx:
        sem_names = {}

        def sem(name):
            sem_names[name] = ctx.enter_context(nc.semaphore(name))
            return sem_names[name]

        base = -(-nc.sbuf_base // 32) * 32
        at = [base]

        def place(name, shape, dt, offset=None):
            size = 4
            for n in shape[1:]:
                size *= n
            if offset is None:
                offset = at[0]
                at[0] += -(-size // 32) * 32
            return nc.alloc_sbuf_tensor_at(name, shape, dt, offset=offset)

        x = place("x", [P, KD, T], f32)
        xn_at = at[0]
        xn = place("xn", [P, KD, 2, T], f32r)
        slots_at = at[0]
        hid = place("hid", [P, NF, 2, T], f32r)
        SLOT = 2 * T * 4
        raw = place("raw", [P, RAW, 8 * P], f32)
        wsp = place("wsp", [P, SPLIT, 2, 8 * P], f32r)
        ident = place("ident", [P, P], f32)
        ones = place("ones", [P, P], f32)
        causal = place("causal", [P, T], f32)
        rope = place("rope", [P, 2, T], f32)
        scale_main = place("scale_main", [P, T], f32)
        scale_aux = place("scale_aux", [P, T], f32)
        vec_all = place("vec_all", [P, DEPTH, NVEC], f32)
        vec = place("vec", [P, NVEC], f32)
        var = place("var", [P, TC], f32)
        rstd = place("rstd", [P, TC], f32)
        power = place("power", [P, TC], f32)
        diag = place("diag", [P, TC, P], f32)
        rstd_mix = place("rstd_mix", [P, TC], f32)
        rowmax = place("rowmax", [P, N_ATT], f32)
        negmax = place("negmax", [P, N_ATT], f32)
        rowsum = place("rowsum", [P, N_ATT], f32)
        rowinv = place("rowinv", [P, N_ATT], f32)
        tmp_at = at[0]
        cf_out = place("cf_out", [P, 2, T], f32, tmp_at)
        sc_u = place("sc_u", [P, T + 2], f32, tmp_at + 4096)
        kr = place("kr", [P, 2, T], f32r, tmp_at + 6176)
        sq = place("sq", [P, 2, T], f32, tmp_at + 10336)
        ml_rot = place("ml_rot", [P, 2, T], f32, tmp_at)
        ml_shuf = place("ml_shuf", [P, T], f32, tmp_at + 4096)
        sm = place("sm", [P, 2, T], f32, tmp_at)
        prob = place("prob", [P, 2, T], f32, tmp_at + 4096)
        e_g = place("e_g", [P, T + 2], f32, tmp_at)
        e_v = place("e_v", [P, T + 2], f32, tmp_at + 2080)
        c_g = place("c_g", [P, T], f32, tmp_at + 4160)
        c_v = place("c_v", [P, T], f32, tmp_at + 6208)
        th = place("th", [P, T], f32, tmp_at + 8256)
        assert tmp_at + 10336 + 4096 <= nc.sbuf_usable_end, (tmp_at + 14432, nc.sbuf_usable_end)

        Y_SLOT = dict(a=0, b=2, c=4, d=6)
        QM, KM, VM, VL, CQN, CKVN, PT = 8, 10, 12, 14, 16, 19, 16

        def slot(n):
            return slots_at + n * SLOT

        vm = hid[:, VM:VM + 2, :, :].rearrange("p a b t -> p (a b t)").rearrange("p (s c d) -> p s c d", s=2, c=TC)
        vl = hid[:, VL:VL + 2, :, :].rearrange("p a b t -> p (a b t)").rearrange("p (s c d) -> p s c d", s=2, c=TC)
        pt = hid[:, PT:PT + 4, :, :].rearrange("p a b t -> p (a b) t").rearrange("p (s k) t -> p s k t", s=2)
        cf_u = place("cf_u", [P, 2, T + CF_TAPS - 1], f32, slot(VL))
        sc_w = place("sc_w", [P, T], f32, slot(VL) + 5120)
        mb_rot = place("mb_rot", [P, 2, T], f32, slot(CQN))
        mb_shuf = place("mb_shuf", [P, T], f32, slot(CQN) + 4096)
        cf_tmp = place("cf_tmp", [P, 2, T], f32, slot(CQN + 2))
        lat = place("lat", [P, 4, T], f32, slot(20))
        x_tok = place("x_tok", [P, TC, D], f32, slot(0))
        rows = place("rows", [P, DEPTH, 3, P], f32, slot(4))
        out_tok = place("out_tok", [P, TC, D], f32, slot(0))
        y = place("y", [P, KD, 2, T], f32, xn_at)
        ml_q = [xn[:, h, :, :] for h in range(HEADS)]
        ml_k = [xn[:, HEADS + h, :, :] for h in range(HEADS)]

        ps = ctx.enter_context(nc.psum_tensor("ps", [P, 8, T], f32))

        x_in = [sem(f"x_in{c}") for c in range(TC)]
        rows_in = sem("rows_in")
        ident_set = sem("ident_set")
        rope_in = sem("rope_in")
        raw_in = [sem(f"raw_in{s}") for s in range(RAW)]
        hi_done = sem("hi_done")
        lo_done = sem("lo_done")
        down_part = sem("down_part")
        xt_done = sem("xt_done")
        vt_done = sem("vt_done")
        vec_all_set = sem("vec_all_set")
        vec_set = sem("vec_set")
        x_done = sem("x_done")
        xh_done = sem("xh_done")
        xl_done = sem("xl_done")
        group_done = sem("group_done")
        evac = sem("evac")
        y_evac = sem("y_evac")
        v_step = sem("v_step")
        sq_done = sem("sq_done")
        add_done = sem("add_done")
        stat_done = sem("stat_done")
        var_done = sem("var_done")
        rstd_done = sem("rstd_done")
        diag_done = sem("diag_done")
        spread_done = sem("spread_done")
        scale_done = sem("scale_done")
        cf_tanh = sem("cf_tanh")
        cf_u_set = sem("cf_u_set")
        cf_prod = sem("cf_prod")
        cf_sum = sem("cf_sum")
        cf_conv = sem("cf_conv")
        mean_done = sem("mean_done")
        cf_cent = sem("cf_cent")
        cf_norm = sem("cf_norm")
        cf_swish = sem("cf_swish")
        cf_val = sem("cf_val")
        sc_val = sem("sc_val")
        y_hi = sem("y_hi")
        y_ready = sem("y_ready")
        rot_done = sem("rot_done")
        rot_hi = sem("rot_hi")
        qk_ready = sem("qk_ready")
        val_hi = sem("val_hi")
        lat_done = sem("lat_done")
        lat_norm = sem("lat_norm")
        lat_hi = sem("lat_hi")
        lat_ready = sem("lat_ready")
        kr_done = sem("kr_done")
        kr_hi = sem("kr_hi")
        kr_lo = sem("kr_lo")
        kr_spread = sem("kr_spread")
        kn_hi = sem("kn_hi")
        score_done = sem("score_done")
        masked = sem("masked")
        negmax_done = sem("negmax_done")
        exp_done = sem("exp_done")
        prob_done = sem("prob_done")
        pt_done = sem("pt_done")
        pt_hi = sem("pt_hi")
        pt_ready = sem("pt_ready")
        pv_hi = sem("pv_hi")
        c_gate = sem("c_gate")
        tanh_done = sem("tanh_done")
        f_done = sem("f_done")
        f_hi = sem("f_hi")
        f_ready = sem("f_ready")
        ot_done = sem("ot_done")
        out_set = sem("out_set")
        stored = sem("stored")

        def weight_source(u, l, i=0):
            if u < U_UQ:
                if u in (U_VAL, U_VAL + 1):
                    r0 = (u - U_VAL) * 4 * P
                    v = inp["w_in"][l, r0:r0 + 4 * P, MB0 + 2 * GW:MB0 + 3 * GW]
                    return v.rearrange("(k p) n -> p k n", p=P), 4, 2 * P
                n = P if u != U_KR else MLA_QK
                if W_IN_COLS[u] == 0:
                    l = (l + DEPTH) % DEPTH
                v = inp["w_in"][l, :, W_IN_COLS[u]:W_IN_COLS[u] + n]
                return v.rearrange("(k p) n -> p k n", p=P), KD, n
            if u < U_UKV:
                c0 = (u - U_UQ) * 2 * MLA_QK
                v = inp["w_uq"][l, :, c0:c0 + 2 * MLA_QK]
                return v.rearrange("(k p) n -> p k n", p=P), 3, 2 * MLA_QK
            if u == U_UKV:
                return inp["w_ukv"][l, :, :].rearrange("(k p) n -> p k n", p=P), 1, 2 * GW
            if u < U_UP:
                m = u - U_OUT
                v = inp["w_out"][l, :, m * P:(m + 1) * P]
                return v.rearrange("(k p) n -> p k n", p=P), KD, P
            if u < U_DOWN:
                j = u - U_UP
                v = inp["w_ffn_up"][l, :, bass.ds((j % 2) * D_FF + (j // 2) * P + i * P, P)]
                return v.rearrange("(k p) n -> p k n", p=P), KD, P
            m, part = divmod(u - U_DOWN, 3)
            k0, nk = DOWN_PARTS[part]
            v = inp["w_ffn_down"][l, k0 * P:(k0 + nk) * P, bass.ds(m * P + i * P, P)]
            return v.rearrange("(k p) n -> p k n", p=P), nk, P

        def unit_elements(u):
            if u == U_KR:
                return KD * MLA_QK
            if U_UQ <= u < U_UKV:
                return 3 * 2 * MLA_QK
            return 2 * GW if u == U_UKV else KD * P

        def released(u):
            if u < U_UQ:
                return group_done, (u + 1 if u != U_VAL else u + 2), NG
            if u < U_OUT:
                return group_done, (G_MQ + 2, G_MQ + 4, G_PV)[u - U_UQ], NG
            if u < U_UP:
                return group_done, G_OUT + u - U_OUT + 1, NG
            if u < U_DOWN:
                return group_done, G_UP + u - U_UP + 1, NG
            m, part = divmod(u - U_DOWN, 3)
            return (group_done, G_DOWN + m + 1, NG) if part == 2 else (down_part, 2 * m + part + 1, 2 * KD)

        def weights(u):
            n = {True: 2 * P}.get(u in (U_VAL, U_VAL + 1), P)
            if u == U_KR:
                n = MLA_QK
            if U_UQ <= u < U_UKV:
                n = 2 * MLA_QK
            if u == U_UKV:
                n = 2 * GW
            nk = unit_elements(u) // n
            return wsp[:, u % SPLIT, :, 0:nk * n].rearrange("p s (k n) -> p s k n", n=n)

        def split_hi(act, u, l, i=0, per=0, first=False):
            n = unit_elements(u % NU)
            act.wait_ge(raw_in[u % RAW], l * (NU // RAW * 16) + i * (per // RAW * 16) + 16 * (u // RAW + 1))
            if not first and u >= SPLIT:
                s, count, step = released(u - SPLIT)
                act.wait_ge(s, l * step + i * (per if s is group_done else 2 * per // 3) + count)
            act.activation(wsp[:, u % SPLIT, 0, 0:n], raw[:, u % RAW, 0:n], ACT.Copy).then_inc(hi_done, 1)

        def split_lo(dve, u, l, i=0, per=0):
            n = unit_elements(u % NU)
            dve.wait_ge(hi_done, l * NU + i * per + u + 1)
            dve.tensor_tensor(wsp[:, u % SPLIT, 1, 0:n], raw[:, u % RAW, 0:n], fp(wsp[:, u % SPLIT, 0, 0:n]),
                              ALU.subtract).then_inc(lo_done, 1)

        def col(name, c=0):
            a = VC[name] + c
            return vec[:, a:a + 1]

        block = ctx.enter_context(nc.Block())

        @block.sync
        def _(sp):
            def load(u, l, i=0, per=0, wait=True):
                if wait:
                    sp.wait_ge(lo_done, l * NU + i * per + u - 1)
                src, nk, n = weight_source(u % NU, l if u < NU else (l + 1) % DEPTH, i)
                dst = raw[:, u % RAW, 0:nk * n].rearrange("p (k n) -> p k n", n=n)
                sp.dma_start(dst, src).then_inc(raw_in[u % RAW], 16)

            for c in range(TC):
                sp.dma_start(x_tok[:, c, :], inp["x"][0, c * P:(c + 1) * P, :]).then_inc(x_in[c], 16)
            load(0, 0, wait=False)
            load(1, 0, wait=False)
            load(2, 0)
            with sp.Fori(0, DEPTH) as l:
                for u in range(LEAD, U_UP):
                    load(u, l)
                with sp.Fori(0, NF // 2) as i:
                    for j in range(4):
                        u = U_UP + j
                        sp_u = l * NU + i * 4 + u - 1
                        src, nk, n = weight_source(u, l, i * 2)
                        dst = raw[:, u % RAW, 0:nk * n].rearrange("p (k n) -> p k n", n=n)
                        sp.wait_ge(raw_in[u % RAW], 16)
                        sp.wait_ge(lo_done, sp_u)
                        sp.dma_start(dst, src).then_inc(raw_in[u % RAW], 16)
                with sp.Fori(0, 2) as i:
                    for j in range(12):
                        u = U_DOWN + j
                        sp_u = l * NU + i * 12 + u - 1
                        src, nk, n = weight_source(u, l, i * 4)
                        dst = raw[:, u % RAW, 0:nk * n].rearrange("p (k n) -> p k n", n=n)
                        sp.wait_ge(raw_in[u % RAW], 16)
                        sp.wait_ge(lo_done, sp_u)
                        sp.dma_start(dst, src).then_inc(raw_in[u % RAW], 16)
                for u in range(NU, NU + LEAD):
                    load(u, l)
            out_v = out[0, :, :].rearrange("(c p) f -> p c f", p=P)
            for k in range(KD):
                sp.wait_ge(out_set, k + 1)
                sp.dma_start(out_v[:, :, k * P:(k + 1) * P], out_tok[:, :, k * P:(k + 1) * P]).then_inc(stored, 16)
            sp.wait_ge(rope_in, 16 * (2 * DEPTH + 1))
            sp.wait_ge(stored, 16 * KD)

        @block.tensor
        def _(pe):
            def product(dst, a, b, start, stop):
                pe.matmul(dst, a[0], b[0], start=start, stop=False, skip_group_check=True)
                pe.matmul(dst, a[0], b[1], start=False, stop=False, skip_group_check=True)
                return pe.matmul(dst, a[1], b[0], start=False, stop=stop, skip_group_check=True)

            def weights_ready(u, l, i=0, per=0):
                pe.wait_ge(lo_done, l * NU + i * per + u + 1)

            def dense(g, u, bank, rhs, l, m=P, c0=0):
                w = weights(u)
                nk = len(rhs)
                for k in range(nk):
                    last = product(ps[0:m, bank, :], (w[:, 0, k, c0:c0 + m], w[:, 1, k, c0:c0 + m]), rhs[k],
                                   k == 0, k == nk - 1)
                last.then_inc(group_done, 1)

            def pair(tile, rows_=slice(0, P)):
                return tile[rows_, 0, :], tile[rows_, 1, :]

            x_pairs = [(xn[:, k, 0, :], xn[:, k, 1, :]) for k in range(KD)]

            def bank_free(l, count):
                pe.wait_ge(evac, l * N_EVAC + count)

            def stat(ev, l):
                n, e = SQUARES[ev], EVENTS.index(ev)
                if n > 1:
                    pe.wait_ge(add_done, l * NADD + adds_before(ev) + n - 1)
                else:
                    pe.wait_ge(sq_done, l * NSQ + squares_before(ev) + n)
                if e:
                    pe.wait_ge(scale_done, l * NEV + e)
                for c in range(TC):
                    last = pe.matmul(ps[:, STAT, c:c + 1], sq[:, 0, c * P:(c + 1) * P], ones[:, 0:1],
                                     start=True, stop=True)
                last.then_inc(stat_done, 1)

            def spread(ev, l):
                pe.wait_ge(diag_done, l * NEV + EVENTS.index(ev) + 1)
                pe.matmul(ps[:, STAT, :], ones[:, :], diag[:, :, :].rearrange("p c t -> p (c t)"),
                          start=True, stop=True).then_inc(spread_done, 1)

            def together(units, groups, l, ready):
                for u in units:
                    weights_ready(u, l)
                for k in range(KD):
                    ready(k)
                    for u, g in zip(units, groups):
                        w = weights(u)
                        last = product(ps[:, bank_of(g), :], (w[:, 0, k, :], w[:, 1, k, :]), x_pairs[k],
                                       k == 0, k == KD - 1)
                        if k == KD - 1:
                            last.then_inc(group_done, 1)

            pe.wait_ge(ident_set, 6)
            for k in range(KD):
                if k >= 4:
                    pe.wait_ge(x_done, k - 3)
                for c in range(TC):
                    if k == 0:
                        pe.wait_ge(x_in[c], 16)
                    last = pe.transpose(ps[:, k % 4, c * P:(c + 1) * P], x_tok[:, c, k * P:(k + 1) * P], ident[:, :])
                last.then_inc(xt_done, 1)
            pe.wait_ge(rows_in, 16 * (len(SMALL) + 2))
            for l0 in range(DEPTH):
                for t, (n, c0) in enumerate(((NSMALL, 0), (HALFROWS, NSMALL), (HALFROWS, NSMALL + HALFROWS))):
                    last = pe.transpose(ps[:, 5 + l0, c0:c0 + n], rows[0:n, l0, t, :], ident[0:n, 0:n])
                last.then_inc(vt_done, 1)

            with pe.Fori(0, DEPTH) as l:
                together([0, 1, 2], [0, 1, 2], l, lambda k: pe.wait_ge(xl_done, l * N_XH + k + 1))
                weights_ready(3, l)
                dense(3, 3, 3, x_pairs, l)
                stat("pre_mix", l)
                spread("pre_mix", l)
                for g in range(4, G_MQ):
                    if g in (G_V, G_V + 1):
                        weights_ready(U_VAL + 1, l)
                        bank_free(l, g - 3)
                        for h in range(2):
                            c = 2 * (g - G_V) + h
                            for k in range(KD):
                                w = weights(U_VAL + k // 4)
                                xk = [xn[:, k, s, c * P:(c + 1) * P] for s in range(2)]
                                last = product(ps[:, bank_of(g), h * GW:(h + 1) * GW], xk,
                                               (w[:, 0, k % 4, :], w[:, 1, k % 4, :]), k == 0, k == KD - 1)
                        last.then_inc(group_done, 1)
                    else:
                        weights_ready(g, l)
                        bank_free(l, g - 3)
                        dense(g, g, bank_of(g), x_pairs, l, m=MLA_QK if g == G_KR else P)
                    if g == 13:
                        pe.wait_ge(cf_conv, l + 1)
                        pe.wait_ge(cf_sum, (l + 1) * (CF_TAPS - 1))
                        pe.wait_ge(scale_done, l * NEV + 1)
                        for c in range(2):
                            last = pe.matmul(ps[:, STAT, :], ones[:, :], cf_out[:, c, :], start=c == 0, stop=c == 1)
                        last.then_inc(mean_done, 1)
                    if g == 14:
                        stat("ln", l)
                    if g == 15:
                        spread("ln", l)
                    if g == 16:
                        stat("ckv", l)
                    if g == 17:
                        spread("ckv", l)
                    if g == 18:
                        stat("cq", l)
                    if g == 19:
                        spread("cq", l)
                def projection_bank(g):
                    bank_free(l, g - 2 if g - G_MQ >= 3 else G_MQ)

                pe.wait_ge(lat_ready, l * 4 + 4)
                for h in range(HEADS):
                    g = G_MQ + h
                    weights_ready(U_UQ + h // 2, l)
                    projection_bank(g)
                    dense(g, U_UQ + h // 2, bank_of(g), [pair(hid[:, CQN + j]) for j in range(3)], l,
                          m=MLA_QK, c0=(h % 2) * MLA_QK)
                weights_ready(U_UKV, l)
                for h in range(HEADS):
                    g = G_MK + h
                    projection_bank(g)
                    dense(g, U_UKV, bank_of(g), [pair(hid[:, CKVN])], l, m=P, c0=h * P)
                wkv = weights(U_UKV)[:, :, 0, :].rearrange("p s (h n) -> p s h n", h=HEADS)
                for half in range(2):
                    g = G_MV + half
                    projection_bank(g)
                    for j in range(2):
                        c = 2 * half + j
                        last = product(ps[:, bank_of(g), j * GW:(j + 1) * GW],
                                       [hid[:, CKVN, s, c * P:(c + 1) * P] for s in range(2)],
                                       [wkv[:, s, :, DH:2 * DH] for s in range(2)], True, True)
                    last.then_inc(group_done, 1)

                def scores(t):
                    h, c = divmod(t, TC)
                    if t >= 2:
                        pe.wait_ge(masked, l * N_ATT + t - 1)
                    if h < HEADS:
                        r0 = DH * (h % 2)
                        q, k = hid[:, QM + h // 2], hid[:, KM + h // 2]
                        r = slice(r0, r0 + DH)
                    else:
                        if c == 0:
                            pe.wait_ge(qk_ready, l * 8 + 8)
                            bank_free(l, G_PV)
                            pe.wait_ge(kr_spread, l * 2 + 2)
                        q, k = ml_q[h - HEADS], ml_k[h - HEADS]
                        r = slice(0, MLA_QK)
                    n = (c + 1) * P
                    product(ps[:, SCORE0 + t % 2, 0:n], (q[r, 0, c * P:n], q[r, 1, c * P:n]),
                            (k[r, 0, 0:n], k[r, 1, 0:n]), True, True).then_inc(score_done, 1)

                def transposes(t):
                    c = t % TC
                    pe.wait_ge(prob_done, l * N_ATT + t + 1)
                    if t >= 2:
                        pe.wait_ge(pt_ready, l * N_ATT + t - 1)
                    for kc in range(c + 1):
                        last = pe.transpose(ps[:, PT_BANKS[t % 2], kc * P:(kc + 1) * P],
                                            prob[:, t % 2, kc * P:(kc + 1) * P], ident[:, :])
                    last.then_inc(pt_done, 1)

                def values(h):
                    g = G_PV + h
                    pe.wait_ge(pt_ready, l * N_ATT + TC * h + TC)
                    projection_bank(g)
                    v = vm if h < HEADS else vl
                    c0 = (h % HEADS) // 2 * P
                    for kc in range(TC):
                        last = product(ps[:, bank_of(g), kc * P:T], [v[:, s, kc, c0:c0 + P] for s in range(2)],
                                       [pt[:, s, kc, kc * P:T] for s in range(2)], kc == 0, kc == TC - 1)
                    last.then_inc(group_done, 1)

                pe.wait_ge(qk_ready, l * 8 + 4)
                for t in range(N_ATT + ATT_TAIL):
                    if t < N_ATT:
                        scores(t)
                    if 2 <= t < N_ATT + 2:
                        transposes(t - 2)
                    if t >= 6 and (t - 6) % TC == 0 and t < N_ATT + 3:
                        values((t - 6) // TC)

                pe.wait_ge(y_ready, l * 4 + 4)
                bank_free(l, G_OUT)
                for m in range(KD):
                    weights_ready(U_OUT + m, l)
                    if m >= 4:
                        pe.wait_ge(y_evac, l * N_YEVAC + m - 3)
                    dense(G_OUT + m, U_OUT + m, m % 4, [pair(hid[:, k]) for k in range(KD)], l)
                stat("post_mix", l)
                spread("post_mix", l)

                pe.wait_ge(y_evac, l * N_YEVAC + KD)
                together([U_UP, U_UP + 1, U_UP + 2], [G_UP, G_UP + 1, G_UP + 2], l,
                         lambda k: pe.wait_ge(xl_done, l * N_XH + KD + k + 1))
                weights_ready(U_UP + 3, l)
                dense(G_UP + 3, U_UP + 3, 3, x_pairs, l)
                stat("pre_ffn", l)
                spread("pre_ffn", l)
                with pe.Fori(1, NF // 2) as i:
                    for j in range(4):
                        pe.wait_ge(lo_done, l * NU + i * 4 + U_UP + j + 1)
                        pe.wait_ge(evac, l * N_EVAC + i * 4 + G_OUT + j - 3)
                        dense(G_UP + j, U_UP + j, j, x_pairs, l)

                with pe.Fori(0, 2) as i:
                    for j in range(12):
                        m, part = divmod(j, 3)
                        k0, nk = DOWN_PARTS[part]
                        pe.wait_ge(lo_done, l * NU + i * 12 + U_DOWN + j + 1)
                        if part == 0:
                            pe.wait_ge(y_evac, l * N_YEVAC + i * 4 + KD + m - 3)
                            bank_free(l, N_EVAC)
                        pe.wait_ge(f_ready, l * NF + k0 + nk)
                        w = weights(U_DOWN + j)
                        for k in range(nk):
                            last = product(ps[:, m, :], (w[:, 0, k, :], w[:, 1, k, :]), pair(hid[:, k0 + k]),
                                           k0 + k == 0, k0 + k == NF - 1)
                        last.then_inc(group_done if part == 2 else down_part, 1)
                stat("post_ffn", l)
                spread("post_ffn", l)

            for k in range(KD):
                pe.wait_ge(x_done, KD + (DEPTH * 2 - 1) * KD + k + 1)
                if k >= 4:
                    pe.wait_ge(out_set, k - 3)
                for c in range(TC):
                    last = pe.transpose(ps[:, k % 4, c * P:(c + 1) * P], x[:, k, c * P:(c + 1) * P], ident[:, :])
                last.then_inc(ot_done, 1)

        @block.gpsimd
        def _(pool):
            pool.memset(ident[:, :], 0.0).then_inc(ident_set, 1)
            pool.memset(causal[:, :], 0.0).then_inc(ident_set, 1)
            pool.memset(ones[:, :], 1.0).then_inc(ident_set, 1)
            pool.wait_ge(ident_set, 3)
            pool.affine_select(out=ident[:, :], in_=ident[:, :], compare_op=ALU.not_equal, fill=1.0, base=0,
                               pattern=[[-1, P]], channel_multiplier=1).then_inc(ident_set, 1)
            pool.affine_select(out=causal[:, T - P:T], in_=causal[:, T - P:T], compare_op=ALU.is_ge, fill=MASKED,
                               base=0, pattern=[[-1, P]], channel_multiplier=1).then_inc(ident_set, 1)
            pool.memset(power[:, :], -0.5).then_inc(ident_set, 1)

            def sums(ev, l):
                for k in range(1, SQUARES[ev]):
                    pool.wait_ge(sq_done, l * NSQ + squares_before(ev) + k + 1)
                    if k > 1:
                        pool.wait_ge(add_done, l * NADD + adds_before(ev) + k - 1)
                    pool.tensor_tensor(sq[:, 0, :], sq[:, 0, :], sq[:, 1, :], ALU.add).then_inc(add_done, 1)
                pool.wait_ge(var_done, l * NEV + EVENTS.index(ev) + 1)
                pool.tensor_tensor(rstd[:, :], var[:, :], power[:, :], ALU.pow).then_inc(rstd_done, 1)

            pool.wait_ge(ident_set, 6)
            with pool.Fori(0, DEPTH) as l:
                sums("pre_mix", l)
                for j in range(1, CF_TAPS):
                    pool.wait_ge(cf_prod, l * CF_TAPS + j + 1)
                    if j > 1:
                        pool.wait_ge(cf_sum, l * (CF_TAPS - 1) + j - 1)
                    pool.tensor_tensor(cf_out[:, 1, :], cf_out[:, 1, :], cf_tmp[:, j % 2, :], ALU.add)\
                        .then_inc(cf_sum, 1)
                sums("ln", l)
                sums("ckv", l)
                sums("cq", l)
                sums("post_mix", l)
                sums("pre_ffn", l)
                sums("post_ffn", l)

        @block.vector
        def _(dve):
            class Steps:
                n, base = 0, 0

                def mark(self, ins):
                    ins.then_inc(v_step, 1)
                    self.n += 1

                def wait(self):
                    dve.wait_ge(v_step, self.base + self.n)

            st = Steps()

            for k in range(KD):
                dve.wait_ge(xt_done, k + 1)
                dve.tensor_copy(x[:, k, :], ps[:, k % 4, :]).then_inc(x_done, 1)
            for l0 in range(DEPTH):
                dve.wait_ge(vt_done, l0 + 1)
                dve.tensor_copy(vec_all[:, l0, :], ps[:, 5 + l0, 0:NVEC]).then_inc(vec_all_set, 1)
            for u in range(LEAD):
                split_lo(dve, u, 0)

            def event_var(ev, l):
                dve.wait_ge(stat_done, l * NEV + EVENTS.index(ev) + 1)
                dve.tensor_scalar(var[:, :], ps[:, STAT, 0:TC], 1.0 / WIDTH[ev], EPS, ALU.mult, ALU.add)\
                   .then_inc(var_done, 1)

            def event_diag(ev, l):
                dve.wait_ge(rstd_done, l * NEV + EVENTS.index(ev) + 1)
                dve.tensor_tensor(diag[:, :, :], ident[:, :].unsqueeze(1).to_broadcast([P, TC, P]),
                                  rstd[:, :].unsqueeze(2).to_broadcast([P, TC, P]), ALU.mult)\
                   .then_inc(diag_done, 1)

            def scale_ready(ev, l):
                dve.wait_ge(scale_done, l * NEV + EVENTS.index(ev) + 1)

            def group_ready(g, l):
                dve.wait_ge(group_done, l * NG + g + 1)

            def normed_lo(name, k, n, l):
                dve.wait_ge(xh_done, l * N_XH + n + 1)
                dve.scalar_tensor_tensor(xn[:, k, 1, :], x[:, k, :], col(name, k), fp(xn[:, k, 0, :]),
                                         ALU.mult, ALU.subtract).then_inc(xl_done, 1)

            def own(s, count):
                dve.wait_ge(s, count)

            with dve.Fori(0, DEPTH) as l:
                st.base, st.n = l * V_STEPS, 0
                dve.wait_ge(vec_all_set, 2)
                dve.tensor_copy(vec[:, :], vec_all[:, l, :]).then_inc(vec_set, 1)
                dve.memset(cf_u[:, :, 0:CF_TAPS - 1], 0.0)
                st.mark(dve.memset(sc_u[:, 0:SC_TAPS - 1], 0.0))
                own(vec_set, l + 1)
                for k in range(KD):
                    normed_lo("norm_mix_pre", k, k, l)
                split_lo(dve, 3, l)
                event_var("pre_mix", l)
                dve.wait_ge(rstd_done, l * NEV + 1)
                dve.tensor_copy(rstd_mix[:, :], rstd[:, :])
                event_diag("pre_mix", l)
                scale_ready("pre_mix", l)

                def ev_count(g):
                    return l * N_EVAC + g + 1

                def scaled(dst, g, rows_=slice(0, P)):
                    dve.tensor_tensor(dst, ps[rows_, bank_of(g), :], scale_main[rows_, :], ALU.mult)\
                       .then_inc(evac, 1)
                    own(evac, ev_count(g))

                def rotate(e, shuf, half, rows_, g):
                    mask = [(j + half) % (2 * half) if j < 2 * half else j for j in range(32)]
                    src = ps[rows_, bank_of(g), :]
                    dve.tensor_tensor(e, src, rope[rows_, 0, :], ALU.mult)
                    dve.stream_shuffle(shuf, src, mask).then_inc(evac, 1)
                    own(evac, ev_count(g))
                    st.mark(dve.tensor_tensor(shuf, shuf, rope[rows_, 1, :], ALU.mult))
                    st.wait()
                    return dve.tensor_tensor(e, e, shuf, ALU.add)

                def rot_lo(n):
                    dve.wait_ge(rot_hi, l * 8 + n + 1)
                    if n < 4:
                        dst, e = hid[:, (QM, KM, QM + 1, KM + 1)[n]], mb_rot[:, n % 2, :]
                    else:
                        dst, e = xn[0:MLA_QK, n - 4], ml_rot[0:MLA_QK, n % 2, :]
                    dve.tensor_tensor(dst[:, 1, :], e, fp(dst[:, 0, :]), ALU.subtract).then_inc(qk_ready, 1)

                cf_j = 0
                for g in range(G_MQ):
                    if g >= 1:
                        split_lo(dve, g + LEAD, l)
                    if 5 <= g <= 8:
                        if g == 8:
                            rot_lo(3)
                    if g == 12:
                        dve.wait_ge(kr_hi, l + 1)
                        dve.tensor_tensor(kr[DH:MLA_QK, 1, :], mb_rot[DH:MLA_QK, 0, :], fp(kr[DH:MLA_QK, 0, :]),
                                          ALU.subtract).then_inc(kr_lo, 1)
                    if g == 18:
                        for n, c in ((0, 0), (1, 1)):
                            dve.wait_ge(y_hi, l * 4 + n + 1)
                            dst = hid[:, Y_SLOT["b"] + c]
                            dve.scalar_tensor_tensor(dst[:, 1, :], cf_out[:, c, :], 0.5, fp(dst[:, 0, :]),
                                                     ALU.mult, ALU.subtract).then_inc(y_ready, 1)
                        dve.wait_ge(y_hi, l * 4 + 3)
                        dst = hid[:, Y_SLOT["a"]]
                        dve.tensor_tensor(dst[:, 1, :], sc_w[:, :], fp(dst[:, 0, :]), ALU.subtract)\
                           .then_inc(y_ready, 1)
                    if g == 19:
                        dve.wait_ge(lat_hi, l * 4 + 1)
                        dst = hid[:, CKVN]
                        dve.scalar_tensor_tensor(dst[:, 1, :], lat[:, 3, :], col("mla_kv_norm"), fp(dst[:, 0, :]),
                                                 ALU.mult, ALU.subtract).then_inc(lat_ready, 1)
                    if g == 20:
                        scale_ready("cq", l)
                        for j in range(3):
                            dve.tensor_tensor(lat[:, j, :], lat[:, j, :], scale_aux[:, :], ALU.mult)\
                               .then_inc(lat_norm, 1)
                        for j in range(3):
                            dve.wait_ge(lat_hi, l * 4 + j + 2)
                            dst = hid[:, CQN + j]
                            dve.scalar_tensor_tensor(dst[:, 1, :], lat[:, j, :], col("mla_q_norm", j),
                                                     fp(dst[:, 0, :]), ALU.mult, ALU.subtract)\
                               .then_inc(lat_ready, 1)
                    group_ready(g, l)
                    if g in (0, 2):
                        scaled(mb_rot[:, g // 2, :], g)
                    elif g in (1, 3):
                        c = g // 2
                        u = cf_u[:, c, CF_TAPS - 1:]
                        dve.scalar_tensor_tensor(u, ps[:, bank_of(g), :], 0.5, scale_main[:, :], ALU.mult,
                                                 ALU.mult).then_inc(evac, 1)
                        dve.wait_ge(cf_tanh, l * 2 + c + 1)
                        own(evac, ev_count(g))
                        ins = dve.scalar_tensor_tensor(u, mb_rot[:, c, :], 1.0, u, ALU.add, ALU.mult)
                        if c:
                            ins.then_inc(cf_u_set, 1)
                        else:
                            st.mark(ins)
                    elif G_QK <= g < G_V:
                        n = g - G_QK
                        if n == 0:
                            dve.wait_ge(rope_in, l * 32 + 16)
                            st.mark(dve.tensor_tensor(rope[:, :, :], rope[:, :, :],
                                                      scale_main[:, :].unsqueeze(1).to_broadcast([P, 2, T]),
                                                      ALU.mult))
                            st.wait()
                        if n == 1:
                            own(rot_done, l * 8 + 1)
                        if n >= 2:
                            own(qk_ready, l * 8 + n - 1)
                        rotate(mb_rot[:, n % 2, :], mb_shuf[:, :], 8, slice(0, P), g).then_inc(rot_done, 1)
                        if n:
                            rot_lo(n - 1)
                    elif g in (G_V, G_V + 1):
                        for j in range(2):
                            c = 2 * (g - G_V) + j
                            dve.wait_ge(val_hi, l * 6 + 2 * (g - G_V) + 2)
                            ins = dve.scalar_tensor_tensor(vm[:, 1, c, :], ps[:, bank_of(g), j * GW:(j + 1) * GW],
                                                           rstd_mix[:, c:c + 1], fp(vm[:, 0, c, :]),
                                                           ALU.mult, ALU.subtract)
                            if j:
                                ins.then_inc(evac, 1)
                    elif g == G_CKV:
                        scaled(lat[:, 3, :], g)
                    elif g == G_KR:
                        r = slice(DH, MLA_QK)
                        dve.wait_ge(rope_in, l * 32 + 32)
                        own(qk_ready, l * 8 + 4)
                        st.mark(rotate(mb_rot[r, 0, :], mb_shuf[r, :], 16, r, g))
                        st.wait()
                        dve.tensor_tensor(mb_rot[r, 0, :], mb_rot[r, 0, :], scale_main[r, :], ALU.mult)\
                           .then_inc(kr_done, 1)
                    elif g < G_SC:
                        scaled(lat[:, g - G_CQ, :], g)
                    else:
                        c, kind = divmod(g - G_SC, 3)
                        if kind == 0:
                            if c:
                                own(y_ready, l * 4 + 3)
                            scaled(sc_w[:, :], g)
                        elif kind == 1:
                            scaled(sc_u[:, SC_TAPS - 1:], g)
                            st.mark(dve.tensor_tensor(sc_u[:, SC_TAPS - 1:], sc_u[:, SC_TAPS - 1:], sc_w[:, :],
                                                      ALU.mult))
                            st.wait()
                            st.mark(dve.tensor_scalar(sc_w[:, :], sc_u[:, 0:T], col("conv_a", c), None, ALU.mult))
                            for j in range(1, SC_TAPS):
                                st.wait()
                                st.mark(dve.scalar_tensor_tensor(sc_w[:, :], sc_u[:, j:j + T],
                                                                 col("conv_a", 2 * j + c), sc_w[:, :],
                                                                 ALU.mult, ALU.add))
                        else:
                            st.wait()
                            scaled(sc_u[:, SC_TAPS - 1:], g)
                            dve.tensor_tensor(sc_w[:, :], sc_w[:, :], sc_u[:, SC_TAPS - 1:], ALU.mult)\
                               .then_inc(sc_val, 1)
                    for _ in range(CF_SHARE.get(g, 0)):
                        st.wait()
                        j, cf_j = cf_j, cf_j + 1
                        if j == 0:
                            ins = dve.tensor_scalar(cf_out[:, 0, :], cf_u[:, 0, 0:T], col("conv_b", 0),
                                                    col("conv_b_bias", 0), ALU.mult, ALU.add)
                        else:
                            ins = dve.scalar_tensor_tensor(cf_out[:, 0, :], cf_u[:, 0, j:j + T],
                                                           col("conv_b", 2 * j), cf_out[:, 0, :],
                                                           ALU.mult, ALU.add)
                        if j == CF_TAPS - 1:
                            ins.then_inc(cf_conv, 1)
                        else:
                            st.mark(ins)
                    if g == 14:
                        dve.wait_ge(mean_done, l + 1)
                        for c in range(2):
                            dve.scalar_tensor_tensor(cf_out[:, c, :], ps[:, STAT, :], -1.0 / GW, cf_out[:, c, :],
                                                     ALU.mult, ALU.add).then_inc(cf_cent, 1)
                    if g in (15, 17, 19):
                        ev = {15: "ln", 17: "ckv", 19: "cq"}[g]
                        event_var(ev, l)
                        event_diag(ev, l)
                    if g == 16:
                        scale_ready("ln", l)
                        for c in range(2):
                            st.mark(dve.tensor_tensor(cf_out[:, c, :], cf_out[:, c, :], scale_aux[:, :], ALU.mult))
                        st.wait()
                        for c in range(2):
                            dve.tensor_scalar(cf_out[:, c, :], cf_out[:, c, :], col("ln_b_gain", c),
                                              col("ln_b_bias", c), ALU.mult, ALU.add).then_inc(cf_norm, 1)
                    if g == 17:
                        for c in range(2):
                            dve.wait_ge(cf_swish, l * 2 + c + 1)
                            dve.scalar_tensor_tensor(cf_out[:, c, :], mb_rot[:, c, :], 1.0, cf_out[:, c, :],
                                                     ALU.add, ALU.mult).then_inc(cf_val, 1)
                    if g == 18:
                        scale_ready("ckv", l)
                        dve.tensor_tensor(lat[:, 3, :], lat[:, 3, :], scale_aux[:, :], ALU.mult)\
                           .then_inc(lat_norm, 1)

                for h in range(HEADS):
                    g, n = G_MQ + h, 4 + h
                    r = slice(0, MLA_QK)
                    if h == 0:
                        own(sc_val, l * 2 + 2)
                    elif h == 1:
                        own(y_ready, l * 4 + 4)
                    else:
                        own(qk_ready, l * 8 + n - 1)
                    group_ready(g, l)
                    rotate(ml_rot[r, n % 2, :], ml_shuf[r, :], 16, r, g)\
                        .then_inc(rot_done, 1)
                    if h == 0:
                        dve.wait_ge(y_hi, l * 4 + 4)
                        dst = hid[:, Y_SLOT["a"] + 1]
                        dve.tensor_tensor(dst[:, 1, :], sc_w[:, :], fp(dst[:, 0, :]), ALU.subtract)\
                           .then_inc(y_ready, 1)
                    else:
                        rot_lo(n - 1)
                rot_lo(7)
                for h in range(HEADS):
                    g = G_MK + h
                    dve.wait_ge(kn_hi, l * 4 + h + 1)
                    dve.tensor_tensor(ml_k[h][0:DH, 1, :], ps[0:DH, bank_of(g), :], fp(ml_k[h][0:DH, 0, :]),
                                      ALU.subtract).then_inc(evac, 1)
                for half in range(2):
                    g = G_MV + half
                    dve.wait_ge(val_hi, l * 6 + 5 + half)
                    dve.tensor_tensor(vl[:, 1, 2 * half:2 * half + 2, :],
                                      ps[:, bank_of(g), :].rearrange("p (c d) -> p c d", c=2),
                                      fp(vl[:, 0, 2 * half:2 * half + 2, :]), ALU.subtract).then_inc(evac, 1)

                def head_rows(h):
                    return slice(DH * (h % 2), DH * (h % 2) + DH)

                for t in range(N_ATT + ATT_TAIL):
                    if t < N_ATT:
                        c = t % TC
                        n = (c + 1) * P
                        dve.wait_ge(ident_set, 6)
                        dve.wait_ge(score_done, l * N_ATT + t + 1)
                        if t >= 2:
                            dve.wait_ge(exp_done, l * N_ATT + t - 1)
                        if t == 0:
                            own(evac, l * N_EVAC + G_PV)
                        dve.memset(negmax[:, t:t + 1], 0.0)
                        dve.tensor_tensor_reduce(out=sm[:, t % 2, 0:n], in0=ps[:, SCORE0 + t % 2, 0:n],
                                                 in1=causal[:, T - n:T], scale=1.0, scalar=-3e38,
                                                 op0=ALU.add, op1=ALU.max, accum_out=rowmax[:, t:t + 1])\
                           .then_inc(masked, 1)
                        own(masked, l * N_ATT + t + 1)
                        dve.tensor_scalar(negmax[:, t:t + 1], rowmax[:, t:t + 1],
                                          -(MOBA_SCALE if t < N_ATT // 2 else MLA_SCALE), None, ALU.mult)\
                           .then_inc(negmax_done, 1)
                    if 1 <= t <= N_ATT:
                        s = t - 1
                        n = (s % TC + 1) * P
                        dve.wait_ge(exp_done, l * N_ATT + s + 1)
                        st.mark(dve.reciprocal(rowinv[:, s:s + 1], rowsum[:, s:s + 1]))
                        st.wait()
                        dve.tensor_scalar(prob[:, s % 2, 0:n], prob[:, s % 2, 0:n], rowinv[:, s:s + 1], None,
                                          ALU.mult).then_inc(prob_done, 1)
                    if 2 <= t < N_ATT + 2:
                        s = t - 2
                        c = s % TC
                        dve.wait_ge(pt_hi, l * N_ATT + s + 1)
                        src = ps[:, PT_BANKS[s % 2], 0:(c + 1) * P].rearrange("p (k t) -> p k t", t=P)
                        dve.tensor_tensor(pt[:, 1, 0:c + 1, c * P:(c + 1) * P], src,
                                          fp(pt[:, 0, 0:c + 1, c * P:(c + 1) * P]), ALU.subtract)\
                           .then_inc(pt_ready, 1)
                    if t in (2, 4, 6):
                        split_lo(dve, U_OUT + t // 2 - 1, l)
                    if t >= 7 and (t - 7) % TC == 0:
                        h = (t - 7) // TC
                        dst = hid[head_rows(h), Y_SLOT["c"] + h // 2]
                        dve.wait_ge(pv_hi, l * 2 * HEADS + h + 1)
                        dve.tensor_tensor(dst[:, 1, :], ps[head_rows(h), bank_of(G_PV + h), :], fp(dst[:, 0, :]),
                                          ALU.subtract).then_inc(evac, 1)

                def update(k, ev, n):
                    st.mark(dve.tensor_tensor(y[:, k, 1, :], y[:, k, 1, :], scale_aux[:, :], ALU.mult))
                    st.wait()
                    dve.tensor_tensor(x[:, k, :], x[:, k, :], y[:, k, 1, :], ALU.add).then_inc(x_done, 1)
                    own(x_done, KD + l * 2 * KD + n + 1)

                for m in range(KD):
                    split_lo(dve, U_OUT + m + LEAD, l)
                dve.memset(e_g[:, 0:FFN_TAPS - 1], 0.0)
                st.mark(dve.memset(e_v[:, 0:FFN_TAPS - 1], 0.0))
                event_var("post_mix", l)
                event_diag("post_mix", l)
                scale_ready("post_mix", l)
                for k in range(KD):
                    update(k, "post_mix", k)
                    if k:
                        normed_lo("norm_ffn_pre", k - 1, KD + k - 1, l)
                normed_lo("norm_ffn_pre", KD - 1, 2 * KD - 1, l)
                split_lo(dve, U_UP + LEAD, l)
                event_var("pre_ffn", l)
                event_diag("pre_ffn", l)
                scale_ready("pre_ffn", l)

                def taps(dst, src, w, last):
                    st.mark(dve.tensor_scalar(dst, src[:, 0:T], w(0), None, ALU.mult))
                    for j in range(1, FFN_TAPS):
                        st.wait()
                        ins = dve.scalar_tensor_tensor(dst, src[:, j:j + T], w(j), dst, ALU.mult, ALU.add)
                        if j == FFN_TAPS - 1 and last is not None:
                            ins.then_inc(last, 1)
                        else:
                            st.mark(ins)

                def hidden_lo(p):
                    dve.wait_ge(f_hi, l * NF + p + 1)
                    dve.tensor_tensor(hid[:, p, 1, :], c_v[:, :], fp(hid[:, p, 0, :]), ALU.subtract)\
                       .then_inc(f_ready, 1)

                def ffn_body(i, first):
                    for jj in range(2):
                        p = i * 2 + jj
                        for half, (e, cc) in enumerate(((e_g, c_g), (e_v, c_v))):
                            j = 2 * jj + half
                            u = U_UP + j + LEAD
                            if not (first and j == 0):
                                dve.wait_ge(hi_done, l * NU + i * 4 + u + 1)
                                dve.tensor_tensor(wsp[:, u % SPLIT, 1, :], raw[:, u % RAW, :],
                                                  fp(wsp[:, u % SPLIT, 0, :]), ALU.subtract).then_inc(lo_done, 1)
                            dve.wait_ge(group_done, l * NG + i * 4 + G_UP + j + 1)
                            dve.tensor_tensor(e[:, FFN_TAPS - 1:], ps[:, j, :], scale_main[:, :], ALU.mult)\
                               .then_inc(evac, 1)
                            if half == 0 and not (first and jj == 0):
                                hidden_lo(p - 1)
                            own(evac, l * N_EVAC + i * 4 + G_OUT + j + 1)

                            def w(k):
                                a = VC["conv_ffn"] + k * 2 * NF + half * NF
                                return vec[:, bass.ds(p + a, 1)]

                            if half and not (first and jj == 0):
                                own(f_ready, l * NF + p)
                            taps(cc[:, :], e, w, c_gate if half == 0 else None)
                        dve.wait_ge(tanh_done, l * NF + p + 1)
                        st.mark(dve.scalar_tensor_tensor(th[:, :], th[:, :], 1.0, c_g[:, :], ALU.add, ALU.mult))
                        st.wait()
                        dve.scalar_tensor_tensor(c_v[:, :], th[:, :], 0.5, c_v[:, :], ALU.mult, ALU.mult)\
                           .then_inc(f_done, 1)

                n0 = st.n
                ffn_body(0, True)
                per_body = st.n - n0
                with dve.Fori(1, NF // 2) as i:
                    st.base, st.n = l * V_STEPS + i * per_body, n0
                    ffn_body(i, False)
                    assert st.n == n0 + per_body
                st.base, st.n = l * V_STEPS, n0 + per_body * (NF // 2)
                hidden_lo(NF - 1)

                with dve.Fori(0, 2) as i:
                    for j in range(12):
                        u = U_DOWN + j + LEAD
                        dve.wait_ge(hi_done, l * NU + i * 12 + u + 1)
                        dve.tensor_tensor(wsp[:, u % SPLIT, 1, :], raw[:, u % RAW, :],
                                          fp(wsp[:, u % SPLIT, 0, :]), ALU.subtract).then_inc(lo_done, 1)
                event_var("post_ffn", l)
                event_diag("post_ffn", l)
                scale_ready("post_ffn", l)
                for k in range(KD):
                    update(k, "post_ffn", KD + k)
                assert st.n == V_STEPS, st.n

        @block.scalar
        def _(act):
            act.preload_act_table_set("exp_and_others")
            for name, a, n in SMALL:
                v = inp[name]
                if len(v.shape) == 3:
                    v = v.rearrange("l j f -> l (j f)")
                act.dma_start(rows[a:a + n, :, 0, :], v.rearrange("l (r c) -> r l c", c=P)).then_inc(rows_in, 16)
            v = inp["conv_ffn"].rearrange("l j f -> l (j f)")
            for t in range(2):
                act.dma_start(rows[0:HALFROWS, :, 1 + t, :],
                              v[:, t * HALFROWS * P:(t + 1) * HALFROWS * P].rearrange("l (r c) -> r l c", c=P))\
                   .then_inc(rows_in, 16)
            rope_v = [r.rearrange("s p t -> p s t") for r in rope_tables]
            act.dma_start(rope[:, :, :], rope_v[0]).then_inc(rope_in, 16)
            for u in range(LEAD):
                split_hi(act, u, 0, first=True)

            def square(ev, k, src, l):
                if k == 0 and ev != EVENTS[0]:
                    act.wait_ge(stat_done, l * NEV + EVENTS.index(ev))
                elif k >= 2:
                    act.wait_ge(add_done, l * NADD + adds_before(ev) + k - 1)
                act.activation(sq[:, min(k, 1), :], src, ACT.Square).then_inc(sq_done, 1)

            def copy_scale(ev, dst, l):
                act.wait_ge(spread_done, l * NEV + EVENTS.index(ev) + 1)
                act.activation(dst[:, :], ps[:, STAT, :], ACT.Copy).then_inc(scale_done, 1)

            def group_ready(g, l):
                act.wait_ge(group_done, l * NG + g + 1)

            def normed_hi(name, k, n, ev, l):
                act.wait_ge(x_done, l * 2 * KD + n + 1)
                act.activation(xn[:, k, 0, :], x[:, k, :], ACT.Copy, scale=col(name, k)).then_inc(xh_done, 1)

            with act.Fori(0, DEPTH) as l:
                act.wait_ge(vec_set, l + 1)
                for k in range(KD):
                    normed_hi("norm_mix_pre", k, k, "pre_mix", l)
                    square("pre_mix", k, x[:, k, :], l)
                split_hi(act, 3, l)
                copy_scale("pre_mix", scale_main, l)

                def rot_hi_part(n):
                    act.wait_ge(rot_done, l * 8 + n + 1)
                    if n < 4:
                        dst, e = hid[:, (QM, KM, QM + 1, KM + 1)[n]], mb_rot[:, n % 2, :]
                    else:
                        dst, e = xn[0:MLA_QK, n - 4], ml_rot[0:MLA_QK, n % 2, :]
                    act.activation(dst[:, 0, :], e, ACT.Copy).then_inc(rot_hi, 1)

                cf_j = 0
                for g in range(G_MQ):
                    if g >= 1:
                        split_hi(act, g + LEAD, l)
                    if g in (0, 2):
                        c = g // 2
                        act.wait_ge(evac, l * N_EVAC + g + 1)
                        act.activation(mb_rot[:, c, :], mb_rot[:, c, :], ACT.Tanh, scale=0.5).then_inc(cf_tanh, 1)
                    if G_QK <= g < G_V:
                        rot_hi_part(g - G_QK)
                    for _ in range(CF_SHARE.get(g, 0)):
                        j, cf_j = cf_j, cf_j + 1
                        if j == 0:
                            act.wait_ge(cf_u_set, l + 1)
                            act.activation(cf_out[:, 1, :], cf_u[:, 1, 0:T], ACT.Identity, scale=col("conv_b", 1),
                                           bias=col("conv_b_bias", 1)).then_inc(cf_prod, 1)
                            continue
                        if j > 2:
                            act.wait_ge(cf_sum, l * (CF_TAPS - 1) + j - 2)
                        act.activation(cf_tmp[:, j % 2, :], cf_u[:, 1, j:j + T], ACT.Copy,
                                       scale=col("conv_b", 2 * j + 1)).then_inc(cf_prod, 1)
                    if g in (G_V, G_V + 1):
                        group_ready(g, l)
                        for j in range(2):
                            c = 2 * (g - G_V) + j
                            act.activation(vm[:, 0, c, :], ps[:, bank_of(g), j * GW:(j + 1) * GW], ACT.Copy,
                                           scale=rstd_mix[:, c:c + 1]).then_inc(val_hi, 1)
                    if g == G_V:
                        act.wait_ge(rot_done, l * 8 + 4)
                        act.dma_start(rope[:, :, :], rope_v[1]).then_inc(rope_in, 16)
                    if g == G_KR:
                        act.wait_ge(kr_done, l + 1)
                        act.activation(kr[DH:MLA_QK, 0, :], mb_rot[DH:MLA_QK, 0, :], ACT.Copy).then_inc(kr_hi, 1)
                    if g == 14:
                        for c in range(2):
                            act.wait_ge(cf_cent, l * 2 + c + 1)
                            square("ln", c, cf_out[:, c, :], l)
                    if g == 15:
                        square("ckv", 0, lat[:, 3, :], l)
                        copy_scale("ln", scale_aux, l)
                    if g == 16:
                        for c in range(2):
                            act.wait_ge(cf_norm, l * 2 + c + 1)
                            act.activation(mb_rot[:, c, :], cf_out[:, c, :], ACT.Tanh, scale=0.5)\
                               .then_inc(cf_swish, 1)
                    if g == 17:
                        for j in range(3):
                            square("cq", j, lat[:, j, :], l)
                        copy_scale("ckv", scale_aux, l)
                        for c in range(2):
                            act.wait_ge(cf_val, l * 2 + c + 1)
                            act.activation(hid[:, Y_SLOT["b"] + c, 0, :], cf_out[:, c, :], ACT.Copy, scale=0.5)\
                               .then_inc(y_hi, 1)
                        act.wait_ge(sc_val, l * 2 + 1)
                        act.activation(hid[:, Y_SLOT["a"], 0, :], sc_w[:, :], ACT.Copy).then_inc(y_hi, 1)
                    if g == 18:
                        act.wait_ge(lat_norm, l * 4 + 1)
                        act.activation(hid[:, CKVN, 0, :], lat[:, 3, :], ACT.Copy, scale=col("mla_kv_norm"))\
                           .then_inc(lat_hi, 1)
                    if g == 19:
                        copy_scale("cq", scale_aux, l)
                    if g == 20:
                        for j in range(3):
                            act.wait_ge(lat_norm, l * 4 + j + 2)
                            act.activation(hid[:, CQN + j, 0, :], lat[:, j, :], ACT.Copy,
                                           scale=col("mla_q_norm", j)).then_inc(lat_hi, 1)
                        act.wait_ge(sc_val, l * 2 + 2)
                        act.activation(hid[:, Y_SLOT["a"] + 1, 0, :], sc_w[:, :], ACT.Copy).then_inc(y_hi, 1)

                for h in range(HEADS):
                    rot_hi_part(4 + h)
                for h in range(HEADS):
                    group_ready(G_MK + h, l)
                    act.activation(ml_k[h][0:DH, 0, :], ps[0:DH, bank_of(G_MK + h), :], ACT.Copy).then_inc(kn_hi, 1)
                for half in range(2):
                    group_ready(G_MV + half, l)
                    act.activation(vl[:, 0, 2 * half:2 * half + 2, :],
                                   ps[:, bank_of(G_MV + half), :].rearrange("p (c d) -> p c d", c=2),
                                   ACT.Copy).then_inc(val_hi, 1)
                act.wait_ge(kr_lo, l + 1)
                for s in range(2):
                    act.activation(xn[DH:MLA_QK, HEADS:2 * HEADS, s, :],
                                   fp(kr[DH:MLA_QK, s, :]).unsqueeze(1).to_broadcast([MLA_ROPE, HEADS, T]),
                                   ACT.Copy).then_inc(kr_spread, 1)
                act.dma_start(rope[:, :, :], rope_v[0]).then_inc(rope_in, 16)

                for t in range(N_ATT + ATT_TAIL):
                    if t < N_ATT:
                        n = (t % TC + 1) * P
                        if t >= 2:
                            act.wait_ge(pt_done, l * N_ATT + t - 1)
                        if t == 0:
                            act.wait_ge(kr_spread, l * 2 + 2)
                        act.wait_ge(negmax_done, l * N_ATT + t + 1)
                        act.activation(prob[:, t % 2, 0:n], sm[:, t % 2, 0:n], ACT.Exp, bias=negmax[:, t:t + 1],
                                       scale=MOBA_SCALE if t < N_ATT // 2 else MLA_SCALE,
                                       accum_out=rowsum[:, t:t + 1]).then_inc(exp_done, 1)
                    if 2 <= t < N_ATT + 2:
                        s = t - 2
                        h, c = divmod(s, TC)
                        if c == 0 and h >= 1:
                            group_ready(G_PV + h - 1, l)
                        act.wait_ge(pt_done, l * N_ATT + s + 1)
                        act.activation(pt[:, 0, 0:c + 1, c * P:(c + 1) * P],
                                       ps[:, PT_BANKS[s % 2], 0:(c + 1) * P].rearrange("p (k t) -> p k t", t=P),
                                       ACT.Copy).then_inc(pt_hi, 1)
                    if t in (2, 4, 6):
                        split_hi(act, U_OUT + t // 2 - 1, l)
                    if t >= 7 and (t - 7) % TC == 0:
                        h = (t - 7) // TC
                        r = slice(DH * (h % 2), DH * (h % 2) + DH)
                        group_ready(G_PV + h, l)
                        act.activation(hid[r, Y_SLOT["c"] + h // 2, 0, :], ps[r, bank_of(G_PV + h), :], ACT.Copy)\
                           .then_inc(pv_hi, 1)

                for m in range(KD):
                    split_hi(act, U_OUT + m + LEAD, l)
                    group_ready(G_OUT + m, l)
                    square("post_mix", m, ps[:, m % 4, :], l)
                    act.activation(y[:, m, 1, :], ps[:, m % 4, :], ACT.Copy, scale=col("norm_mix_post", m))\
                       .then_inc(y_evac, 1)
                copy_scale("post_mix", scale_aux, l)
                for k in range(KD):
                    normed_hi("norm_ffn_pre", k, KD + k, "pre_ffn", l)
                    square("pre_ffn", k, x[:, k, :], l)
                split_hi(act, U_UP + LEAD, l)
                copy_scale("pre_ffn", scale_main, l)

                def hidden_hi(p):
                    act.wait_ge(f_done, l * NF + p + 1)
                    act.activation(hid[:, p, 0, :], c_v[:, :], ACT.Copy).then_inc(f_hi, 1)

                def split_up(i, j):
                    u = U_UP + j + LEAD
                    act.wait_ge(raw_in[u % RAW], l * (NU // RAW * 16) + i * 32 + 16 * (u // RAW + 1))
                    act.wait_ge(group_done, l * NG + i * 4 + G_UP + j)
                    act.activation(wsp[:, u % SPLIT, 0, :], raw[:, u % RAW, :], ACT.Copy).then_inc(hi_done, 1)

                def ffn_body(i, first):
                    for jj in range(2):
                        p = i * 2 + jj
                        if not (first and jj == 0):
                            split_up(i, 2 * jj)
                            hidden_hi(p - 1)
                        split_up(i, 2 * jj + 1)
                        act.wait_ge(c_gate, l * NF + p + 1)
                        act.activation(th[:, :], c_g[:, :], ACT.Tanh, scale=0.5).then_inc(tanh_done, 1)

                ffn_body(0, True)
                with act.Fori(1, NF // 2) as i:
                    ffn_body(i, False)
                hidden_hi(NF - 1)

                for m in range(KD):
                    for part in range(3):
                        u = U_DOWN + 3 * m + part + LEAD
                        act.wait_ge(raw_in[u % RAW], l * (NU // RAW * 16) + 16 * (u // RAW + 1))
                        if part == 0:
                            act.wait_ge(group_done, l * NG + G_DOWN + m)
                        else:
                            act.wait_ge(down_part, l * 2 * KD + 2 * m + part)
                        act.activation(wsp[:, u % SPLIT, 0, :], raw[:, u % RAW, :], ACT.Copy).then_inc(hi_done, 1)
                    group_ready(G_DOWN + m, l)
                    square("post_ffn", m, ps[:, m % 4, :], l)
                    act.activation(y[:, m, 1, :], ps[:, m % 4, :], ACT.Copy, scale=col("norm_ffn_post", m))\
                       .then_inc(y_evac, 1)
                copy_scale("post_ffn", scale_aux, l)

            for k in range(KD):
                act.wait_ge(ot_done, k + 1)
                act.activation(out_tok[:, :, k * P:(k + 1) * P], ps[:, k % 4, :].rearrange("p (c f) -> p c f", f=P),
                               ACT.Copy).then_inc(out_set, 1)


_INS = ["x", "norm_mix_pre", "norm_mix_post", "norm_ffn_pre", "norm_ffn_post", "w_in", "conv_a", "conv_b",
        "conv_b_bias", "ln_b_gain", "ln_b_bias", "mla_q_norm", "mla_kv_norm", "w_uq", "w_ukv", "w_out",
        "w_ffn_up", "conv_ffn", "w_ffn_down"]
ROPE_THETA = 500000.0


def rope_table(dim, first, period, np):
    half = dim // 2
    inv = (1.0 / (np.float32(ROPE_THETA) ** (np.arange(0, dim, 2, dtype=np.float32) / np.float32(dim))))
    ang = np.arange(T, dtype=np.float32)[:, None] * inv.astype(np.float32)[None, :]
    table = np.zeros((2, P, T), np.float32)
    table[0] = 1.0
    for p0 in range(first, P, period):
        for j in range(dim):
            table[0, p0 + j] = np.cos(ang[:, j % half])
            table[1, p0 + j] = np.sin(ang[:, j % half]) * np.float32(-1.0 if j < half else 1.0)
    return table


def kernel(**inputs):
    import numpy as np
    import concourse.bacc as bacc
    from concourse.bass_utils import run_bass_kernel_spmd

    nc = bacc.Bacc("TRN2", target_bir_lowering=False, num_devices=1)
    arrays = {}

    def dram(name, a):
        arrays[name] = a
        return nc.dram_tensor(name, a.shape, mybir.dt.from_np(a.dtype), kind="ExternalInput").ap()

    inp = {name: dram(f"in_{name}", np.ascontiguousarray(inputs[name])) for name in _INS}
    tables = [dram("rope_moba", rope_table(DH // 4, 0, DH, np)), dram("rope_mla", rope_table(MLA_ROPE, DH, P, np))]
    out = nc.dram_tensor("out_x", (1, T, D), mybir.dt.float32, kind="ExternalOutput").ap()
    hybrid_trunk_kernel(nc, inp, tables, out)
    r = run_bass_kernel_spmd(nc, [arrays], core_ids=[0])
    return r.results[0]["out_x"]
```

```python
import concourse.bass as bass
from concourse import mybir
from contextlib import ExitStack

P = 128
T = 512
TC = T // P
D = 1024
KD = D // P
DEPTH = 2
GW = 256
HEADS = 4
DH = 64
MLA_ROPE = 32
MLA_QK = DH + MLA_ROPE
Q_RANK, KV_RANK = 384, 128
D_FF = 2816
NF = D_FF // P
EPS = 1e-6
MASKED = -1e30
MOBA_SCALE = DH ** -0.5
MLA_SCALE = MLA_QK ** -0.5
CF_TAPS, SC_TAPS, FFN_TAPS = 31, 3, 3

SC0 = 0
CF0 = 3 * GW
MB0 = CF0 + 2 * GW
ML0 = MB0 + 3 * GW
KR0 = ML0 + Q_RANK + KV_RANK
IN_COLS = KR0 + MLA_ROPE

SMALL = []
_at = 0
for _name, _rows in (("norm_mix_pre", KD), ("norm_mix_post", KD), ("norm_ffn_pre", KD), ("norm_ffn_post", KD),
                     ("conv_a", SC_TAPS * 2), ("conv_b", CF_TAPS * 2), ("conv_b_bias", 2), ("ln_b_gain", 2),
                     ("ln_b_bias", 2), ("mla_q_norm", 3), ("mla_kv_norm", 1)):
    SMALL.append((_name, _at, _rows))
    _at += _rows
NSMALL = _at
VC = {n: a for n, a, _ in SMALL}
VC["conv_ffn"] = NSMALL
NTAPROWS = FFN_TAPS * 2 * NF
HALFROWS = NTAPROWS // 2
NVEC = NSMALL + NTAPROWS

W_IN_COLS = ([CF0 + GW, CF0, CF0 + GW + P, CF0 + P]
             + [MB0, MB0 + GW, MB0 + P, MB0 + GW + P]
             + [None, None]
             + [ML0 + Q_RANK, KR0 - DH]
             + [ML0, ML0 + P, ML0 + 2 * P]
             + [SC0 + 2 * GW, SC0, SC0 + GW, SC0 + 2 * GW + P, SC0 + P, SC0 + GW + P])
U_VAL = 8
U_KR = 11
U_UQ, U_UKV = 21, 23
U_OUT = 24
U_UP = U_OUT + KD
U_DOWN = U_UP + 2 * NF
DOWN_PARTS = ((0, 8), (8, 8), (16, 6))
NU = U_DOWN + 3 * KD
RAW, SPLIT = 2, 4
LEAD = 3

G_CF, G_QK, G_V, G_CKV, G_KR, G_CQ, G_SC = 0, 4, 8, 10, 11, 12, 15
G_MQ, G_MK, G_MV, G_PV = 21, 25, 29, 31
G_OUT = 39
G_UP = G_OUT + KD
G_DOWN = G_UP + 2 * NF
NG = G_DOWN + KD

STAT, SCORE0, PT_BANKS = 4, 5, (3, 7)
RING = (0, 1, 2, 3, 5, 6, 7)


def bank_of(g):
    if g < G_PV:
        return RING[g % len(RING)]
    if g < G_OUT:
        return (g - G_PV) % 3
    return (g - (G_OUT if g < G_UP else G_UP if g < G_DOWN else G_DOWN)) % 4


def bank_up(j, first):
    return (5, 6, 7, 3)[j] if first else j


def bank_before(g):
    return max((p + 1 for p in range(g) if bank_of(p) == bank_of(g)), default=0)


EVENTS = ["pre_mix", "ckv", "cq", "ln", "post_mix", "pre_ffn", "post_ffn"]
SQUARES = dict(pre_mix=KD, ln=2, ckv=1, cq=3, post_mix=KD, pre_ffn=KD, post_ffn=KD)
POST = ("post_mix", "post_ffn")
WIDTH = dict(pre_mix=D, ln=GW, ckv=KV_RANK, cq=Q_RANK, post_mix=D, pre_ffn=D, post_ffn=D)
NEV = len(EVENTS)
NSQ = sum(SQUARES.values())
NADD = sum(n - 1 for n in SQUARES.values())


def squares_before(ev):
    return sum(SQUARES[e] for e in EVENTS[:EVENTS.index(ev)])


def adds_before(ev):
    return sum(SQUARES[e] - 1 for e in EVENTS[:EVENTS.index(ev)])


N_EVAC = G_OUT + 2 * NF
N_YEVAC = 2 * KD
N_XH = 2 * KD
CF_VECTOR = {3: 2, 8: 4, 9: 4, 10: 4, 11: 1, 12: 4, 13: 4, 14: 4, 15: 4}
CF_SCALAR = {3: 1, **{g: 3 for g in range(4, 14)}}
assert sum(CF_VECTOR.values()) == CF_TAPS and sum(CF_SCALAR.values()) == CF_TAPS
N_ATT = 2 * HEADS * TC
V_STEPS = 2 + 1 + (CF_TAPS - 1) + (4 + 1 + 2) + 2 * (1 + SC_TAPS) + N_ATT + 2 * KD + NF * (2 * FFN_TAPS)
SPLIT_AFTER = (1, 2, 5)
NPROB = 3
TRAIL = 3
VALUES_AFTER = (3, 5, 6)
ATT_TAIL = TRAIL + 4


def hybrid_trunk_kernel(nc, inp, rope_tables, out):
    f32 = mybir.dt.float32
    f32r = mybir.dt.float32r
    ALU = mybir.AluOpType
    ACT = mybir.ActivationFunctionType

    def fp(ap):
        return ap.bitcast(f32)

    with ExitStack() as ctx:
        sem_names = {}

        def sem(name):
            sem_names[name] = ctx.enter_context(nc.semaphore(name))
            return sem_names[name]

        base = -(-nc.sbuf_base // 32) * 32
        at = [base]

        def place(name, shape, dt, offset=None):
            size = 4
            for n in shape[1:]:
                size *= n
            if offset is None:
                offset = at[0]
                at[0] += -(-size // 32) * 32
            return nc.alloc_sbuf_tensor_at(name, shape, dt, offset=offset)

        x = place("x", [P, KD, T], f32)
        xn_at = at[0]
        xn = place("xn", [P, KD, 2, T], f32r)
        slots_at = at[0]
        hid = place("hid", [P, NF, 2, T], f32r)
        SLOT = 2 * T * 4
        raw = place("raw", [P, RAW, 8 * P], f32)
        wsp = place("wsp", [P, SPLIT, 2, 8 * P], f32r)
        ident = place("ident", [P, P], f32)
        ones = place("ones", [P, P], f32)
        causal = place("causal", [P, T], f32)
        rope = place("rope", [P, 2, T], f32)
        scale_main = place("scale_main", [P, T], f32)
        vec_all = place("vec_all", [P, DEPTH, NVEC], f32)
        vec = place("vec", [P, NVEC], f32)
        gain_next = place("gain_next", [P, KD], f32)
        var = place("var", [P, TC], f32)
        rstd = place("rstd", [P, TC], f32)
        power = place("power", [P, TC], f32)
        rstd_mix = place("rstd_mix", [P, TC], f32)
        rowmax = place("rowmax", [P, N_ATT], f32)
        negmax = place("negmax", [P, N_ATT], f32)
        rowsum = place("rowsum", [P, N_ATT], f32)
        rowinv = place("rowinv", [P, N_ATT], f32)
        tmp_at = at[0]
        cf_out = place("cf_out", [P, 2, T], f32, tmp_at)
        sc_u = place("sc_u", [P, T + 2], f32, tmp_at + 4096)
        kr = place("kr", [P, 2, T], f32r, tmp_at + 6176)
        sq = place("sq", [P, 2, T], f32, tmp_at + 10336)
        sm = place("sm", [P, 2, T], f32, tmp_at + 10336)
        prob = place("prob", [P, NPROB, T], f32, tmp_at + 4096)
        e_g = place("e_g", [P, T + 2], f32, tmp_at)
        e_v = place("e_v", [P, T + 2], f32, tmp_at + 2080)
        c_g = place("c_g", [P, T], f32, tmp_at + 4160)
        c_v = place("c_v", [P, T], f32, tmp_at + 6208)
        th = place("th", [P, T], f32, tmp_at + 8256)
        assert tmp_at + 10336 + 4096 <= nc.sbuf_usable_end, (tmp_at + 14432, nc.sbuf_usable_end)

        Y_SLOT = dict(a=0, b=2, c=4, d=6)
        QM, KM, VM, VL, CQN, CKVN, PT = 8, 10, 12, 14, 16, 19, 16

        def slot(n):
            return slots_at + n * SLOT

        vm = hid[:, VM:VM + 2, :, :].rearrange("p a b t -> p (a b t)").rearrange("p (s c d) -> p s c d", s=2, c=TC)
        vl = hid[:, VL:VL + 2, :, :].rearrange("p a b t -> p (a b t)").rearrange("p (s c d) -> p s c d", s=2, c=TC)
        pt_early = hid[:, PT:PT + 2, :, :].rearrange("p a b t -> p (a b t)")\
            .rearrange("p (n s k t) -> p n s k t", n=2, s=2, k=2)
        pt_late = hid[:, PT + 2:PT + 6, :, :].rearrange("p a b t -> p (a b t)")\
            .rearrange("p (n s k t) -> p n s k t", n=2, s=2, k=4)

        def pt_of(h, c, s):
            tile = pt_early if c < 2 else pt_late
            return tile[:, h % 2, s, 0:c + 1, (c % 2) * P:(c % 2 + 1) * P]

        cf_u = place("cf_u", [P, 2, T + CF_TAPS - 1], f32, slot(VL))
        sc_w = place("sc_w", [P, T], f32, slot(VL) + 5120)
        rot = place("rot", [P, 2, T], f32, slot(Y_SLOT["d"]))
        shuf = place("shuf", [P, T], f32, slot(Y_SLOT["d"] + 1))
        cf_th = place("cf_th", [P, 2, T], f32, slot(Y_SLOT["c"]))
        ml_shuf = place("ml_shuf", [P, 2, T], f32, slot(Y_SLOT["c"] + 1))
        ml_rot = place("ml_rot", [P, HEADS, T], f32, slot(Y_SLOT["d"]))
        cf_tmp = place("cf_tmp", [P, 2, T], f32, slot(CQN + 2))
        lat = place("lat", [P, 4, T], f32, slot(20))
        x_tok = place("x_tok", [P, TC, D], f32, slot(0))
        rows = place("rows", [P, DEPTH, 3, P], f32, slot(4))
        out_tok = place("out_tok", [P, TC, D], f32, slot(0))
        y = place("y", [P, KD, 2, T], f32, xn_at)
        ml_q = [xn[:, h, :, :] for h in range(HEADS)]
        ml_k = [xn[:, HEADS + h, :, :] for h in range(HEADS)]

        ps = ctx.enter_context(nc.psum_tensor("ps", [P, 8, T], f32))

        x_in = [sem(f"x_in{c}") for c in range(TC)]
        rows_in = sem("rows_in")
        ident_set = sem("ident_set")
        rope_in = sem("rope_in")
        raw_in = [sem(f"raw_in{s}") for s in range(RAW)]
        hi_done = sem("hi_done")
        lo_done = sem("lo_done")
        down_part = sem("down_part")
        xt_done = sem("xt_done")
        vt_done = sem("vt_done")
        vec_all_set = sem("vec_all_set")
        vec_set = sem("vec_set")
        gain_set = sem("gain_set")
        x_done = sem("x_done")
        xh_done = sem("xh_done")
        xl_done = sem("xl_done")
        group_done = sem("group_done")
        evac = sem("evac")
        y_evac = sem("y_evac")
        v_step = sem("v_step")
        sq_done = sem("sq_done")
        add_done = sem("add_done")
        stat_done = sem("stat_done")
        var_done = sem("var_done")
        rstd_done = sem("rstd_done")
        spread_done = sem("spread_done")
        scale_done = sem("scale_done")
        mix_set = sem("mix_set")
        cf_tanh = sem("cf_tanh")
        cf_u_set = sem("cf_u_set")
        cf_prod = sem("cf_prod")
        cf_sum = sem("cf_sum")
        cf_conv = sem("cf_conv")
        mean_done = sem("mean_done")
        cf_cent = sem("cf_cent")
        cf_norm = sem("cf_norm")
        cf_affine = sem("cf_affine")
        cf_swish = sem("cf_swish")
        cf_val = sem("cf_val")
        sc_val = sem("sc_val")
        y_hi = sem("y_hi")
        y_ready = sem("y_ready")
        rot_done = sem("rot_done")
        rot_sin = sem("rot_sin")
        rot_hi = sem("rot_hi")
        qk_ready = sem("qk_ready")
        val_hi = sem("val_hi")
        lat_done = sem("lat_done")
        lat_norm = sem("lat_norm")
        lat_hi = sem("lat_hi")
        lat_ready = sem("lat_ready")
        kr_done = sem("kr_done")
        kr_hi = sem("kr_hi")
        kr_lo = sem("kr_lo")
        kr_spread = sem("kr_spread")
        kn_hi = sem("kn_hi")
        score_done = sem("score_done")
        masked = sem("masked")
        negmax_done = sem("negmax_done")
        exp_done = sem("exp_done")
        prob_done = sem("prob_done")
        pt_done = sem("pt_done")
        pt_hi = sem("pt_hi")
        pt_ready = sem("pt_ready")
        pv_hi = sem("pv_hi")
        c_gate = sem("c_gate")
        tanh_done = sem("tanh_done")
        f_done = sem("f_done")
        f_hi = sem("f_hi")
        f_ready = sem("f_ready")
        ot_done = sem("ot_done")
        out_set = sem("out_set")
        stored = sem("stored")

        def weight_source(u, l, i=0):
            if u < U_UQ:
                if u in (U_VAL, U_VAL + 1):
                    r0 = (u - U_VAL) * 4 * P
                    v = inp["w_in"][l, r0:r0 + 4 * P, MB0 + 2 * GW:MB0 + 3 * GW]
                    return v.rearrange("(k p) n -> p k n", p=P), 4, 2 * P
                n = P if u != U_KR else MLA_QK
                if W_IN_COLS[u] == 0:
                    l = (l + DEPTH) % DEPTH
                v = inp["w_in"][l, :, W_IN_COLS[u]:W_IN_COLS[u] + n]
                return v.rearrange("(k p) n -> p k n", p=P), KD, n
            if u < U_UKV:
                c0 = (u - U_UQ) * 2 * MLA_QK
                v = inp["w_uq"][l, :, c0:c0 + 2 * MLA_QK]
                return v.rearrange("(k p) n -> p k n", p=P), 3, 2 * MLA_QK
            if u == U_UKV:
                return inp["w_ukv"][l, :, :].rearrange("(k p) n -> p k n", p=P), 1, 2 * GW
            if u < U_UP:
                m = u - U_OUT
                v = inp["w_out"][l, :, m * P:(m + 1) * P]
                return v.rearrange("(k p) n -> p k n", p=P), KD, P
            if u < U_DOWN:
                j = u - U_UP
                v = inp["w_ffn_up"][l, :, bass.ds((j % 2) * D_FF + (j // 2) * P + i * P, P)]
                return v.rearrange("(k p) n -> p k n", p=P), KD, P
            m, part = divmod(u - U_DOWN, 3)
            k0, nk = DOWN_PARTS[part]
            v = inp["w_ffn_down"][l, k0 * P:(k0 + nk) * P, bass.ds(m * P + i * P, P)]
            return v.rearrange("(k p) n -> p k n", p=P), nk, P

        def unit_elements(u):
            if u == U_KR:
                return KD * MLA_QK
            if U_UQ <= u < U_UKV:
                return 3 * 2 * MLA_QK
            return 2 * GW if u == U_UKV else KD * P

        def released(u):
            if u < U_UQ:
                return group_done, (u + 1 if u != U_VAL else u + 2), NG
            if u < U_OUT:
                return group_done, (G_MQ + 2, G_MQ + 4, G_PV)[u - U_UQ], NG
            if u < U_UP:
                return group_done, G_OUT + u - U_OUT + 1, NG
            if u < U_DOWN:
                return group_done, G_UP + u - U_UP + 1, NG
            m, part = divmod(u - U_DOWN, 3)
            return (group_done, G_DOWN + m + 1, NG) if part == 2 else (down_part, 2 * m + part + 1, 2 * KD)

        def weights(u):
            n = {True: 2 * P}.get(u in (U_VAL, U_VAL + 1), P)
            if u == U_KR:
                n = MLA_QK
            if U_UQ <= u < U_UKV:
                n = 2 * MLA_QK
            if u == U_UKV:
                n = 2 * GW
            nk = unit_elements(u) // n
            return wsp[:, u % SPLIT, :, 0:nk * n].rearrange("p s (k n) -> p s k n", n=n)

        def split_hi(act, u, l, i=0, per=0, first=False):
            n = unit_elements(u % NU)
            act.wait_ge(raw_in[u % RAW], l * (NU // RAW * 16) + i * (per // RAW * 16) + 16 * (u // RAW + 1))
            if not first and u >= SPLIT:
                s, count, step = released(u - SPLIT)
                act.wait_ge(s, l * step + i * (per if s is group_done else 2 * per // 3) + count)
            act.activation(wsp[:, u % SPLIT, 0, 0:n], raw[:, u % RAW, 0:n], ACT.Copy).then_inc(hi_done, 1)

        def split_lo(dve, u, l, i=0, per=0):
            n = unit_elements(u % NU)
            dve.wait_ge(hi_done, l * NU + i * per + u + 1)
            dve.tensor_tensor(wsp[:, u % SPLIT, 1, 0:n], raw[:, u % RAW, 0:n], fp(wsp[:, u % SPLIT, 0, 0:n]),
                              ALU.subtract).then_inc(lo_done, 1)

        def col(name, c=0):
            a = VC[name] + c
            return vec[:, a:a + 1]

        block = ctx.enter_context(nc.Block())

        @block.sync
        def _(sp):
            def load(u, l, i=0, per=0, wait=True):
                if wait:
                    sp.wait_ge(lo_done, l * NU + i * per + u - 1)
                src, nk, n = weight_source(u % NU, l if u < NU else (l + 1) % DEPTH, i)
                dst = raw[:, u % RAW, 0:nk * n].rearrange("p (k n) -> p k n", n=n)
                sp.dma_start(dst, src).then_inc(raw_in[u % RAW], 16)

            for c in range(TC):
                sp.dma_start(x_tok[:, c, :], inp["x"][0, c * P:(c + 1) * P, :]).then_inc(x_in[c], 16)
            load(0, 0, wait=False)
            load(1, 0, wait=False)
            load(2, 0)
            with sp.Fori(0, DEPTH) as l:
                for u in range(LEAD, U_UP):
                    load(u, l)
                with sp.Fori(0, NF // 2) as i:
                    for j in range(4):
                        u = U_UP + j
                        sp_u = l * NU + i * 4 + u - 1
                        src, nk, n = weight_source(u, l, i * 2)
                        dst = raw[:, u % RAW, 0:nk * n].rearrange("p (k n) -> p k n", n=n)
                        sp.wait_ge(raw_in[u % RAW], 16)
                        sp.wait_ge(lo_done, sp_u)
                        sp.dma_start(dst, src).then_inc(raw_in[u % RAW], 16)
                with sp.Fori(0, 2) as i:
                    for j in range(12):
                        u = U_DOWN + j
                        sp_u = l * NU + i * 12 + u - 1
                        src, nk, n = weight_source(u, l, i * 4)
                        dst = raw[:, u % RAW, 0:nk * n].rearrange("p (k n) -> p k n", n=n)
                        sp.wait_ge(raw_in[u % RAW], 16)
                        sp.wait_ge(lo_done, sp_u)
                        sp.dma_start(dst, src).then_inc(raw_in[u % RAW], 16)
                for u in range(NU, NU + LEAD):
                    load(u, l)
            out_v = out[0, :, :].rearrange("(c p) f -> p c f", p=P)
            for k in range(KD):
                sp.wait_ge(out_set, k + 1)
                sp.dma_start(out_v[:, :, k * P:(k + 1) * P], out_tok[:, :, k * P:(k + 1) * P]).then_inc(stored, 16)
            sp.wait_ge(rope_in, 16 * (2 * DEPTH + 1))
            sp.wait_ge(stored, 16 * KD)

        @block.tensor
        def _(pe):
            def product(dst, a, b, start, stop):
                pe.matmul(dst, a[0], b[0], start=start, stop=False, skip_group_check=True)
                pe.matmul(dst, a[0], b[1], start=False, stop=False, skip_group_check=True)
                return pe.matmul(dst, a[1], b[0], start=False, stop=stop, skip_group_check=True)

            def weights_ready(u, l, i=0, per=0):
                pe.wait_ge(lo_done, l * NU + i * per + u + 1)

            def dense(g, u, bank, rhs, l, m=P, c0=0, between=None):
                w = weights(u)
                nk = len(rhs)
                for k in range(nk):
                    last = product(ps[0:m, bank, :], (w[:, 0, k, c0:c0 + m], w[:, 1, k, c0:c0 + m]), rhs[k],
                                   k == 0, k == nk - 1)
                    if between and k == nk // 2:
                        between()
                last.then_inc(group_done, 1)

            def pair(tile, rows_=slice(0, P)):
                return tile[rows_, 0, :], tile[rows_, 1, :]

            x_pairs = [(xn[:, k, 0, :], xn[:, k, 1, :]) for k in range(KD)]

            def bank_free(l, count):
                pe.wait_ge(evac, l * N_EVAC + count)

            def stat(ev, l):
                n = SQUARES[ev]
                if n > 1:
                    pe.wait_ge(add_done, l * NADD + adds_before(ev) + n - 1)
                else:
                    pe.wait_ge(sq_done, l * NSQ + squares_before(ev) + n)
                if ev == "ckv":
                    pe.wait_ge(scale_done, l * 2 + 1)
                elif ev == "cq":
                    pe.wait_ge(lat_norm, l * 4 + 1)
                elif ev == "ln":
                    pe.wait_ge(cf_cent, l * 2 + 2)
                elif ev == "post_mix":
                    pe.wait_ge(cf_norm, l * 2 + 2)
                elif ev == "pre_ffn":
                    pe.wait_ge(x_done, KD + l * 2 * KD + KD)
                elif ev == "post_ffn":
                    pe.wait_ge(scale_done, l * 2 + 2)
                for c in range(TC):
                    last = pe.matmul(ps[:, STAT, c:c + 1], sq[:, 0, c * P:(c + 1) * P], ones[:, 0:1],
                                     start=True, stop=True)
                last.then_inc(stat_done, 1)

            def spread(ev, l):
                pe.wait_ge(rstd_done, l * NEV + EVENTS.index(ev) + 1)
                for c in range(TC):
                    last = pe.matmul(ps[:, STAT, c * P:(c + 1) * P], rstd[:, c:c + 1].to_broadcast([P, P]),
                                     ident[:, :], start=True, stop=True)
                last.then_inc(spread_done, 1)

            def together(units, groups, l, ready):
                for u in units:
                    weights_ready(u, l)
                for k in range(KD):
                    ready(k)
                    for u, g in zip(units, groups):
                        w = weights(u)
                        bank = bank_of(g) if g < G_UP else bank_up(g - G_UP, True)
                        last = product(ps[:, bank, :], (w[:, 0, k, :], w[:, 1, k, :]), x_pairs[k],
                                       k == 0, k == KD - 1)
                        if k == KD - 1:
                            last.then_inc(group_done, 1)

            pe.wait_ge(ident_set, 6)
            pe.wait_ge(rows_in, 16 * (len(SMALL) + 2))
            for l0 in range(DEPTH):
                for t, (n, c0) in enumerate(((NSMALL, 0), (HALFROWS, NSMALL), (HALFROWS, NSMALL + HALFROWS))):
                    last = pe.transpose(ps[:, 5 + l0, c0:c0 + n], rows[0:n, l0, t, :], ident[0:n, 0:n])
                last.then_inc(vt_done, 1)
            for k in range(KD):
                if k >= 4:
                    pe.wait_ge(x_done, k - 3)
                for c in range(TC):
                    if k == 0:
                        pe.wait_ge(x_in[c], 16)
                    last = pe.transpose(ps[:, k % 4, c * P:(c + 1) * P], x_tok[:, c, k * P:(k + 1) * P], ident[:, :])
                last.then_inc(xt_done, 1)
            pe.wait_ge(x_done, KD)

            with pe.Fori(0, DEPTH) as l:
                together([0, 1, 2], [0, 1, 2], l, lambda k: pe.wait_ge(xl_done, l * N_XH + k + 1))
                weights_ready(3, l)
                dense(3, 3, bank_of(3), x_pairs, l, between=lambda: stat("pre_mix", l))
                spread("pre_mix", l)
                for g in range(4, G_MQ):
                    if g in (G_V, G_V + 1):
                        weights_ready(U_VAL + 1, l)
                        bank_free(l, bank_before(g))
                        for h in range(2):
                            c = 2 * (g - G_V) + h
                            for k in range(KD):
                                w = weights(U_VAL + k // 4)
                                xk = [xn[:, k, s, c * P:(c + 1) * P] for s in range(2)]
                                last = product(ps[:, bank_of(g), h * GW:(h + 1) * GW], xk,
                                               (w[:, 0, k % 4, :], w[:, 1, k % 4, :]), k == 0, k == KD - 1)
                        last.then_inc(group_done, 1)
                    else:
                        weights_ready(g, l)
                        if bank_before(g):
                            bank_free(l, bank_before(g))
                        dense(g, g, bank_of(g), x_pairs, l, m=MLA_QK if g == G_KR else P)
                    if g == 13:
                        stat("ckv", l)
                    if g == 15:
                        spread("ckv", l)
                    if g == 16:
                        stat("cq", l)
                    if g == 17:
                        spread("cq", l)
                    if g == 18:
                        pe.wait_ge(cf_conv, l + 1)
                        pe.wait_ge(cf_sum, (l + 1) * (CF_TAPS - 1))
                        pe.wait_ge(lat_norm, l * 4 + 4)
                        for c in range(2):
                            last = pe.matmul(ps[:, STAT, :], ones[:, :], cf_out[:, c, :], start=c == 0, stop=c == 1)
                        last.then_inc(mean_done, 1)
                def projection_bank(g):
                    bank_free(l, bank_before(g))

                pe.wait_ge(lat_ready, l * 4 + 4)
                for h in range(HEADS):
                    g = G_MQ + h
                    weights_ready(U_UQ + h // 2, l)
                    projection_bank(g)
                    dense(g, U_UQ + h // 2, bank_of(g), [pair(hid[:, CQN + j]) for j in range(3)], l,
                          m=MLA_QK, c0=(h % 2) * MLA_QK)
                    if h == 0:
                        stat("ln", l)
                weights_ready(U_UKV, l)
                for h in range(HEADS):
                    g = G_MK + h
                    projection_bank(g)
                    dense(g, U_UKV, bank_of(g), [pair(hid[:, CKVN])], l, m=P, c0=h * P)
                spread("ln", l)
                wkv = weights(U_UKV)[:, :, 0, :].rearrange("p s (h n) -> p s h n", h=HEADS)
                for half in range(2):
                    g = G_MV + half
                    projection_bank(g)
                    for j in range(2):
                        c = 2 * half + j
                        last = product(ps[:, bank_of(g), j * GW:(j + 1) * GW],
                                       [hid[:, CKVN, s, c * P:(c + 1) * P] for s in range(2)],
                                       [wkv[:, s, :, DH:2 * DH] for s in range(2)], True, True)
                    last.then_inc(group_done, 1)

                def scores(t):
                    h, c = divmod(t, TC)
                    if t == 0:
                        bank_free(l, G_PV)
                    if t >= 2:
                        pe.wait_ge(masked, l * N_ATT + t - 1)
                    if h < HEADS:
                        r0 = DH * (h % 2)
                        q, k = hid[:, QM + h // 2], hid[:, KM + h // 2]
                        r = slice(r0, r0 + DH)
                    else:
                        if c == 0:
                            pe.wait_ge(qk_ready, l * 8 + 8)
                            bank_free(l, G_PV)
                            pe.wait_ge(kr_spread, l * 2 + 2)
                        q, k = ml_q[h - HEADS], ml_k[h - HEADS]
                        r = slice(0, MLA_QK)
                    n = (c + 1) * P
                    product(ps[:, SCORE0 + t % 2, 0:n], (q[r, 0, c * P:n], q[r, 1, c * P:n]),
                            (k[r, 0, 0:n], k[r, 1, 0:n]), True, True).then_inc(score_done, 1)

                def transposes(t):
                    c = t % TC
                    pe.wait_ge(prob_done, l * N_ATT + t + 1)
                    if t >= 2:
                        pe.wait_ge(pt_ready, l * N_ATT + t - 1)
                    for kc in range(c + 1):
                        last = pe.transpose(ps[:, PT_BANKS[t % 2], kc * P:(kc + 1) * P],
                                            prob[:, t % NPROB, kc * P:(kc + 1) * P], ident[:, :])
                    last.then_inc(pt_done, 1)

                def values(h, part):
                    g = G_PV + h
                    late = part > 0
                    if part < 2:
                        pe.wait_ge(pt_ready, l * N_ATT + TC * h + (TC if late else 2))
                    if part == 0:
                        bank_free(l, bank_before(g) if h >= 3 else G_PV)
                    v = vm if h < HEADS else vl
                    c0 = (h % HEADS) // 2 * P
                    tile, q0, kcs = (pt_late, 2, (0, 1) if part == 1 else (2, 3)) if late else (pt_early, 0, (0, 1))
                    for kc in kcs:
                        skip = max(kc - q0, 0) * P
                        last = product(ps[:, bank_of(g), q0 * P + skip:(q0 + 2) * P],
                                       [v[:, s, kc, c0:c0 + P] for s in range(2)],
                                       [tile[:, h % 2, s, kc, skip:2 * P] for s in range(2)],
                                       kc == 0, kc == q0 + 1)
                    if part == 2:
                        last.then_inc(group_done, 1)

                pe.wait_ge(qk_ready, l * 8 + 4)
                for t in range(N_ATT + ATT_TAIL):
                    if t < N_ATT:
                        scores(t)
                    if TRAIL <= t < N_ATT + TRAIL:
                        transposes(t - TRAIL)
                    for part, after in enumerate(VALUES_AFTER):
                        h, r = divmod(t - TRAIL - after, TC)
                        if r == 0 and 0 <= h < 2 * HEADS:
                            values(h, part)

                pe.wait_ge(y_ready, l * 4 + 4)
                bank_free(l, G_OUT)
                for m in range(KD):
                    weights_ready(U_OUT + m, l)
                    if m >= 4:
                        pe.wait_ge(y_evac, l * N_YEVAC + m - 3)
                    dense(G_OUT + m, U_OUT + m, m % 4, [pair(hid[:, k]) for k in range(KD)], l)
                stat("post_mix", l)
                spread("post_mix", l)

                pe.wait_ge(y_evac, l * N_YEVAC + KD)
                together([U_UP, U_UP + 1, U_UP + 2], [G_UP, G_UP + 1, G_UP + 2], l,
                         lambda k: pe.wait_ge(xl_done, l * N_XH + KD + k + 1))
                weights_ready(U_UP + 3, l)
                dense(G_UP + 3, U_UP + 3, 3, x_pairs, l, between=lambda: stat("pre_ffn", l))
                spread("pre_ffn", l)
                for j in range(4):
                    weights_ready(U_UP + 4 + j, l)
                    if j == 3:
                        bank_free(l, G_OUT + 4)
                    dense(G_UP + 4 + j, U_UP + 4 + j, j, x_pairs, l)
                with pe.Fori(2, NF // 2) as i:
                    for j in range(4):
                        pe.wait_ge(lo_done, l * NU + i * 4 + U_UP + j + 1)
                        pe.wait_ge(evac, l * N_EVAC + i * 4 + G_OUT + j - 3)
                        dense(G_UP + j, U_UP + j, j, x_pairs, l)

                with pe.Fori(0, 2) as i:
                    for j in range(12):
                        m, part = divmod(j, 3)
                        k0, nk = DOWN_PARTS[part]
                        pe.wait_ge(lo_done, l * NU + i * 12 + U_DOWN + j + 1)
                        if part == 0:
                            pe.wait_ge(y_evac, l * N_YEVAC + i * 4 + KD + m - 3)
                            bank_free(l, N_EVAC - 3 + m)
                        pe.wait_ge(f_ready, l * NF + k0 + nk)
                        w = weights(U_DOWN + j)
                        for k in range(nk):
                            last = product(ps[:, m, :], (w[:, 0, k, :], w[:, 1, k, :]), pair(hid[:, k0 + k]),
                                           k0 + k == 0, k0 + k == NF - 1)
                        last.then_inc(group_done if part == 2 else down_part, 1)
                stat("post_ffn", l)
                spread("post_ffn", l)

            pe.wait_ge(y_evac, DEPTH * N_YEVAC)
            for k in range(KD):
                pe.wait_ge(x_done, KD + (DEPTH * 2 - 1) * KD + k + 1)
                if k >= 4:
                    pe.wait_ge(out_set, k - 3)
                for c in range(TC):
                    last = pe.transpose(ps[:, k % 4, c * P:(c + 1) * P], x[:, k, c * P:(c + 1) * P], ident[:, :])
                last.then_inc(ot_done, 1)

        @block.gpsimd
        def _(pool):
            pool.memset(ident[:, :], 0.0).then_inc(ident_set, 1)
            pool.memset(causal[:, :], 0.0).then_inc(ident_set, 1)
            pool.memset(ones[:, :], 1.0).then_inc(ident_set, 1)
            pool.wait_ge(ident_set, 3)
            pool.affine_select(out=ident[:, :], in_=ident[:, :], compare_op=ALU.not_equal, fill=1.0, base=0,
                               pattern=[[-1, P]], channel_multiplier=1).then_inc(ident_set, 1)
            pool.affine_select(out=causal[:, T - P:T], in_=causal[:, T - P:T], compare_op=ALU.is_ge, fill=MASKED,
                               base=0, pattern=[[-1, P]], channel_multiplier=1).then_inc(ident_set, 1)
            pool.memset(power[:, :], -0.5).then_inc(ident_set, 1)

            def sums(ev, l):
                for k in range(1, SQUARES[ev] - (ev in POST)):
                    pool.wait_ge(sq_done, l * NSQ + squares_before(ev) + k + 1)
                    if k > 1:
                        pool.wait_ge(add_done, l * NADD + adds_before(ev) + k - 1)
                    pool.tensor_tensor(sq[:, 0, :], sq[:, 0, :], sq[:, 1, :], ALU.add).then_inc(add_done, 1)

            def rsqrt(ev, l):
                pool.wait_ge(var_done, l * NEV + EVENTS.index(ev) + 1)
                pool.tensor_tensor(rstd[:, :], var[:, :], power[:, :], ALU.pow).then_inc(rstd_done, 1)

            pool.wait_ge(ident_set, 6)
            sums("pre_mix", 0)
            with pool.Fori(0, DEPTH) as l:
                rsqrt("pre_mix", l)
                for j in range(1, CF_TAPS):
                    pool.wait_ge(cf_prod, l * CF_TAPS + j + 1)
                    if j > 1:
                        pool.wait_ge(cf_sum, l * (CF_TAPS - 1) + j - 1)
                    pool.tensor_tensor(cf_out[:, 1, :], cf_out[:, 1, :], cf_tmp[:, j % 2, :], ALU.add)\
                        .then_inc(cf_sum, 1)
                for ev in ("ckv", "cq"):
                    sums(ev, l)
                    rsqrt(ev, l)
                sums("ln", l)
                r = slice(0, MLA_QK)
                pool.wait_ge(rope_in, l * 32 + 32)
                for h in range(HEADS + 1):
                    if h < HEADS:
                        pool.wait_ge(evac, l * N_EVAC + G_MQ + h + 1)
                        pool.tensor_tensor(ml_shuf[r, h % 2, :], ml_shuf[r, h % 2, :], rope[r, 1, :], ALU.mult)\
                            .then_inc(rot_sin, 1)
                        pool.wait_ge(rot_sin, l * HEADS + h + 1)
                        pool.tensor_tensor(ml_rot[r, h, :], ml_rot[r, h, :], ml_shuf[r, h % 2, :], ALU.add)\
                            .then_inc(rot_done, 1)
                    if h == 1:
                        rsqrt("ln", l)
                    if h:
                        pool.wait_ge(rot_hi, l * 8 + 4 + h)
                        pool.tensor_tensor(ml_q[h - 1][r, 1, :], ml_rot[r, h - 1, :], fp(ml_q[h - 1][r, 0, :]),
                                           ALU.subtract).then_inc(qk_ready, 1)
                for u in range(U_OUT, U_OUT + LEAD):
                    pool.wait_ge(lo_done, l * NU + u)
                    split_lo(pool, u, l)
                for ev in EVENTS[4:]:
                    sums(ev, l)
                    rsqrt(ev, l)
                sums("pre_mix", l + 1)

        @block.vector
        def _(dve):
            class Steps:
                n, base = 0, 0

                def mark(self, ins):
                    ins.then_inc(v_step, 1)
                    self.n += 1

                def wait(self):
                    dve.wait_ge(v_step, self.base + self.n)

            st = Steps()

            def own(s, count):
                dve.wait_ge(s, count)

            def normed_lo(gain, k, n, l):
                dve.wait_ge(xh_done, l * N_XH + n + 1)
                dve.scalar_tensor_tensor(xn[:, k, 1, :], x[:, k, :], gain, fp(xn[:, k, 0, :]),
                                         ALU.mult, ALU.subtract).then_inc(xl_done, 1)

            for l0 in range(DEPTH):
                dve.wait_ge(vt_done, l0 + 1)
                dve.tensor_copy(vec_all[:, l0, :], ps[:, 5 + l0, 0:NVEC]).then_inc(vec_all_set, 1)
            own(vec_all_set, DEPTH)
            dve.tensor_copy(gain_next[:, :], vec_all[:, 0, VC["norm_mix_pre"]:VC["norm_mix_pre"] + KD])\
               .then_inc(gain_set, 1)
            for k in range(KD + 1):
                if k < KD:
                    dve.wait_ge(xt_done, k + 1)
                    dve.tensor_copy(x[:, k, :], ps[:, k % 4, :]).then_inc(x_done, 1)
                if k:
                    own(x_done, k)
                    normed_lo(gain_next[:, k - 1:k], k - 1, k - 1, 0)
                if k in SPLIT_AFTER:
                    split_lo(dve, SPLIT_AFTER.index(k), 0)

            def event_var(ev, l):
                dve.wait_ge(stat_done, l * NEV + EVENTS.index(ev) + 1)
                dve.tensor_scalar(var[:, :], ps[:, STAT, 0:TC], 1.0 / WIDTH[ev], EPS, ALU.mult, ALU.add)\
                   .then_inc(var_done, 1)

            def scale_ready(ev, l):
                if ev == "pre_mix":
                    dve.wait_ge(scale_done, l * 2 + 1)
                elif ev == "pre_ffn":
                    dve.wait_ge(scale_done, l * 2 + 2)
                else:
                    dve.wait_ge(spread_done, l * NEV + EVENTS.index(ev) + 1)

            def group_ready(g, l):
                dve.wait_ge(group_done, l * NG + g + 1)

            with dve.Fori(0, DEPTH) as l:
                st.base, st.n = l * V_STEPS, 0
                dve.wait_ge(vec_all_set, 2)
                dve.tensor_copy(vec[:, :], vec_all[:, l, :]).then_inc(vec_set, 1)
                dve.memset(cf_u[:, :, 0:CF_TAPS - 1], 0.0)
                st.mark(dve.memset(sc_u[:, 0:SC_TAPS - 1], 0.0))
                own(vec_set, l + 1)
                split_lo(dve, 3, l)
                split_lo(dve, 4, l)
                event_var("pre_mix", l)
                dve.wait_ge(rstd_done, l * NEV + 1)
                dve.tensor_copy(rstd_mix[:, :], rstd[:, :]).then_inc(mix_set, 1)
                own(mix_set, l + 1)
                split_lo(dve, 5, l)
                scale_ready("pre_mix", l)

                def ev_count(g):
                    return l * N_EVAC + g + 1

                def scaled(dst, g, rows_=slice(0, P)):
                    dve.tensor_tensor(dst, ps[rows_, bank_of(g), :], scale_main[rows_, :], ALU.mult)\
                       .then_inc(evac, 1)
                    own(evac, ev_count(g))

                def rotate(e, shuf, half, rows_, g):
                    mask = [(j + half) % (2 * half) if j < 2 * half else j for j in range(32)]
                    src = ps[rows_, bank_of(g), :]
                    dve.tensor_tensor(e, src, rope[rows_, 0, :], ALU.mult)
                    dve.stream_shuffle(shuf, src, mask).then_inc(evac, 1)
                    own(evac, ev_count(g))
                    st.mark(dve.tensor_tensor(shuf, shuf, rope[rows_, 1, :], ALU.mult))
                    st.wait()
                    return dve.tensor_tensor(e, e, shuf, ALU.add)

                def rot_lo(n):
                    dve.wait_ge(rot_hi, l * 8 + n + 1)
                    dst, e = hid[:, (QM, KM, QM + 1, KM + 1)[n]], rot[:, n % 2, :]
                    dve.tensor_tensor(dst[:, 1, :], e, fp(dst[:, 0, :]), ALU.subtract).then_inc(qk_ready, 1)

                def group_a_lo(c):
                    dve.wait_ge(y_hi, l * 4 + c + 1)
                    dst = hid[:, Y_SLOT["a"] + c]
                    dve.tensor_tensor(dst[:, 1, :], sc_w[:, :], fp(dst[:, 0, :]), ALU.subtract).then_inc(y_ready, 1)

                cf_j = 0
                for g in range(G_MQ):
                    if g >= 3:
                        split_lo(dve, g + LEAD, l)
                    if g == G_V + 1:
                        rot_lo(3)
                    if G_V < g <= G_V + 2:
                        for j in range(2):
                            c = 2 * (g - 1 - G_V) + j
                            dve.wait_ge(val_hi, l * 6 + 2 * (g - 1 - G_V) + 2)
                            ins = dve.scalar_tensor_tensor(vm[:, 1, c, :],
                                                           ps[:, bank_of(g - 1), j * GW:(j + 1) * GW],
                                                           rstd_mix[:, c:c + 1], fp(vm[:, 0, c, :]),
                                                           ALU.mult, ALU.subtract)
                            if j:
                                ins.then_inc(evac, 1)
                    if g == G_KR + 2:
                        dve.wait_ge(kr_hi, l + 1)
                        dve.tensor_tensor(kr[DH:MLA_QK, 1, :], rot[DH:MLA_QK, 0, :], fp(kr[DH:MLA_QK, 0, :]),
                                          ALU.subtract).then_inc(kr_lo, 1)
                    if g in (14, 17):
                        event_var("ckv" if g == 14 else "cq", l)
                    if g == 16:
                        scale_ready("ckv", l)
                        dve.tensor_tensor(lat[:, 3, :], lat[:, 3, :], ps[:, STAT, :], ALU.mult).then_inc(lat_norm, 1)
                    if g == 18:
                        dve.wait_ge(lat_hi, l * 4 + 1)
                        dst = hid[:, CKVN]
                        dve.scalar_tensor_tensor(dst[:, 1, :], lat[:, 3, :], col("mla_kv_norm"), fp(dst[:, 0, :]),
                                                 ALU.mult, ALU.subtract).then_inc(lat_ready, 1)
                    if g == 18:
                        scale_ready("cq", l)
                        for j in range(3):
                            dve.tensor_tensor(lat[:, j, :], lat[:, j, :], ps[:, STAT, :], ALU.mult)\
                               .then_inc(lat_norm, 1)
                        group_a_lo(0)
                    if g == 19:
                        dve.wait_ge(mean_done, l + 1)
                        for c in range(2):
                            dve.scalar_tensor_tensor(cf_out[:, c, :], ps[:, STAT, :], -1.0 / GW, cf_out[:, c, :],
                                                     ALU.mult, ALU.add).then_inc(cf_cent, 1)
                    if g == 20:
                        for j in range(3):
                            dve.wait_ge(lat_hi, l * 4 + j + 2)
                            dst = hid[:, CQN + j]
                            dve.scalar_tensor_tensor(dst[:, 1, :], lat[:, j, :], col("mla_q_norm", j),
                                                     fp(dst[:, 0, :]), ALU.mult, ALU.subtract)\
                               .then_inc(lat_ready, 1)
                    if g not in (G_V, G_V + 1):
                        group_ready(g, l)
                    if g in (0, 2):
                        scaled(rot[:, g // 2, :], g)
                    elif g in (1, 3):
                        c = g // 2
                        u = cf_u[:, c, CF_TAPS - 1:]
                        dve.scalar_tensor_tensor(u, ps[:, bank_of(g), :], 0.5, scale_main[:, :], ALU.mult,
                                                 ALU.mult).then_inc(evac, 1)
                        dve.wait_ge(cf_tanh, l * 2 + c + 1)
                        own(evac, ev_count(g))
                        ins = dve.scalar_tensor_tensor(u, rot[:, c, :], 1.0, u, ALU.add, ALU.mult)
                        if c:
                            ins.then_inc(cf_u_set, 1)
                        else:
                            st.mark(ins)
                    elif G_QK <= g < G_V:
                        n = g - G_QK
                        if n == 0:
                            dve.wait_ge(rope_in, l * 32 + 16)
                            st.mark(dve.tensor_tensor(rope[:, :, :], rope[:, :, :],
                                                      scale_main[:, :].unsqueeze(1).to_broadcast([P, 2, T]),
                                                      ALU.mult))
                            st.wait()
                        if n == 1:
                            own(rot_done, l * 8 + 1)
                        if n >= 2:
                            own(qk_ready, l * 8 + n - 1)
                        rotate(rot[:, n % 2, :], shuf[:, :], 8, slice(0, P), g).then_inc(rot_done, 1)
                        if n:
                            rot_lo(n - 1)
                    elif g in (G_V, G_V + 1):
                        pass
                    elif g == G_CKV:
                        scaled(lat[:, 3, :], g)
                    elif g == G_KR:
                        r = slice(DH, MLA_QK)
                        dve.wait_ge(rope_in, l * 32 + 32)
                        own(qk_ready, l * 8 + 4)
                        st.mark(rotate(rot[r, 0, :], shuf[r, :], 16, r, g))
                        st.wait()
                        dve.tensor_tensor(rot[r, 0, :], rot[r, 0, :], scale_main[r, :], ALU.mult)\
                           .then_inc(kr_done, 1)
                    elif g < G_SC:
                        scaled(lat[:, g - G_CQ, :], g)
                    else:
                        c, kind = divmod(g - G_SC, 3)
                        if kind == 0:
                            if c:
                                own(y_ready, l * 4 + 1)
                            scaled(sc_w[:, :], g)
                        elif kind == 1:
                            scaled(sc_u[:, SC_TAPS - 1:], g)
                            st.mark(dve.tensor_tensor(sc_u[:, SC_TAPS - 1:], sc_u[:, SC_TAPS - 1:], sc_w[:, :],
                                                      ALU.mult))
                            st.wait()
                            st.mark(dve.tensor_scalar(sc_w[:, :], sc_u[:, 0:T], col("conv_a", c), None, ALU.mult))
                            for j in range(1, SC_TAPS):
                                st.wait()
                                st.mark(dve.scalar_tensor_tensor(sc_w[:, :], sc_u[:, j:j + T],
                                                                 col("conv_a", 2 * j + c), sc_w[:, :],
                                                                 ALU.mult, ALU.add))
                        else:
                            st.wait()
                            scaled(sc_u[:, SC_TAPS - 1:], g)
                            dve.tensor_tensor(sc_w[:, :], sc_w[:, :], sc_u[:, SC_TAPS - 1:], ALU.mult)\
                               .then_inc(sc_val, 1)
                    for _ in range(CF_VECTOR.get(g, 0)):
                        st.wait()
                        j, cf_j = cf_j, cf_j + 1
                        if j == 0:
                            ins = dve.tensor_scalar(cf_out[:, 0, :], cf_u[:, 0, 0:T], col("conv_b", 0),
                                                    col("conv_b_bias", 0), ALU.mult, ALU.add)
                        else:
                            ins = dve.scalar_tensor_tensor(cf_out[:, 0, :], cf_u[:, 0, j:j + T],
                                                           col("conv_b", 2 * j), cf_out[:, 0, :],
                                                           ALU.mult, ALU.add)
                        if j == CF_TAPS - 1:
                            ins.then_inc(cf_conv, 1)
                        else:
                            st.mark(ins)
                for h in range(HEADS):
                    g, n = G_MQ + h, 4 + h
                    r = slice(0, MLA_QK)
                    if h == 0:
                        own(sc_val, l * 2 + 2)
                    elif h >= 2:
                        dve.wait_ge(rot_done, l * 8 + n - 1)
                    group_ready(g, l)
                    dve.tensor_tensor(ml_rot[r, h, :], ps[r, bank_of(g), :], rope[r, 0, :], ALU.mult)
                    dve.stream_shuffle(ml_shuf[r, h % 2, :], ps[r, bank_of(g), :],
                                       [(j + 16) % 32 for j in range(32)]).then_inc(evac, 1)
                    if h == 0:
                        group_a_lo(1)
                    if h == 1:
                        event_var("ln", l)
                scale_ready("ln", l)
                for c in range(2):
                    dve.tensor_tensor(cf_out[:, c, :], cf_out[:, c, :], ps[:, STAT, :], ALU.mult).then_inc(cf_norm, 1)
                for h in range(HEADS):
                    g = G_MK + h
                    dve.wait_ge(kn_hi, l * 4 + h + 1)
                    dve.tensor_tensor(ml_k[h][0:DH, 1, :], ps[0:DH, bank_of(g), :], fp(ml_k[h][0:DH, 0, :]),
                                      ALU.subtract).then_inc(evac, 1)
                for half in range(2):
                    g = G_MV + half
                    dve.wait_ge(val_hi, l * 6 + 5 + half)
                    dve.tensor_tensor(vl[:, 1, 2 * half:2 * half + 2, :],
                                      ps[:, bank_of(g), :].rearrange("p (c d) -> p c d", c=2),
                                      fp(vl[:, 0, 2 * half:2 * half + 2, :]), ALU.subtract).then_inc(evac, 1)

                def head_rows(h):
                    return slice(DH * (h % 2), DH * (h % 2) + DH)

                for t in range(N_ATT + ATT_TAIL):
                    if t < N_ATT:
                        c = t % TC
                        n = (c + 1) * P
                        dve.wait_ge(ident_set, 6)
                        dve.wait_ge(score_done, l * N_ATT + t + 1)
                        if t >= 2:
                            dve.wait_ge(exp_done, l * N_ATT + t - 1)
                        if t == 0:
                            own(evac, l * N_EVAC + G_PV)
                        dve.memset(negmax[:, t:t + 1], 0.0)
                        dve.tensor_tensor_reduce(out=sm[:, t % 2, 0:n], in0=ps[:, SCORE0 + t % 2, 0:n],
                                                 in1=causal[:, T - n:T], scale=1.0, scalar=-3e38,
                                                 op0=ALU.add, op1=ALU.max, accum_out=rowmax[:, t:t + 1])\
                           .then_inc(masked, 1)
                        own(masked, l * N_ATT + t + 1)
                        dve.tensor_scalar(negmax[:, t:t + 1], rowmax[:, t:t + 1],
                                          -(MOBA_SCALE if t < N_ATT // 2 else MLA_SCALE), None, ALU.mult)\
                           .then_inc(negmax_done, 1)
                    if 1 <= t <= N_ATT:
                        s = t - 1
                        n = (s % TC + 1) * P
                        dve.wait_ge(exp_done, l * N_ATT + s + 1)
                        st.mark(dve.reciprocal(rowinv[:, s:s + 1], rowsum[:, s:s + 1]))
                        st.wait()
                        dve.tensor_scalar(prob[:, s % NPROB, 0:n], prob[:, s % NPROB, 0:n], rowinv[:, s:s + 1], None,
                                          ALU.mult).then_inc(prob_done, 1)
                    if TRAIL <= t < N_ATT + TRAIL:
                        s = t - TRAIL
                        c = s % TC
                        dve.wait_ge(pt_hi, l * N_ATT + s + 1)
                        src = ps[:, PT_BANKS[s % 2], 0:(c + 1) * P].rearrange("p (k t) -> p k t", t=P)
                        dve.tensor_tensor(pt_of(s // TC, c, 1), src, fp(pt_of(s // TC, c, 0)), ALU.subtract)\
                           .then_inc(pt_ready, 1)
                    if t in (1, 2):
                        c = t - 1
                        dve.wait_ge(cf_swish, l * 2 + c + 1)
                        dve.scalar_tensor_tensor(cf_out[:, c, :], cf_th[:, c, :], 1.0, cf_out[:, c, :],
                                                 ALU.add, ALU.mult).then_inc(cf_val, 1)
                    if t in (5, 6):
                        c = t - 5
                        dve.wait_ge(y_hi, l * 4 + c + 3)
                        dst = hid[:, Y_SLOT["b"] + c]
                        dve.scalar_tensor_tensor(dst[:, 1, :], cf_out[:, c, :], 0.5, fp(dst[:, 0, :]),
                                                 ALU.mult, ALU.subtract).then_inc(y_ready, 1)
                    h, r = divmod(t - TRAIL - VALUES_AFTER[2] - 1, TC)
                    if r == 0 and 0 <= h < 2 * HEADS:
                        dst = hid[head_rows(h), Y_SLOT["c"] + h // 2]
                        dve.wait_ge(pv_hi, l * 2 * HEADS + h + 1)
                        dve.tensor_tensor(dst[:, 1, :], ps[head_rows(h), bank_of(G_PV + h), :], fp(dst[:, 0, :]),
                                          ALU.subtract).then_inc(evac, 1)

                def updates(ev, n0, normed):
                    last = SQUARES[ev] - 1
                    dve.wait_ge(sq_done, l * NSQ + squares_before(ev) + last + 1)
                    dve.wait_ge(add_done, l * NADD + adds_before(ev) + last - 1)
                    dve.tensor_tensor(sq[:, 0, :], sq[:, 0, :], sq[:, 1, :], ALU.add).then_inc(add_done, 1)
                    event_var(ev, l)
                    dve.wait_ge(y_evac, l * N_YEVAC + n0 + KD)
                    scale_ready(ev, l)
                    for k in range(KD + 1):
                        if k < KD:
                            st.mark(dve.tensor_tensor(y[:, k, 1, :], y[:, k, 1, :], ps[:, STAT, :], ALU.mult))
                        if k:
                            normed(k - 1)
                        if k < KD:
                            st.wait()
                            dve.tensor_tensor(x[:, k, :], x[:, k, :], y[:, k, 1, :], ALU.add).then_inc(x_done, 1)
                            own(x_done, KD + l * 2 * KD + n0 + k + 1)

                dve.wait_ge(lo_done, l * NU + U_OUT + LEAD)
                for m in range(KD):
                    split_lo(dve, U_OUT + m + LEAD, l)
                dve.tensor_copy(gain_next[:, :],
                                vec_all[:, (l + 1) % DEPTH, VC["norm_mix_pre"]:VC["norm_mix_pre"] + KD])\
                   .then_inc(gain_set, 1)
                dve.memset(e_g[:, 0:FFN_TAPS - 1], 0.0)
                st.mark(dve.memset(e_v[:, 0:FFN_TAPS - 1], 0.0))
                updates("post_mix", 0, lambda k: normed_lo(col("norm_ffn_pre", k), k, KD + k, l))
                split_lo(dve, U_UP + LEAD, l)
                split_lo(dve, U_UP + LEAD + 1, l)
                event_var("pre_ffn", l)
                split_lo(dve, U_UP + LEAD + 2, l)
                scale_ready("pre_ffn", l)

                def taps(dst, src, w, last):
                    st.mark(dve.tensor_scalar(dst, src[:, 0:T], w(0), None, ALU.mult))
                    for j in range(1, FFN_TAPS):
                        st.wait()
                        ins = dve.scalar_tensor_tensor(dst, src[:, j:j + T], w(j), dst, ALU.mult, ALU.add)
                        if j == FFN_TAPS - 1 and last is not None:
                            ins.then_inc(last, 1)
                        else:
                            st.mark(ins)

                def hidden_lo(p):
                    dve.wait_ge(f_hi, l * NF + p + 1)
                    dve.tensor_tensor(hid[:, p, 1, :], c_v[:, :], fp(hid[:, p, 0, :]), ALU.subtract)\
                       .then_inc(f_ready, 1)

                def ffn_body(i, first):
                    for jj in range(2):
                        p = i * 2 + jj
                        for half, (e, cc) in enumerate(((e_g, c_g), (e_v, c_v))):
                            j = 2 * jj + half
                            u = U_UP + j + LEAD
                            if not (first and j < 3):
                                dve.wait_ge(hi_done, l * NU + i * 4 + u + 1)
                                dve.tensor_tensor(wsp[:, u % SPLIT, 1, :], raw[:, u % RAW, :],
                                                  fp(wsp[:, u % SPLIT, 0, :]), ALU.subtract).then_inc(lo_done, 1)
                            dve.wait_ge(group_done, l * NG + i * 4 + G_UP + j + 1)
                            dve.tensor_tensor(e[:, FFN_TAPS - 1:], ps[:, bank_up(j, first), :], scale_main[:, :], ALU.mult)\
                               .then_inc(evac, 1)
                            if half == 0 and not (first and jj == 0):
                                hidden_lo(p - 1)
                            own(evac, l * N_EVAC + i * 4 + G_OUT + j + 1)

                            def w(k):
                                a = VC["conv_ffn"] + k * 2 * NF + half * NF
                                return vec[:, bass.ds(p + a, 1)]

                            if half and not (first and jj == 0):
                                own(f_ready, l * NF + p)
                            taps(cc[:, :], e, w, c_gate if half == 0 else None)
                        dve.wait_ge(tanh_done, l * NF + p + 1)
                        st.mark(dve.scalar_tensor_tensor(th[:, :], th[:, :], 1.0, c_g[:, :], ALU.add, ALU.mult))
                        st.wait()
                        dve.scalar_tensor_tensor(c_v[:, :], th[:, :], 0.5, c_v[:, :], ALU.mult, ALU.mult)\
                           .then_inc(f_done, 1)

                n0 = st.n
                ffn_body(0, True)
                per_body = st.n - n0
                with dve.Fori(1, NF // 2) as i:
                    st.base, st.n = l * V_STEPS + i * per_body, n0
                    ffn_body(i, False)
                    assert st.n == n0 + per_body
                st.base, st.n = l * V_STEPS, n0 + per_body * (NF // 2)
                hidden_lo(NF - 1)

                with dve.Fori(0, 2) as i:
                    for j in range(12):
                        u = U_DOWN + j + LEAD
                        dve.wait_ge(hi_done, l * NU + i * 12 + u + 1)
                        dve.tensor_tensor(wsp[:, u % SPLIT, 1, :], raw[:, u % RAW, :],
                                          fp(wsp[:, u % SPLIT, 0, :]), ALU.subtract).then_inc(lo_done, 1)
                updates("post_ffn", KD, lambda k: normed_lo(gain_next[:, k:k + 1], k, k, l + 1))
                assert st.n == V_STEPS, st.n

        @block.scalar
        def _(act):
            act.preload_act_table_set("exp_and_others")
            for name, a, n in SMALL:
                v = inp[name]
                if len(v.shape) == 3:
                    v = v.rearrange("l j f -> l (j f)")
                act.dma_start(rows[a:a + n, :, 0, :], v.rearrange("l (r c) -> r l c", c=P)).then_inc(rows_in, 16)
            v = inp["conv_ffn"].rearrange("l j f -> l (j f)")
            for t in range(2):
                act.dma_start(rows[0:HALFROWS, :, 1 + t, :],
                              v[:, t * HALFROWS * P:(t + 1) * HALFROWS * P].rearrange("l (r c) -> r l c", c=P))\
                   .then_inc(rows_in, 16)
            rope_v = [r.rearrange("s p t -> p s t") for r in rope_tables]
            act.dma_start(rope[:, :, :], rope_v[0]).then_inc(rope_in, 16)
            def square(ev, k, src, l):
                if k == 0 and not (isinstance(l, int) and l == 0):
                    act.wait_ge(stat_done, l * NEV + EVENTS.index(ev))
                elif k >= 2:
                    act.wait_ge(add_done, l * NADD + adds_before(ev) + k - 1)
                act.activation(sq[:, min(k, 1), :], src, ACT.Square).then_inc(sq_done, 1)

            def copy_scale(ev, l):
                act.wait_ge(spread_done, l * NEV + EVENTS.index(ev) + 1)
                act.activation(scale_main[:, :], ps[:, STAT, :], ACT.Copy).then_inc(scale_done, 1)

            def group_ready(g, l):
                act.wait_ge(group_done, l * NG + g + 1)

            def normed_hi(gain, k, n, l):
                act.wait_ge(x_done, l * 2 * KD + n + 1)
                act.activation(xn[:, k, 0, :], x[:, k, :], ACT.Copy, scale=gain).then_inc(xh_done, 1)

            act.wait_ge(gain_set, 1)
            for k in range(KD):
                normed_hi(gain_next[:, k:k + 1], k, k, 0)
                square("pre_mix", k, x[:, k, :], 0)
                if k + 1 in SPLIT_AFTER:
                    split_hi(act, SPLIT_AFTER.index(k + 1), 0, first=True)
            with act.Fori(0, DEPTH) as l:
                act.wait_ge(vec_set, l + 1)
                for u in (3, 4, 5):
                    split_hi(act, u, l)
                copy_scale("pre_mix", l)

                def rot_hi_part(n):
                    act.wait_ge(rot_done, l * 8 + n + 1)
                    if n < 4:
                        dst, e = hid[:, (QM, KM, QM + 1, KM + 1)[n]], rot[:, n % 2, :]
                    else:
                        dst, e = xn[0:MLA_QK, n - 4], ml_rot[0:MLA_QK, n - 4, :]
                    act.activation(dst[:, 0, :], e, ACT.Copy).then_inc(rot_hi, 1)

                def group_a_hi(c):
                    act.wait_ge(sc_val, l * 2 + c + 1)
                    act.activation(hid[:, Y_SLOT["a"] + c, 0, :], sc_w[:, :], ACT.Copy).then_inc(y_hi, 1)

                cf_j = 0
                for g in range(G_MQ):
                    if g >= 3:
                        split_hi(act, g + LEAD, l)
                    if g in (0, 2):
                        c = g // 2
                        act.wait_ge(evac, l * N_EVAC + g + 1)
                        act.activation(rot[:, c, :], rot[:, c, :], ACT.Tanh, scale=0.5).then_inc(cf_tanh, 1)
                    if G_QK < g <= G_V:
                        rot_hi_part(g - 1 - G_QK)
                    if G_V < g <= G_V + 2:
                        act.wait_ge(mix_set, l + 1)
                        group_ready(g - 1, l)
                        for j in range(2):
                            c = 2 * (g - 1 - G_V) + j
                            act.activation(vm[:, 0, c, :], ps[:, bank_of(g - 1), j * GW:(j + 1) * GW], ACT.Copy,
                                           scale=rstd_mix[:, c:c + 1]).then_inc(val_hi, 1)
                    for _ in range(CF_SCALAR.get(g, 0)):
                        j, cf_j = cf_j, cf_j + 1
                        if j == 0:
                            act.wait_ge(cf_u_set, l + 1)
                            act.activation(cf_out[:, 1, :], cf_u[:, 1, 0:T], ACT.Identity, scale=col("conv_b", 1),
                                           bias=col("conv_b_bias", 1)).then_inc(cf_prod, 1)
                            continue
                        if j > 2:
                            act.wait_ge(cf_sum, l * (CF_TAPS - 1) + j - 2)
                        act.activation(cf_tmp[:, j % 2, :], cf_u[:, 1, j:j + T], ACT.Copy,
                                       scale=col("conv_b", 2 * j + 1)).then_inc(cf_prod, 1)
                    if g == G_V + 1:
                        act.wait_ge(rot_done, l * 8 + 4)
                        act.dma_start(rope[:, :, :], rope_v[1]).then_inc(rope_in, 16)
                    if g == G_KR + 1:
                        act.wait_ge(kr_done, l + 1)
                        act.activation(kr[DH:MLA_QK, 0, :], rot[DH:MLA_QK, 0, :], ACT.Copy).then_inc(kr_hi, 1)
                    if g == 12:
                        act.wait_ge(evac, l * N_EVAC + G_CKV + 1)
                        square("ckv", 0, lat[:, 3, :], l)
                    if g == 17:
                        act.wait_ge(lat_norm, l * 4 + 1)
                        act.activation(hid[:, CKVN, 0, :], lat[:, 3, :], ACT.Copy, scale=col("mla_kv_norm"))\
                           .then_inc(lat_hi, 1)
                    if g == 16:
                        for j in range(3):
                            act.wait_ge(evac, l * N_EVAC + G_CQ + j + 1)
                            square("cq", j, lat[:, j, :], l)
                    if g == 17:
                        group_a_hi(0)
                    if g == 19:
                        for j in range(3):
                            act.wait_ge(lat_norm, l * 4 + j + 2)
                            act.activation(hid[:, CQN + j, 0, :], lat[:, j, :], ACT.Copy,
                                           scale=col("mla_q_norm", j)).then_inc(lat_hi, 1)
                    if g == 20:
                        for c in range(2):
                            act.wait_ge(cf_cent, l * 2 + c + 1)
                            square("ln", c, cf_out[:, c, :], l)
                group_a_hi(1)

                act.wait_ge(kr_lo, l + 1)
                act.wait_ge(group_done, l * NG + G_MQ)
                for s in range(2):
                    act.activation(xn[DH:MLA_QK, HEADS:2 * HEADS, s, :],
                                   fp(kr[DH:MLA_QK, s, :]).unsqueeze(1).to_broadcast([MLA_ROPE, HEADS, T]),
                                   ACT.Copy).then_inc(kr_spread, 1)
                rot_hi_part(4)
                for h in range(HEADS):
                    group_ready(G_MK + h, l)
                    act.activation(ml_k[h][0:DH, 0, :], ps[0:DH, bank_of(G_MK + h), :], ACT.Copy).then_inc(kn_hi, 1)
                for half in range(2):
                    group_ready(G_MV + half, l)
                    act.activation(vl[:, 0, 2 * half:2 * half + 2, :],
                                   ps[:, bank_of(G_MV + half), :].rearrange("p (c d) -> p c d", c=2),
                                   ACT.Copy).then_inc(val_hi, 1)
                for c in range(2):
                    act.wait_ge(cf_norm, l * 2 + c + 1)
                    act.activation(cf_out[:, c, :], cf_out[:, c, :], ACT.Identity, scale=col("ln_b_gain", c),
                                   bias=col("ln_b_bias", c)).then_inc(cf_affine, 1)
                for c in range(2):
                    act.wait_ge(cf_affine, l * 2 + c + 1)
                    act.activation(cf_th[:, c, :], cf_out[:, c, :], ACT.Tanh, scale=0.5).then_inc(cf_swish, 1)
                rot_hi_part(5)

                for t in range(N_ATT + ATT_TAIL):
                    if TRAIL <= t < N_ATT + TRAIL:
                        s = t - TRAIL
                        h, c = divmod(s, TC)
                        if c == 0 and h >= 2:
                            group_ready(G_PV + h - 2, l)
                        act.wait_ge(pt_done, l * N_ATT + s + 1)
                        act.activation(pt_of(h, c, 0),
                                       ps[:, PT_BANKS[s % 2], 0:(c + 1) * P].rearrange("p (k t) -> p k t", t=P),
                                       ACT.Copy).then_inc(pt_hi, 1)
                    if t < N_ATT:
                        n = (t % TC + 1) * P
                        if t >= NPROB:
                            act.wait_ge(pt_done, l * N_ATT + t - NPROB + 1)
                        if t == 0:
                            act.wait_ge(kr_spread, l * 2 + 2)
                        act.wait_ge(negmax_done, l * N_ATT + t + 1)
                        act.activation(prob[:, t % NPROB, 0:n], sm[:, t % 2, 0:n], ACT.Exp, bias=negmax[:, t:t + 1],
                                       scale=MOBA_SCALE if t < N_ATT // 2 else MLA_SCALE,
                                       accum_out=rowsum[:, t:t + 1]).then_inc(exp_done, 1)
                    if t in (3, 4):
                        c = t - 3
                        act.wait_ge(cf_val, l * 2 + c + 1)
                        act.activation(hid[:, Y_SLOT["b"] + c, 0, :], cf_out[:, c, :], ACT.Copy, scale=0.5)\
                           .then_inc(y_hi, 1)
                    if t in (5, 6):
                        rot_hi_part(t + 1)
                    if t in (7, 8, 9):
                        split_hi(act, U_OUT + t - 7, l)
                    if t == 8:
                        act.wait_ge(rot_done, l * 8 + 8)
                        act.dma_start(rope[:, :, :], rope_v[0]).then_inc(rope_in, 16)
                    h, r = divmod(t - TRAIL - VALUES_AFTER[2] - 1, TC)
                    if r == 0 and 0 <= h < 2 * HEADS:
                        rr = slice(DH * (h % 2), DH * (h % 2) + DH)
                        group_ready(G_PV + h, l)
                        act.activation(hid[rr, Y_SLOT["c"] + h // 2, 0, :], ps[rr, bank_of(G_PV + h), :], ACT.Copy)\
                           .then_inc(pv_hi, 1)

                for m in range(KD):
                    split_hi(act, U_OUT + m + LEAD, l)
                    group_ready(G_OUT + m, l)
                    square("post_mix", m, ps[:, m % 4, :], l)
                    act.activation(y[:, m, 1, :], ps[:, m % 4, :], ACT.Copy, scale=col("norm_mix_post", m))\
                       .then_inc(y_evac, 1)
                for k in range(KD):
                    normed_hi(col("norm_ffn_pre", k), k, KD + k, l)
                    square("pre_ffn", k, x[:, k, :], l)
                for u in range(U_UP + LEAD, U_UP + LEAD + 3):
                    split_hi(act, u, l)
                copy_scale("pre_ffn", l)

                def hidden_hi(p):
                    act.wait_ge(f_done, l * NF + p + 1)
                    act.activation(hid[:, p, 0, :], c_v[:, :], ACT.Copy).then_inc(f_hi, 1)

                def split_up(i, j):
                    u = U_UP + j + LEAD
                    act.wait_ge(raw_in[u % RAW], l * (NU // RAW * 16) + i * 32 + 16 * (u // RAW + 1))
                    act.wait_ge(group_done, l * NG + i * 4 + G_UP + j)
                    act.activation(wsp[:, u % SPLIT, 0, :], raw[:, u % RAW, :], ACT.Copy).then_inc(hi_done, 1)

                def ffn_body(i, first):
                    for jj in range(2):
                        p = i * 2 + jj
                        if not first:
                            split_up(i, 2 * jj)
                        if not (first and jj == 0):
                            hidden_hi(p - 1)
                            split_up(i, 2 * jj + 1)
                        act.wait_ge(c_gate, l * NF + p + 1)
                        act.activation(th[:, :], c_g[:, :], ACT.Tanh, scale=0.5).then_inc(tanh_done, 1)

                ffn_body(0, True)
                with act.Fori(1, NF // 2) as i:
                    ffn_body(i, False)
                hidden_hi(NF - 1)

                for m in range(KD):
                    for part in range(3):
                        u = U_DOWN + 3 * m + part + LEAD
                        act.wait_ge(raw_in[u % RAW], l * (NU // RAW * 16) + 16 * (u // RAW + 1))
                        if part == 0:
                            act.wait_ge(group_done, l * NG + G_DOWN + m)
                        else:
                            act.wait_ge(down_part, l * 2 * KD + 2 * m + part)
                        act.activation(wsp[:, u % SPLIT, 0, :], raw[:, u % RAW, :], ACT.Copy).then_inc(hi_done, 1)
                    group_ready(G_DOWN + m, l)
                    square("post_ffn", m, ps[:, m % 4, :], l)
                    act.activation(y[:, m, 1, :], ps[:, m % 4, :], ACT.Copy, scale=col("norm_ffn_post", m))\
                       .then_inc(y_evac, 1)
                act.wait_ge(gain_set, l + 2)
                for k in range(KD):
                    normed_hi(gain_next[:, k:k + 1], k, k, l + 1)
                    square("pre_mix", k, x[:, k, :], l + 1)

            for k in range(KD):
                act.wait_ge(ot_done, k + 1)
                act.activation(out_tok[:, :, k * P:(k + 1) * P], ps[:, k % 4, :].rearrange("p (c f) -> p c f", f=P),
                               ACT.Copy).then_inc(out_set, 1)


_INS = ["x", "norm_mix_pre", "norm_mix_post", "norm_ffn_pre", "norm_ffn_post", "w_in", "conv_a", "conv_b",
        "conv_b_bias", "ln_b_gain", "ln_b_bias", "mla_q_norm", "mla_kv_norm", "w_uq", "w_ukv", "w_out",
        "w_ffn_up", "conv_ffn", "w_ffn_down"]
ROPE_THETA = 500000.0


def rope_table(dim, first, period, np):
    half = dim // 2
    inv = (1.0 / (np.float32(ROPE_THETA) ** (np.arange(0, dim, 2, dtype=np.float32) / np.float32(dim))))
    ang = np.arange(T, dtype=np.float32)[:, None] * inv.astype(np.float32)[None, :]
    table = np.zeros((2, P, T), np.float32)
    table[0] = 1.0
    for p0 in range(first, P, period):
        for j in range(dim):
            table[0, p0 + j] = np.cos(ang[:, j % half])
            table[1, p0 + j] = np.sin(ang[:, j % half]) * np.float32(-1.0 if j < half else 1.0)
    return table


def kernel(**inputs):
    import numpy as np
    import concourse.bacc as bacc
    from concourse.bass_utils import run_bass_kernel_spmd

    nc = bacc.Bacc("TRN2", target_bir_lowering=False, num_devices=1)
    arrays = {}

    def dram(name, a):
        arrays[name] = a
        return nc.dram_tensor(name, a.shape, mybir.dt.from_np(a.dtype), kind="ExternalInput").ap()

    inp = {name: dram(f"in_{name}", np.ascontiguousarray(inputs[name])) for name in _INS}
    tables = [dram("rope_moba", rope_table(DH // 4, 0, DH, np)), dram("rope_mla", rope_table(MLA_ROPE, DH, P, np))]
    out = nc.dram_tensor("out_x", (1, T, D), mybir.dt.float32, kind="ExternalOutput").ap()
    hybrid_trunk_kernel(nc, inp, tables, out)
    r = run_bass_kernel_spmd(nc, [arrays], core_ids=[0])
    return r.results[0]["out_x"]
```

```python
import concourse.bass as bass
from concourse import mybir
from contextlib import ExitStack

P = 128
T = 512
TC = T // P
D = 1024
KD = D // P
DEPTH = 2
GW = 256
HEADS = 4
DH = 64
MLA_ROPE = 32
MLA_QK = DH + MLA_ROPE
Q_RANK, KV_RANK = 384, 128
D_FF = 2816
NF = D_FF // P
EPS = 1e-6
MASKED = -1e30
MOBA_SCALE = DH ** -0.5
MLA_SCALE = MLA_QK ** -0.5
CF_TAPS, SC_TAPS, FFN_TAPS = 31, 3, 3

SC0 = 0
CF0 = 3 * GW
MB0 = CF0 + 2 * GW
ML0 = MB0 + 3 * GW
KR0 = ML0 + Q_RANK + KV_RANK
IN_COLS = KR0 + MLA_ROPE

SMALL = []
_at = 0
for _name, _rows in (("norm_mix_pre", KD), ("norm_mix_post", KD), ("norm_ffn_pre", KD), ("norm_ffn_post", KD),
                     ("conv_a", SC_TAPS * 2), ("conv_b", CF_TAPS * 2), ("conv_b_bias", 2), ("ln_b_gain", 2),
                     ("ln_b_bias", 2), ("mla_q_norm", 3), ("mla_kv_norm", 1)):
    SMALL.append((_name, _at, _rows))
    _at += _rows
NSMALL = _at
VC = {n: a for n, a, _ in SMALL}
VC["conv_ffn"] = NSMALL
NVEC = NSMALL + FFN_TAPS * 2 * NF
HALFROWS = NVEC // 2

W_IN_COLS = ([CF0 + GW, CF0, CF0 + GW + P, CF0 + P]
             + [MB0, MB0 + GW, MB0 + P, MB0 + GW + P]
             + [None, None]
             + [ML0 + Q_RANK, KR0 - DH]
             + [ML0, ML0 + P, ML0 + 2 * P]
             + [SC0 + 2 * GW, SC0, SC0 + GW, SC0 + 2 * GW + P, SC0 + P, SC0 + GW + P])
U_VAL = 8
U_KR = 11
U_UKV, U_UQ = 21, 22
U_OUT = 24
U_UP = U_OUT + KD
U_DOWN = U_UP + 2 * NF
DOWN_PARTS = ((0, 8), (8, 8), (16, 6))
DOWN_ORDER = [(0, 0), (0, 1), (1, 0), (0, 2), (1, 1), (1, 2)] + [(m, part) for m in (2, 3) for part in range(3)]
NU = U_DOWN + 3 * KD
RAW, SPLIT = 2, 4
LEAD = 3

G_CF, G_QK, G_V, G_CKV, G_KR, G_CQ, G_SC = 0, 4, 8, 10, 11, 12, 15
G_MK, G_MV, G_MQ, G_PV = 21, 25, 27, 31
G_OUT = 39
G_UP = G_OUT + KD
G_DOWN = G_UP + 2 * NF
NG = G_DOWN + KD

STAT, SCORE0, PT_BANKS = 4, 5, (3, 7)
RING = (0, 1, 2, 3, 5, 6, 7)
OUT_BANKS = (5, 6, 7, 3)


def bank_of(g):
    if g < G_PV:
        return RING[g % len(RING)]
    if g < G_OUT:
        return (g - G_PV) % 3
    if g < G_UP:
        return OUT_BANKS[(g - G_OUT) % 4]
    return (g - (G_UP if g < G_DOWN else G_DOWN)) % 4


def down_unit(n):
    m, part = DOWN_ORDER[n % 12]
    return n // 12 * 4 + m, part


def down_count(n):
    ends = [down_unit(i)[1] == 2 for i in range(n + 1)]
    return ends[n], ends.count(ends[n])


def bank_up(j, first):
    return OUT_BANKS[j] if first else j


def bank_before(g):
    return max((p + 1 for p in range(g) if bank_of(p) == bank_of(g)), default=0)


EVENTS = ["pre_mix", "ckv", "cq", "ln", "post_mix", "pre_ffn", "post_ffn"]
SQUARES = dict(pre_mix=KD, ln=2, ckv=1, cq=3, post_mix=KD, pre_ffn=KD, post_ffn=KD)
POST = ("post_mix", "post_ffn")
WIDTH = dict(pre_mix=D, ln=GW, ckv=KV_RANK, cq=Q_RANK, post_mix=D, pre_ffn=D, post_ffn=D)
NEV = len(EVENTS)
NSQ = sum(SQUARES.values())
ADDS = {ev: n - 1 - (ev in POST) for ev, n in SQUARES.items()}
NADD = sum(ADDS.values())


def squares_before(ev):
    return sum(SQUARES[e] for e in EVENTS[:EVENTS.index(ev)])


def adds_before(ev):
    return sum(ADDS[e] for e in EVENTS[:EVENTS.index(ev)])


N_EVAC = G_OUT + 2 * NF
N_YEVAC = 2 * KD
N_XH = 2 * KD
CF_VECTOR = {3: 2, 8: 4, 9: 4, 10: 4, 11: 1, 12: 4, 13: 4, 14: 4, 15: 4}
CF_SCALAR = {3: 1, **{g: 3 for g in range(4, 14)}}
assert sum(CF_VECTOR.values()) == CF_TAPS and sum(CF_SCALAR.values()) == CF_TAPS
N_ATT = 2 * HEADS * TC
V_STEPS = 2 + 1 + (CF_TAPS - 1) + (4 + 1 + 2) + 2 * (1 + SC_TAPS) + 2 * (1 + KD) + NF * (2 * FFN_TAPS)
SPLIT_AFTER = (1, 2, 4)
NPROB = 3
TRAIL = 3
VALUES_AFTER = (3, 5, 6)
ATT_TAIL = TRAIL + 5


def hybrid_trunk_kernel(nc, inp, rope_tables, out):
    f32 = mybir.dt.float32
    f32r = mybir.dt.float32r
    ALU = mybir.AluOpType
    ACT = mybir.ActivationFunctionType

    def fp(ap):
        return ap.bitcast(f32)

    with ExitStack() as ctx:
        sem_names = {}

        def sem(name):
            sem_names[name] = ctx.enter_context(nc.semaphore(name))
            return sem_names[name]

        base = -(-nc.sbuf_base // 32) * 32
        at = [base]

        def place(name, shape, dt, offset=None):
            size = 4
            for n in shape[1:]:
                size *= n
            if offset is None:
                offset = at[0]
                at[0] += -(-size // 32) * 32
            return nc.alloc_sbuf_tensor_at(name, shape, dt, offset=offset)

        x = place("x", [P, KD, T], f32)
        xn_at = at[0]
        xn = place("xn", [P, KD, 2, T], f32r)
        slots_at = at[0]
        hid = place("hid", [P, NF, 2, T], f32r)
        SLOT = 2 * T * 4
        raw = place("raw", [P, RAW, 8 * P], f32)
        wsp = place("wsp", [P, SPLIT, 2, 8 * P], f32r)
        ident = place("ident", [P, P], f32)
        ones = place("ones", [P, P], f32)
        causal = place("causal", [P, T], f32)
        rope = place("rope", [P, 2, T], f32)
        scale_main = place("scale_main", [P, T], f32)
        vec_all = place("vec_all", [P, DEPTH, NVEC], f32)
        vec = place("vec", [P, NVEC], f32)
        gain_next = place("gain_next", [P, KD], f32)
        var = place("var", [P, TC], f32)
        rstd = place("rstd", [P, TC], f32)
        power = place("power", [P, TC], f32)
        rstd_mix = place("rstd_mix", [P, TC], f32)
        rowmax = place("rowmax", [P, N_ATT], f32)
        negmax = place("negmax", [P, N_ATT], f32)
        rowsum = place("rowsum", [P, N_ATT], f32)
        rowinv = place("rowinv", [P, N_ATT], f32)
        tmp_at = at[0]
        cf_out = place("cf_out", [P, 2, T], f32, tmp_at)
        sc_u = place("sc_u", [P, T + 2], f32, tmp_at + 4096)
        kr = place("kr", [P, 2, T], f32r, tmp_at + 6176)
        sq = place("sq", [P, 2, T], f32, tmp_at + 10336)
        sm = place("sm", [P, 2, T], f32, tmp_at + 10336)
        prob = place("prob", [P, NPROB, T], f32, tmp_at + 4096)
        e_g = place("e_g", [P, T + 2], f32, tmp_at)
        e_v = place("e_v", [P, T + 2], f32, tmp_at + 2080)
        c_g = place("c_g", [P, T], f32, tmp_at + 4160)
        c_v = place("c_v", [P, T], f32, tmp_at + 6208)
        th = place("th", [P, T], f32, tmp_at + 8256)
        assert tmp_at + 10336 + 4096 <= nc.sbuf_usable_end, (tmp_at + 14432, nc.sbuf_usable_end)

        Y_SLOT = dict(a=0, b=2, c=4, d=6)
        QM, KM, VM, VL, CQN, CKVN, PT = 8, 10, 12, 14, 16, 19, 16

        def slot(n):
            return slots_at + n * SLOT

        vm = hid[:, VM:VM + 2, :, :].rearrange("p a b t -> p (a b t)").rearrange("p (s c d) -> p s c d", s=2, c=TC)
        vl = hid[:, VL:VL + 2, :, :].rearrange("p a b t -> p (a b t)").rearrange("p (s c d) -> p s c d", s=2, c=TC)
        pt_early = hid[:, PT:PT + 2, :, :].rearrange("p a b t -> p (a b t)")\
            .rearrange("p (n s k t) -> p n s k t", n=2, s=2, k=2)
        pt_late = hid[:, PT + 2:PT + 6, :, :].rearrange("p a b t -> p (a b t)")\
            .rearrange("p (n s k t) -> p n s k t", n=2, s=2, k=4)

        def pt_of(h, c, s):
            tile = pt_early if c < 2 else pt_late
            return tile[:, h % 2, s, 0:c + 1, (c % 2) * P:(c % 2 + 1) * P]

        cf_u = place("cf_u", [P, 2, T + CF_TAPS - 1], f32, slot(VL))
        sc_w = place("sc_w", [P, T], f32, slot(VL) + 5120)
        rot = place("rot", [P, 2, T], f32, slot(Y_SLOT["d"]))
        shuf = place("shuf", [P, T], f32, slot(Y_SLOT["d"] + 1))
        cf_th = place("cf_th", [P, 2, T], f32, slot(Y_SLOT["c"]))
        ml_shuf = place("ml_shuf", [P, 2, T], f32, slot(Y_SLOT["c"] + 1))
        ml_rot = place("ml_rot", [P, HEADS, T], f32, slot(Y_SLOT["d"]))
        cf_tmp = place("cf_tmp", [P, 2, T], f32, slot(CQN + 2))
        lat = place("lat", [P, 4, T], f32, slot(20))
        x_tok = place("x_tok", [P, TC, D], f32, slot(0))
        rows = place("rows", [P, DEPTH, 2, P], f32, slot(4))
        out_tok = place("out_tok", [P, TC, D], f32, slot(0))
        y = place("y", [P, KD, 2, T], f32, xn_at)
        ml_q = [xn[:, h, :, :] for h in range(HEADS)]
        ml_k = [xn[:, HEADS + h, :, :] for h in range(HEADS)]

        ps = ctx.enter_context(nc.psum_tensor("ps", [P, 8, T], f32))

        x_in = [sem(f"x_in{q}") for q in range(4)]
        rows_in = sem("rows_in")
        ident_set = sem("ident_set")
        rope_in = sem("rope_in")
        raw_in = [sem(f"raw_in{s}") for s in range(RAW)]
        hi_done = sem("hi_done")
        lo_done = sem("lo_done")
        down_part = sem("down_part")
        xt_done = sem("xt_done")
        vt_done = sem("vt_done")
        vec_all_set = sem("vec_all_set")
        vec_set = sem("vec_set")
        gain_set = sem("gain_set")
        x_done = sem("x_done")
        xh_done = sem("xh_done")
        xl_done = sem("xl_done")
        group_done = sem("group_done")
        evac = sem("evac")
        y_evac = sem("y_evac")
        v_step = sem("v_step")
        sq_done = sem("sq_done")
        add_done = sem("add_done")
        stat_done = sem("stat_done")
        var_done = sem("var_done")
        rstd_done = sem("rstd_done")
        spread_done = sem("spread_done")
        scale_done = sem("scale_done")
        mix_set = sem("mix_set")
        cf_tanh = sem("cf_tanh")
        cf_u_set = sem("cf_u_set")
        cf_prod = sem("cf_prod")
        cf_sum = sem("cf_sum")
        cf_conv = sem("cf_conv")
        mean_done = sem("mean_done")
        cf_cent = sem("cf_cent")
        cf_norm = sem("cf_norm")
        cf_affine = sem("cf_affine")
        cf_swish = sem("cf_swish")
        cf_val = sem("cf_val")
        sc_val = sem("sc_val")
        y_hi = sem("y_hi")
        y_ready = sem("y_ready")
        rot_done = sem("rot_done")
        rot_sin = sem("rot_sin")
        rot_hi = sem("rot_hi")
        qk_ready = sem("qk_ready")
        val_hi = sem("val_hi")
        lat_done = sem("lat_done")
        lat_norm = sem("lat_norm")
        lat_hi = sem("lat_hi")
        lat_ready = sem("lat_ready")
        kr_done = sem("kr_done")
        kr_hi = sem("kr_hi")
        kr_lo = sem("kr_lo")
        kr_spread = sem("kr_spread")
        kn_hi = sem("kn_hi")
        score_done = sem("score_done")
        masked = sem("masked")
        negmax_done = sem("negmax_done")
        exp_done = sem("exp_done")
        inv_done = sem("inv_done")
        prob_done = sem("prob_done")
        pt_done = sem("pt_done")
        pt_hi = sem("pt_hi")
        pt_ready = sem("pt_ready")
        pv_hi = sem("pv_hi")
        c_gate = sem("c_gate")
        tanh_done = sem("tanh_done")
        f_done = sem("f_done")
        f_hi = sem("f_hi")
        f_ready = sem("f_ready")
        ot_done = sem("ot_done")
        out_set = [sem("out_set_even"), sem("out_set_odd")]
        stored = sem("stored")

        def weight_source(u, l, i=0):
            if u < U_UKV:
                if u in (U_VAL, U_VAL + 1):
                    r0 = (u - U_VAL) * 4 * P
                    v = inp["w_in"][l, r0:r0 + 4 * P, MB0 + 2 * GW:MB0 + 3 * GW]
                    return v.rearrange("(k p) n -> p k n", p=P), 4, 2 * P
                n = P if u != U_KR else MLA_QK
                if W_IN_COLS[u] == 0:
                    l = (l + DEPTH) % DEPTH
                v = inp["w_in"][l, :, W_IN_COLS[u]:W_IN_COLS[u] + n]
                return v.rearrange("(k p) n -> p k n", p=P), KD, n
            if U_UQ <= u < U_OUT:
                c0 = (u - U_UQ) * 2 * MLA_QK
                v = inp["w_uq"][l, :, c0:c0 + 2 * MLA_QK]
                return v.rearrange("(k p) n -> p k n", p=P), 3, 2 * MLA_QK
            if u == U_UKV:
                return inp["w_ukv"][l, :, :].rearrange("(k p) n -> p k n", p=P), 1, 2 * GW
            if u < U_UP:
                m = u - U_OUT
                v = inp["w_out"][l, :, m * P:(m + 1) * P]
                return v.rearrange("(k p) n -> p k n", p=P), KD, P
            if u < U_DOWN:
                j = u - U_UP
                v = inp["w_ffn_up"][l, :, bass.ds((j % 2) * D_FF + (j // 2) * P + i * P, P)]
                return v.rearrange("(k p) n -> p k n", p=P), KD, P
            m, part = down_unit(u - U_DOWN)
            k0, nk = DOWN_PARTS[part]
            v = inp["w_ffn_down"][l, k0 * P:(k0 + nk) * P, bass.ds(m * P + i * P, P)]
            return v.rearrange("(k p) n -> p k n", p=P), nk, P

        def unit_elements(u):
            if u == U_KR:
                return KD * MLA_QK
            if U_UQ <= u < U_OUT:
                return 3 * 2 * MLA_QK
            return 2 * GW if u == U_UKV else KD * P

        def released(u):
            if u < U_UKV:
                return group_done, (u + 1 if u != U_VAL else u + 2), NG
            if u < U_OUT:
                return group_done, (G_MQ, G_MQ + 2, G_MQ + 4)[u - U_UKV], NG
            if u < U_UP:
                return group_done, G_OUT + u - U_OUT + 1, NG
            if u < U_DOWN:
                return group_done, G_UP + u - U_UP + 1, NG
            ends, count = down_count(u - U_DOWN)
            return (group_done, G_DOWN + count, NG) if ends else (down_part, count, 2 * KD)

        def weights(u):
            n = {True: 2 * P}.get(u in (U_VAL, U_VAL + 1), P)
            if u == U_KR:
                n = MLA_QK
            if U_UQ <= u < U_OUT:
                n = 2 * MLA_QK
            if u == U_UKV:
                n = 2 * GW
            nk = unit_elements(u) // n
            return wsp[:, u % SPLIT, :, 0:nk * n].rearrange("p s (k n) -> p s k n", n=n)

        def split_hi(act, u, l, i=0, per=0, first=False):
            n = unit_elements(u % NU)
            act.wait_ge(raw_in[u % RAW], l * (NU // RAW * 16) + i * (per // RAW * 16) + 16 * (u // RAW + 1))
            if not first and u >= SPLIT:
                s, count, step = released(u - SPLIT)
                act.wait_ge(s, l * step + i * (per if s is group_done else 2 * per // 3) + count)
            act.activation(wsp[:, u % SPLIT, 0, 0:n], raw[:, u % RAW, 0:n], ACT.Copy).then_inc(hi_done, 1)

        def split_lo(dve, u, l, i=0, per=0):
            n = unit_elements(u % NU)
            dve.wait_ge(hi_done, l * NU + i * per + u + 1)
            dve.tensor_tensor(wsp[:, u % SPLIT, 1, 0:n], raw[:, u % RAW, 0:n], fp(wsp[:, u % SPLIT, 0, 0:n]),
                              ALU.subtract).then_inc(lo_done, 1)

        def col(name, c=0):
            a = VC[name] + c
            return vec[:, a:a + 1]

        block = ctx.enter_context(nc.Block())

        @block.sync
        def _(sp):
            def load(u, l, i=0, per=0, wait=True):
                if wait:
                    sp.wait_ge(lo_done, l * NU + i * per + u - 1)
                src, nk, n = weight_source(u % NU, l if u < NU else (l + 1) % DEPTH, i)
                dst = raw[:, u % RAW, 0:nk * n].rearrange("p (k n) -> p k n", n=n)
                sp.dma_start(dst, src).then_inc(raw_in[u % RAW], 16)

            x_v = inp["x"][0, :, :].rearrange("(c p) f -> p c f", p=P)
            for q in range(4):
                f = slice(q * D // 4, (q + 1) * D // 4)
                sp.dma_start(x_tok[:, :, f], x_v[:, :, f]).then_inc(x_in[q], 16)
                if q < RAW:
                    load(q, 0, wait=False)
            load(2, 0)
            with sp.Fori(0, DEPTH) as l:
                for u in range(LEAD, U_UP):
                    load(u, l)
                with sp.Fori(0, NF // 2) as i:
                    for j in range(4):
                        u = U_UP + j
                        sp_u = l * NU + i * 4 + u - 1
                        src, nk, n = weight_source(u, l, i * 2)
                        dst = raw[:, u % RAW, 0:nk * n].rearrange("p (k n) -> p k n", n=n)
                        sp.wait_ge(raw_in[u % RAW], 16)
                        sp.wait_ge(lo_done, sp_u)
                        sp.dma_start(dst, src).then_inc(raw_in[u % RAW], 16)
                with sp.Fori(0, 2) as i:
                    for j in range(12):
                        u = U_DOWN + j
                        sp_u = l * NU + i * 12 + u - 1
                        src, nk, n = weight_source(u, l, i * 4)
                        dst = raw[:, u % RAW, 0:nk * n].rearrange("p (k n) -> p k n", n=n)
                        sp.wait_ge(raw_in[u % RAW], 16)
                        sp.wait_ge(lo_done, sp_u)
                        sp.dma_start(dst, src).then_inc(raw_in[u % RAW], 16)
                for u in range(NU, NU + LEAD):
                    load(u, l)
            out_v = out[0, :, :].rearrange("(c p) f -> p c f", p=P)
            for k in range(KD):
                sp.wait_ge(out_set[k % 2], k // 2 + 1)
                sp.dma_start(out_v[:, :, k * P:(k + 1) * P], out_tok[:, :, k * P:(k + 1) * P]).then_inc(stored, 16)
            sp.wait_ge(rope_in, 16 * (2 * DEPTH + 1))
            sp.wait_ge(stored, 16 * KD)

        @block.tensor
        def _(pe):
            def product(dst, a, b, start, stop):
                pe.matmul(dst, a[0], b[0], start=start, stop=False, skip_group_check=True)
                pe.matmul(dst, a[0], b[1], start=False, stop=False, skip_group_check=True)
                return pe.matmul(dst, a[1], b[0], start=False, stop=stop, skip_group_check=True)

            def weights_ready(u, l, i=0, per=0):
                pe.wait_ge(lo_done, l * NU + i * per + u + 1)

            def dense(g, u, bank, rhs, l, m=P, c0=0, between=None):
                w = weights(u)
                nk = len(rhs)
                for k in range(nk):
                    last = product(ps[0:m, bank, :], (w[:, 0, k, c0:c0 + m], w[:, 1, k, c0:c0 + m]), rhs[k],
                                   k == 0, k == nk - 1)
                    if between and k == nk // 2:
                        between()
                last.then_inc(group_done, 1)

            def pair(tile, rows_=slice(0, P)):
                return tile[rows_, 0, :], tile[rows_, 1, :]

            x_pairs = [(xn[:, k, 0, :], xn[:, k, 1, :]) for k in range(KD)]

            def bank_free(l, count):
                pe.wait_ge(evac, l * N_EVAC + count)

            def stat(ev, l):
                n = SQUARES[ev]
                if n > 1:
                    pe.wait_ge(add_done, l * NADD + adds_before(ev) + ADDS[ev])
                else:
                    pe.wait_ge(sq_done, l * NSQ + squares_before(ev) + n)
                if ev == "ckv":
                    pe.wait_ge(scale_done, l * 2 + 1)
                elif ev == "cq":
                    pe.wait_ge(lat_norm, l * 4 + 1)
                elif ev == "ln":
                    pe.wait_ge(cf_cent, l * 2 + 2)
                elif ev == "post_mix":
                    pe.wait_ge(cf_norm, l * 2 + 2)
                elif ev == "pre_ffn":
                    pe.wait_ge(x_done, KD + l * 2 * KD + KD)
                elif ev == "post_ffn":
                    pe.wait_ge(scale_done, l * 2 + 2)
                for part in range(1 + (ev in POST)):
                    if part:
                        pe.wait_ge(sq_done, l * NSQ + squares_before(ev) + n)
                    for c in range(TC):
                        a = part * TC + c
                        last = pe.matmul(ps[:, STAT, a:a + 1], sq[:, part, c * P:(c + 1) * P], ones[:, 0:1],
                                         start=True, stop=True)
                last.then_inc(stat_done, 1)

            def spread(ev, l):
                pe.wait_ge(rstd_done, l * NEV + EVENTS.index(ev) + 1)
                for c in range(TC):
                    last = pe.matmul(ps[:, STAT, c * P:(c + 1) * P], rstd[:, c:c + 1].to_broadcast([P, P]),
                                     ident[:, :], start=True, stop=True)
                last.then_inc(spread_done, 1)

            def together(units, groups, l, n0):
                for u in units:
                    weights_ready(u, l)
                banks = [bank_of(g) if g < G_UP else bank_up(g - G_UP, True) for g in groups]
                for k in range(KD):
                    pe.wait_ge(xh_done, l * N_XH + n0 + k + 1)
                    for u, bank in zip(units, banks):
                        for s in range(2):
                            pe.matmul(ps[:, bank, :], weights(u)[:, s, k, :], x_pairs[k][0],
                                      start=k == 0 and s == 0, stop=False, skip_group_check=True)
                    pe.wait_ge(xl_done, l * N_XH + n0 + k + 1)
                    for u, bank in zip(units, banks):
                        last = pe.matmul(ps[:, bank, :], weights(u)[:, 0, k, :], x_pairs[k][1],
                                         start=False, stop=k == KD - 1, skip_group_check=True)
                        if k == KD - 1:
                            last.then_inc(group_done, 1)

            pe.wait_ge(ident_set, 6)
            pe.wait_ge(rows_in, 16)
            for l0 in range(DEPTH):
                for t in range(2):
                    last = pe.transpose(ps[:, 5 + l0, t * HALFROWS:(t + 1) * HALFROWS], rows[0:HALFROWS, l0, t, :],
                                        ident[0:HALFROWS, 0:HALFROWS])
                last.then_inc(vt_done, 1)
            for k in range(KD):
                if k >= 4:
                    pe.wait_ge(x_done, k - 3)
                if k % 2 == 0:
                    pe.wait_ge(x_in[k // 2], 16)
                for c in range(TC):
                    last = pe.transpose(ps[:, k % 4, c * P:(c + 1) * P], x_tok[:, c, k * P:(k + 1) * P], ident[:, :])
                last.then_inc(xt_done, 1)
            pe.wait_ge(x_done, KD)

            with pe.Fori(0, DEPTH) as l:
                together([0, 1, 2], [0, 1, 2], l, 0)
                weights_ready(3, l)
                dense(3, 3, bank_of(3), x_pairs, l, between=lambda: stat("pre_mix", l))
                spread("pre_mix", l)
                for g in range(4, G_MK):
                    if g in (G_V, G_V + 1):
                        weights_ready(U_VAL + 1, l)
                        bank_free(l, bank_before(g))
                        for h in range(2):
                            c = 2 * (g - G_V) + h
                            for k in range(KD):
                                w = weights(U_VAL + k // 4)
                                xk = [xn[:, k, s, c * P:(c + 1) * P] for s in range(2)]
                                last = product(ps[:, bank_of(g), h * GW:(h + 1) * GW], xk,
                                               (w[:, 0, k % 4, :], w[:, 1, k % 4, :]), k == 0, k == KD - 1)
                        last.then_inc(group_done, 1)
                    else:
                        weights_ready(g, l)
                        if bank_before(g):
                            bank_free(l, bank_before(g))
                        dense(g, g, bank_of(g), x_pairs, l, m=MLA_QK if g == G_KR else P,
                              between=(lambda: stat("cq", l)) if g == 17 else None)
                    if g == 13:
                        stat("ckv", l)
                    if g == 15:
                        spread("ckv", l)
                    if g == 18:
                        spread("cq", l)
                    if g == 19:
                        pe.wait_ge(cf_conv, l + 1)
                        pe.wait_ge(cf_sum, (l + 1) * (CF_TAPS - 1))
                        pe.wait_ge(lat_norm, l * 4 + 4)
                        for c in range(2):
                            last = pe.matmul(ps[:, STAT, :], ones[:, :], cf_out[:, c, :], start=c == 0, stop=c == 1)
                        last.then_inc(mean_done, 1)
                def projection_bank(g):
                    bank_free(l, bank_before(g))

                pe.wait_ge(lat_ready, l * 4 + 1)
                weights_ready(U_UKV, l)
                for h in range(HEADS):
                    g = G_MK + h
                    projection_bank(g)
                    dense(g, U_UKV, bank_of(g), [pair(hid[:, CKVN])], l, m=P, c0=h * P)
                wkv = weights(U_UKV)[:, :, 0, :].rearrange("p s (h n) -> p s h n", h=HEADS)
                for half in range(2):
                    g = G_MV + half
                    projection_bank(g)
                    for j in range(2):
                        c = 2 * half + j
                        last = product(ps[:, bank_of(g), j * GW:(j + 1) * GW],
                                       [hid[:, CKVN, s, c * P:(c + 1) * P] for s in range(2)],
                                       [wkv[:, s, :, DH:2 * DH] for s in range(2)], True, True)
                    last.then_inc(group_done, 1)
                pe.wait_ge(lat_ready, l * 4 + 4)
                for h in range(HEADS):
                    g = G_MQ + h
                    weights_ready(U_UQ + h // 2, l)
                    projection_bank(g)
                    dense(g, U_UQ + h // 2, bank_of(g), [pair(hid[:, CQN + j]) for j in range(3)], l,
                          m=MLA_QK, c0=(h % 2) * MLA_QK)
                    if h == 1:
                        stat("ln", l)

                def scores(t):
                    h, c = divmod(t, TC)
                    if t == 0:
                        bank_free(l, G_MQ + 1)
                    if t >= 2:
                        pe.wait_ge(masked, l * N_ATT + t - 1)
                    if h < HEADS:
                        r0 = DH * (h % 2)
                        q, k = hid[:, QM + h // 2], hid[:, KM + h // 2]
                        r = slice(r0, r0 + DH)
                    else:
                        if c == 0:
                            pe.wait_ge(qk_ready, l * 8 + 8)
                            bank_free(l, G_PV)
                            pe.wait_ge(kr_spread, l * 2 + 2)
                        q, k = ml_q[h - HEADS], ml_k[h - HEADS]
                        r = slice(0, MLA_QK)
                    n = (c + 1) * P
                    product(ps[:, SCORE0 + t % 2, 0:n], (q[r, 0, c * P:n], q[r, 1, c * P:n]),
                            (k[r, 0, 0:n], k[r, 1, 0:n]), True, True).then_inc(score_done, 1)

                def transposes(t):
                    c = t % TC
                    pe.wait_ge(prob_done, l * N_ATT + t + 1)
                    if t >= 2:
                        pe.wait_ge(pt_ready, l * N_ATT + t - 1)
                    for kc in range(c + 1):
                        last = pe.transpose(ps[:, PT_BANKS[t % 2], kc * P:(kc + 1) * P],
                                            prob[:, t % NPROB, kc * P:(kc + 1) * P], ident[:, :])
                    last.then_inc(pt_done, 1)

                def values(h, part):
                    g = G_PV + h
                    late = part > 0
                    if part < 2:
                        pe.wait_ge(pt_ready, l * N_ATT + TC * h + (TC if late else 2))
                    if part == 0:
                        bank_free(l, bank_before(g) if h >= 3 else G_PV)
                    v = vm if h < HEADS else vl
                    c0 = (h % HEADS) // 2 * P
                    tile, q0, kcs = (pt_late, 2, (0, 1) if part == 1 else (2, 3)) if late else (pt_early, 0, (0, 1))
                    for kc in kcs:
                        skip = max(kc - q0, 0) * P
                        last = product(ps[:, bank_of(g), q0 * P + skip:(q0 + 2) * P],
                                       [v[:, s, kc, c0:c0 + P] for s in range(2)],
                                       [tile[:, h % 2, s, kc, skip:2 * P] for s in range(2)],
                                       kc == 0, kc == q0 + 1)
                    if part == 2:
                        last.then_inc(group_done, 1)

                pe.wait_ge(qk_ready, l * 8 + 4)
                for t in range(N_ATT + ATT_TAIL):
                    if t < N_ATT:
                        scores(t)
                    if t == 2:
                        spread("ln", l)
                    if TRAIL <= t < N_ATT + TRAIL:
                        transposes(t - TRAIL)
                    for part, after in enumerate(VALUES_AFTER):
                        h, r = divmod(t - TRAIL - after, TC)
                        if r == 0 and 0 <= h < 2 * HEADS:
                            values(h, part)

                pe.wait_ge(y_ready, l * 4 + 4)
                bank_free(l, G_PV + 6)
                pe.wait_ge(masked, l * N_ATT + N_ATT)
                y_pairs = [pair(hid[:, k]) for k in range(KD)]
                for m in range(KD):
                    weights_ready(U_OUT + m, l)
                    if m >= 4:
                        pe.wait_ge(y_evac, l * N_YEVAC + m - 3)
                    w = weights(U_OUT + m)
                    for k in range(KD):
                        if m == 0 and k == KD - 1:
                            bank_free(l, G_OUT)
                        last = product(ps[:, bank_of(G_OUT + m), :], (w[:, 0, k, :], w[:, 1, k, :]), y_pairs[k],
                                       k == 0, k == KD - 1)
                    last.then_inc(group_done, 1)
                stat("post_mix", l)
                spread("post_mix", l)

                pe.wait_ge(y_evac, l * N_YEVAC + KD)
                together([U_UP, U_UP + 1, U_UP + 2], [G_UP, G_UP + 1, G_UP + 2], l, KD)
                weights_ready(U_UP + 3, l)
                dense(G_UP + 3, U_UP + 3, 3, x_pairs, l, between=lambda: stat("pre_ffn", l))
                spread("pre_ffn", l)
                for j in range(4):
                    weights_ready(U_UP + 4 + j, l)
                    if j == 3:
                        bank_free(l, G_OUT + 4)
                    dense(G_UP + 4 + j, U_UP + 4 + j, j, x_pairs, l)
                with pe.Fori(2, NF // 2) as i:
                    for j in range(4):
                        pe.wait_ge(lo_done, l * NU + i * 4 + U_UP + j + 1)
                        pe.wait_ge(evac, l * N_EVAC + i * 4 + G_OUT + j - 3)
                        dense(G_UP + j, U_UP + j, j, x_pairs, l)

                with pe.Fori(0, 2) as i:
                    for j in range(12):
                        m, part = down_unit(j)
                        k0, nk = DOWN_PARTS[part]
                        pe.wait_ge(lo_done, l * NU + i * 12 + U_DOWN + j + 1)
                        if part == 0:
                            pe.wait_ge(y_evac, l * N_YEVAC + i * 4 + KD + m - 3)
                            bank_free(l, N_EVAC - 3 + m)
                        pe.wait_ge(f_ready, l * NF + k0 + nk)
                        w = weights(U_DOWN + j)
                        for k in range(nk):
                            last = product(ps[:, m, :], (w[:, 0, k, :], w[:, 1, k, :]), pair(hid[:, k0 + k]),
                                           k0 + k == 0, k0 + k == NF - 1)
                        last.then_inc(group_done if part == 2 else down_part, 1)
                stat("post_ffn", l)
                spread("post_ffn", l)

            pe.wait_ge(y_evac, DEPTH * N_YEVAC)
            for k in range(KD):
                pe.wait_ge(x_done, KD + (DEPTH * 2 - 1) * KD + k + 1)
                if k >= len(RING):
                    pe.wait_ge(out_set[(k - len(RING)) % 2], (k - len(RING)) // 2 + 1)
                for c in range(TC):
                    last = pe.transpose(ps[:, RING[k % len(RING)], c * P:(c + 1) * P], x[:, k, c * P:(c + 1) * P], ident[:, :])
                last.then_inc(ot_done, 1)

        @block.gpsimd
        def _(pool):
            pool.memset(ident[:, :], 0.0).then_inc(ident_set, 1)
            pool.memset(causal[:, :], 0.0).then_inc(ident_set, 1)
            pool.memset(ones[:, :], 1.0).then_inc(ident_set, 1)
            pool.wait_ge(ident_set, 3)
            pool.affine_select(out=ident[:, :], in_=ident[:, :], compare_op=ALU.not_equal, fill=1.0, base=0,
                               pattern=[[-1, P]], channel_multiplier=1).then_inc(ident_set, 1)
            pool.affine_select(out=causal[:, T - P:T], in_=causal[:, T - P:T], compare_op=ALU.is_ge, fill=MASKED,
                               base=0, pattern=[[-1, P]], channel_multiplier=1).then_inc(ident_set, 1)
            pool.memset(power[:, :], -0.5).then_inc(ident_set, 1)

            def sums(ev, l):
                for k in range(1, ADDS[ev] + 1):
                    pool.wait_ge(sq_done, l * NSQ + squares_before(ev) + k + 1)
                    if k > 1:
                        pool.wait_ge(add_done, l * NADD + adds_before(ev) + k - 1)
                    pool.tensor_tensor(sq[:, 0, :], sq[:, 0, :], sq[:, 1, :], ALU.add).then_inc(add_done, 1)

            def rsqrt(ev, l):
                pool.wait_ge(var_done, l * NEV + EVENTS.index(ev) + 1)
                pool.tensor_tensor(rstd[:, :], var[:, :], power[:, :], ALU.pow).then_inc(rstd_done, 1)

            pool.wait_ge(ident_set, 6)
            sums("pre_mix", 0)
            with pool.Fori(0, DEPTH) as l:
                rsqrt("pre_mix", l)
                for j in range(1, CF_TAPS):
                    pool.wait_ge(cf_prod, l * CF_TAPS + j + 1)
                    if j > 1:
                        pool.wait_ge(cf_sum, l * (CF_TAPS - 1) + j - 1)
                    pool.tensor_tensor(cf_out[:, 1, :], cf_out[:, 1, :], cf_tmp[:, j % 2, :], ALU.add)\
                        .then_inc(cf_sum, 1)
                for ev in ("ckv", "cq"):
                    sums(ev, l)
                    rsqrt(ev, l)
                sums("ln", l)
                r = slice(0, MLA_QK)
                pool.wait_ge(rope_in, l * 32 + 32)

                def rotated_lo(h):
                    pool.wait_ge(rot_hi, l * 8 + 5 + h)
                    pool.tensor_tensor(ml_q[h][r, 1, :], ml_rot[r, h, :], fp(ml_q[h][r, 0, :]),
                                       ALU.subtract).then_inc(qk_ready, 1)

                def query_sin(h):
                    pool.wait_ge(evac, l * N_EVAC + G_MQ + h + 1)
                    pool.tensor_tensor(ml_shuf[r, h % 2, :], ml_shuf[r, h % 2, :], rope[r, 1, :], ALU.mult)\
                        .then_inc(rot_sin, 1)

                def query_sum(h):
                    pool.wait_ge(rot_sin, l * HEADS + h + 1)
                    pool.tensor_tensor(ml_rot[r, h, :], ml_rot[r, h, :], ml_shuf[r, h % 2, :], ALU.add)\
                        .then_inc(rot_done, 1)

                for h in range(2):
                    query_sin(h)
                    query_sum(h)
                rsqrt("ln", l)
                for t in range(N_ATT):
                    n = (t % TC + 1) * P
                    pool.wait_ge(inv_done, l * N_ATT + t + 1)
                    pool.tensor_tensor(prob[:, t % NPROB, 0:n], prob[:, t % NPROB, 0:n],
                                       rowinv[:, t:t + 1].to_broadcast([P, n]), ALU.mult).then_inc(prob_done, 1)
                    if t in (0, 3):
                        query_sin({0: 2, 3: 3}[t])
                    if t in (1, 4):
                        query_sum({1: 2, 4: 3}[t])
                    if t in (2, 6, 9, 12):
                        rotated_lo((2, 6, 9, 12).index(t))
                    if t in (15, 19, 23):
                        u = U_OUT + (t - 15) // 4
                        pool.wait_ge(lo_done, l * NU + u)
                        split_lo(pool, u, l)
                for ev in EVENTS[4:]:
                    sums(ev, l)
                    rsqrt(ev, l)
                sums("pre_mix", l + 1)

        @block.vector
        def _(dve):
            class Steps:
                n, base = 0, 0

                def mark(self, ins):
                    ins.then_inc(v_step, 1)
                    self.n += 1

                def wait(self):
                    dve.wait_ge(v_step, self.base + self.n)

            st = Steps()

            def own(s, count):
                dve.wait_ge(s, count)

            def normed_lo(gain, k, n, l):
                dve.wait_ge(xh_done, l * N_XH + n + 1)
                dve.scalar_tensor_tensor(xn[:, k, 1, :], x[:, k, :], gain, fp(xn[:, k, 0, :]),
                                         ALU.mult, ALU.subtract).then_inc(xl_done, 1)

            for l0 in range(DEPTH):
                dve.wait_ge(vt_done, l0 + 1)
                dve.tensor_copy(vec_all[:, l0, :], ps[:, 5 + l0, 0:NVEC]).then_inc(vec_all_set, 1)
            own(vec_all_set, DEPTH)
            dve.tensor_copy(gain_next[:, :], vec_all[:, 0, VC["norm_mix_pre"]:VC["norm_mix_pre"] + KD])\
               .then_inc(gain_set, 1)
            for k in range(KD + 1):
                if k < KD:
                    dve.wait_ge(xt_done, k + 1)
                    dve.tensor_copy(x[:, k, :], ps[:, k % 4, :]).then_inc(x_done, 1)
                if k:
                    own(x_done, k)
                    normed_lo(gain_next[:, k - 1:k], k - 1, k - 1, 0)
                if k in SPLIT_AFTER:
                    split_lo(dve, SPLIT_AFTER.index(k), 0)

            def event_var(ev, l):
                dve.wait_ge(stat_done, l * NEV + EVENTS.index(ev) + 1)
                ins = dve.tensor_scalar(var[:, :], ps[:, STAT, 0:TC], 1.0 / WIDTH[ev], EPS, ALU.mult, ALU.add)
                if ev in POST:
                    st.mark(ins)
                    st.wait()
                    ins = dve.scalar_tensor_tensor(var[:, :], ps[:, STAT, TC:2 * TC], 1.0 / WIDTH[ev], var[:, :],
                                                   ALU.mult, ALU.add)
                ins.then_inc(var_done, 1)

            def scale_ready(ev, l):
                if ev == "pre_mix":
                    dve.wait_ge(scale_done, l * 2 + 1)
                elif ev == "pre_ffn":
                    dve.wait_ge(scale_done, l * 2 + 2)
                else:
                    dve.wait_ge(spread_done, l * NEV + EVENTS.index(ev) + 1)

            def group_ready(g, l):
                dve.wait_ge(group_done, l * NG + g + 1)

            with dve.Fori(0, DEPTH) as l:
                st.base, st.n = l * V_STEPS, 0
                dve.wait_ge(vec_all_set, 2)
                dve.tensor_copy(vec[:, :], vec_all[:, l, :]).then_inc(vec_set, 1)
                dve.memset(cf_u[:, :, 0:CF_TAPS - 1], 0.0)
                st.mark(dve.memset(sc_u[:, 0:SC_TAPS - 1], 0.0))
                own(vec_set, l + 1)
                split_lo(dve, 3, l)
                split_lo(dve, 4, l)
                event_var("pre_mix", l)
                dve.wait_ge(rstd_done, l * NEV + 1)
                dve.tensor_copy(rstd_mix[:, :], rstd[:, :]).then_inc(mix_set, 1)
                own(mix_set, l + 1)
                split_lo(dve, 5, l)
                scale_ready("pre_mix", l)

                def ev_count(g):
                    return l * N_EVAC + g + 1

                def scaled(dst, g, rows_=slice(0, P)):
                    dve.tensor_tensor(dst, ps[rows_, bank_of(g), :], scale_main[rows_, :], ALU.mult)\
                       .then_inc(evac, 1)
                    own(evac, ev_count(g))

                def rotate(e, shuf, half, rows_, g):
                    mask = [(j + half) % (2 * half) if j < 2 * half else j for j in range(32)]
                    src = ps[rows_, bank_of(g), :]
                    dve.tensor_tensor(e, src, rope[rows_, 0, :], ALU.mult)
                    dve.stream_shuffle(shuf, src, mask).then_inc(evac, 1)
                    own(evac, ev_count(g))
                    st.mark(dve.tensor_tensor(shuf, shuf, rope[rows_, 1, :], ALU.mult))
                    st.wait()
                    return dve.tensor_tensor(e, e, shuf, ALU.add)

                def rot_lo(n):
                    dve.wait_ge(rot_hi, l * 8 + n + 1)
                    dst, e = hid[:, (QM, KM, QM + 1, KM + 1)[n]], rot[:, n % 2, :]
                    dve.tensor_tensor(dst[:, 1, :], e, fp(dst[:, 0, :]), ALU.subtract).then_inc(qk_ready, 1)

                def group_a_lo(c):
                    dve.wait_ge(y_hi, l * 4 + c + 1)
                    dst = hid[:, Y_SLOT["a"] + c]
                    dve.tensor_tensor(dst[:, 1, :], sc_w[:, :], fp(dst[:, 0, :]), ALU.subtract).then_inc(y_ready, 1)

                cf_j = 0
                for g in range(G_MK):
                    if g >= 3:
                        split_lo(dve, g + LEAD, l)
                    if g == G_V + 1:
                        rot_lo(3)
                    if G_V < g <= G_V + 2:
                        for j in range(2):
                            c = 2 * (g - 1 - G_V) + j
                            dve.wait_ge(val_hi, l * 6 + 2 * (g - 1 - G_V) + 2)
                            ins = dve.scalar_tensor_tensor(vm[:, 1, c, :],
                                                           ps[:, bank_of(g - 1), j * GW:(j + 1) * GW],
                                                           rstd_mix[:, c:c + 1], fp(vm[:, 0, c, :]),
                                                           ALU.mult, ALU.subtract)
                            if j:
                                ins.then_inc(evac, 1)
                    if g == G_KR + 2:
                        dve.wait_ge(kr_hi, l + 1)
                        dve.tensor_tensor(kr[DH:MLA_QK, 1, :], rot[DH:MLA_QK, 0, :], fp(kr[DH:MLA_QK, 0, :]),
                                          ALU.subtract).then_inc(kr_lo, 1)
                    if g in (14, 18):
                        event_var("ckv" if g == 14 else "cq", l)
                    if g == 16:
                        scale_ready("ckv", l)
                        dve.tensor_tensor(lat[:, 3, :], lat[:, 3, :], ps[:, STAT, :], ALU.mult).then_inc(lat_norm, 1)
                    if g == 18:
                        dve.wait_ge(lat_hi, l * 4 + 1)
                        dst = hid[:, CKVN]
                        dve.scalar_tensor_tensor(dst[:, 1, :], lat[:, 3, :], col("mla_kv_norm"), fp(dst[:, 0, :]),
                                                 ALU.mult, ALU.subtract).then_inc(lat_ready, 1)
                    if g == 18:
                        group_a_lo(0)
                    if g == 19:
                        scale_ready("cq", l)
                        for j in range(3):
                            dve.tensor_tensor(lat[:, j, :], lat[:, j, :], ps[:, STAT, :], ALU.mult)\
                               .then_inc(lat_norm, 1)
                    if g == 20:
                        dve.wait_ge(mean_done, l + 1)
                        for c in range(2):
                            dve.scalar_tensor_tensor(cf_out[:, c, :], ps[:, STAT, :], -1.0 / GW, cf_out[:, c, :],
                                                     ALU.mult, ALU.add).then_inc(cf_cent, 1)
                    if g not in (G_V, G_V + 1):
                        group_ready(g, l)
                    if g in (0, 2):
                        scaled(rot[:, g // 2, :], g)
                    elif g in (1, 3):
                        c = g // 2
                        u = cf_u[:, c, CF_TAPS - 1:]
                        dve.scalar_tensor_tensor(u, ps[:, bank_of(g), :], 0.5, scale_main[:, :], ALU.mult,
                                                 ALU.mult).then_inc(evac, 1)
                        dve.wait_ge(cf_tanh, l * 2 + c + 1)
                        own(evac, ev_count(g))
                        ins = dve.scalar_tensor_tensor(u, rot[:, c, :], 1.0, u, ALU.add, ALU.mult)
                        if c:
                            ins.then_inc(cf_u_set, 1)
                        else:
                            st.mark(ins)
                    elif G_QK <= g < G_V:
                        n = g - G_QK
                        if n == 0:
                            dve.wait_ge(rope_in, l * 32 + 16)
                            st.mark(dve.tensor_tensor(rope[:, :, :], rope[:, :, :],
                                                      scale_main[:, :].unsqueeze(1).to_broadcast([P, 2, T]),
                                                      ALU.mult))
                            st.wait()
                        if n == 1:
                            own(rot_done, l * 8 + 1)
                        if n >= 2:
                            own(qk_ready, l * 8 + n - 1)
                        rotate(rot[:, n % 2, :], shuf[:, :], 8, slice(0, P), g).then_inc(rot_done, 1)
                        if n:
                            rot_lo(n - 1)
                    elif g in (G_V, G_V + 1):
                        pass
                    elif g == G_CKV:
                        scaled(lat[:, 3, :], g)
                    elif g == G_KR:
                        r = slice(DH, MLA_QK)
                        dve.wait_ge(rope_in, l * 32 + 32)
                        own(qk_ready, l * 8 + 4)
                        st.mark(rotate(rot[r, 0, :], shuf[r, :], 16, r, g))
                        st.wait()
                        dve.tensor_tensor(rot[r, 0, :], rot[r, 0, :], scale_main[r, :], ALU.mult)\
                           .then_inc(kr_done, 1)
                    elif g < G_SC:
                        scaled(lat[:, g - G_CQ, :], g)
                    else:
                        c, kind = divmod(g - G_SC, 3)
                        if kind == 0:
                            if c:
                                own(y_ready, l * 4 + 1)
                            scaled(sc_w[:, :], g)
                        elif kind == 1:
                            scaled(sc_u[:, SC_TAPS - 1:], g)
                            st.mark(dve.tensor_tensor(sc_u[:, SC_TAPS - 1:], sc_u[:, SC_TAPS - 1:], sc_w[:, :],
                                                      ALU.mult))
                            st.wait()
                            st.mark(dve.tensor_scalar(sc_w[:, :], sc_u[:, 0:T], col("conv_a", c), None, ALU.mult))
                            for j in range(1, SC_TAPS):
                                st.wait()
                                st.mark(dve.scalar_tensor_tensor(sc_w[:, :], sc_u[:, j:j + T],
                                                                 col("conv_a", 2 * j + c), sc_w[:, :],
                                                                 ALU.mult, ALU.add))
                        else:
                            st.wait()
                            scaled(sc_u[:, SC_TAPS - 1:], g)
                            dve.tensor_tensor(sc_w[:, :], sc_w[:, :], sc_u[:, SC_TAPS - 1:], ALU.mult)\
                               .then_inc(sc_val, 1)
                    for _ in range(CF_VECTOR.get(g, 0)):
                        st.wait()
                        j, cf_j = cf_j, cf_j + 1
                        if j == 0:
                            ins = dve.tensor_scalar(cf_out[:, 0, :], cf_u[:, 0, 0:T], col("conv_b", 0),
                                                    col("conv_b_bias", 0), ALU.mult, ALU.add)
                        else:
                            ins = dve.scalar_tensor_tensor(cf_out[:, 0, :], cf_u[:, 0, j:j + T],
                                                           col("conv_b", 2 * j), cf_out[:, 0, :],
                                                           ALU.mult, ALU.add)
                        if j == CF_TAPS - 1:
                            ins.then_inc(cf_conv, 1)
                        else:
                            st.mark(ins)
                own(sc_val, l * 2 + 2)
                for j in range(3):
                    dve.wait_ge(lat_hi, l * 4 + j + 2)
                    dst = hid[:, CQN + j]
                    dve.scalar_tensor_tensor(dst[:, 1, :], lat[:, j, :], col("mla_q_norm", j),
                                             fp(dst[:, 0, :]), ALU.mult, ALU.subtract).then_inc(lat_ready, 1)

                group_a_lo(1)

                for h in range(HEADS):
                    g = G_MK + h
                    dve.wait_ge(kn_hi, l * 4 + h + 1)
                    dve.tensor_tensor(ml_k[h][0:DH, 1, :], ps[0:DH, bank_of(g), :], fp(ml_k[h][0:DH, 0, :]),
                                      ALU.subtract).then_inc(evac, 1)
                own(y_ready, l * 4 + 2)
                for half in range(2):
                    g = G_MV + half
                    dve.wait_ge(val_hi, l * 6 + 5 + half)
                    dve.tensor_tensor(vl[:, 1, 2 * half:2 * half + 2, :],
                                      ps[:, bank_of(g), :].rearrange("p (c d) -> p c d", c=2),
                                      fp(vl[:, 0, 2 * half:2 * half + 2, :]), ALU.subtract).then_inc(evac, 1)

                def query_parts(h):
                    g = G_MQ + h
                    r = slice(0, MLA_QK)
                    if h >= 2:
                        dve.wait_ge(rot_done, l * 8 + 3 + h)
                    group_ready(g, l)
                    dve.tensor_tensor(ml_rot[r, h, :], ps[r, bank_of(g), :], rope[r, 0, :], ALU.mult)
                    dve.stream_shuffle(ml_shuf[r, h % 2, :], ps[r, bank_of(g), :],
                                       [(j + 16) % 32 for j in range(32)]).then_inc(evac, 1)

                for h in range(HEADS - 1):
                    query_parts(h)
                    if h == 1:
                        event_var("ln", l)

                def head_rows(h):
                    return slice(DH * (h % 2), DH * (h % 2) + DH)

                for t in range(N_ATT + ATT_TAIL):
                    if t < N_ATT:
                        c = t % TC
                        n = (c + 1) * P
                        dve.wait_ge(ident_set, 6)
                        dve.wait_ge(score_done, l * N_ATT + t + 1)
                        if t >= 2:
                            dve.wait_ge(exp_done, l * N_ATT + t - 1)
                        if t == 0:
                            own(evac, l * N_EVAC + G_PV - 1)
                        dve.memset(negmax[:, t:t + 1], 0.0)
                        dve.tensor_tensor_reduce(out=sm[:, t % 2, 0:n], in0=ps[:, SCORE0 + t % 2, 0:n],
                                                 in1=causal[:, T - n:T], scale=1.0, scalar=-3e38,
                                                 op0=ALU.add, op1=ALU.max, accum_out=rowmax[:, t:t + 1])\
                           .then_inc(masked, 1)
                        own(masked, l * N_ATT + t + 1)
                        dve.tensor_scalar(negmax[:, t:t + 1], rowmax[:, t:t + 1],
                                          -(MOBA_SCALE if t < N_ATT // 2 else MLA_SCALE), None, ALU.mult)\
                           .then_inc(negmax_done, 1)
                    if 1 <= t <= N_ATT:
                        s = t - 1
                        dve.wait_ge(exp_done, l * N_ATT + s + 1)
                        dve.reciprocal(rowinv[:, s:s + 1], rowsum[:, s:s + 1]).then_inc(inv_done, 1)
                    if TRAIL <= t < N_ATT + TRAIL:
                        s = t - TRAIL
                        c = s % TC
                        dve.wait_ge(pt_hi, l * N_ATT + s + 1)
                        src = ps[:, PT_BANKS[s % 2], 0:(c + 1) * P].rearrange("p (k t) -> p k t", t=P)
                        dve.tensor_tensor(pt_of(s // TC, c, 1), src, fp(pt_of(s // TC, c, 0)), ALU.subtract)\
                           .then_inc(pt_ready, 1)
                    if t == 1:
                        query_parts(HEADS - 1)
                    if t == 2:
                        scale_ready("ln", l)
                        for c in range(2):
                            dve.tensor_tensor(cf_out[:, c, :], cf_out[:, c, :], ps[:, STAT, :], ALU.mult)\
                               .then_inc(cf_norm, 1)
                    if t in (5, 6):
                        c = t - 5
                        dve.wait_ge(cf_swish, l * 2 + c + 1)
                        dve.scalar_tensor_tensor(cf_out[:, c, :], cf_th[:, c, :], 1.0, cf_out[:, c, :],
                                                 ALU.add, ALU.mult).then_inc(cf_val, 1)
                    if t in (9, 10):
                        c = t - 9
                        dve.wait_ge(y_hi, l * 4 + c + 3)
                        dst = hid[:, Y_SLOT["b"] + c]
                        dve.scalar_tensor_tensor(dst[:, 1, :], cf_out[:, c, :], 0.5, fp(dst[:, 0, :]),
                                                 ALU.mult, ALU.subtract).then_inc(y_ready, 1)
                    h, r = divmod(t - TRAIL - VALUES_AFTER[2] - 2, TC)
                    if r == 0 and 0 <= h < 2 * HEADS:
                        dst = hid[head_rows(h), Y_SLOT["c"] + h // 2]
                        dve.wait_ge(pv_hi, l * 2 * HEADS + h + 1)
                        dve.tensor_tensor(dst[:, 1, :], ps[head_rows(h), bank_of(G_PV + h), :], fp(dst[:, 0, :]),
                                          ALU.subtract).then_inc(evac, 1)

                def updates(ev, n0, normed):
                    event_var(ev, l)
                    dve.wait_ge(y_evac, l * N_YEVAC + n0 + KD)
                    scale_ready(ev, l)
                    for k in range(KD + 1):
                        if k < KD:
                            st.mark(dve.tensor_tensor(y[:, k, 1, :], y[:, k, 1, :], ps[:, STAT, :], ALU.mult))
                        if k == 1:
                            normed(0)
                        if k < KD:
                            st.wait()
                            dve.tensor_tensor(x[:, k, :], x[:, k, :], y[:, k, 1, :], ALU.add).then_inc(x_done, 1)
                        if k >= 2:
                            normed(k - 1)

                dve.wait_ge(lo_done, l * NU + U_OUT + LEAD)
                for m in range(KD):
                    split_lo(dve, U_OUT + m + LEAD, l)
                dve.tensor_copy(gain_next[:, :],
                                vec_all[:, (l + 1) % DEPTH, VC["norm_mix_pre"]:VC["norm_mix_pre"] + KD])\
                   .then_inc(gain_set, 1)
                dve.memset(e_g[:, 0:FFN_TAPS - 1], 0.0)
                st.mark(dve.memset(e_v[:, 0:FFN_TAPS - 1], 0.0))
                updates("post_mix", 0, lambda k: normed_lo(col("norm_ffn_pre", k), k, KD + k, l))
                split_lo(dve, U_UP + LEAD, l)
                split_lo(dve, U_UP + LEAD + 1, l)
                event_var("pre_ffn", l)
                split_lo(dve, U_UP + LEAD + 2, l)
                scale_ready("pre_ffn", l)

                def taps(dst, src, w, last):
                    st.mark(dve.tensor_scalar(dst, src[:, 0:T], w(0), None, ALU.mult))
                    for j in range(1, FFN_TAPS):
                        st.wait()
                        ins = dve.scalar_tensor_tensor(dst, src[:, j:j + T], w(j), dst, ALU.mult, ALU.add)
                        if j == FFN_TAPS - 1 and last is not None:
                            ins.then_inc(last, 1)
                        else:
                            st.mark(ins)

                def hidden_lo(p):
                    dve.wait_ge(f_hi, l * NF + p + 1)
                    dve.tensor_tensor(hid[:, p, 1, :], c_v[:, :], fp(hid[:, p, 0, :]), ALU.subtract)\
                       .then_inc(f_ready, 1)

                def ffn_body(i, first=False, second=False):
                    for jj in range(2):
                        p = i * 2 + jj
                        for half, (e, cc) in enumerate(((e_g, c_g), (e_v, c_v))):
                            j = 2 * jj + half
                            u = U_UP + LEAD + (j if not first else 3 if j < 2 else 4)
                            if j in ((1, 3) if first else (1, 2, 3) if second else (0, 1, 2, 3)):
                                dve.wait_ge(hi_done, l * NU + i * 4 + u + 1)
                                dve.tensor_tensor(wsp[:, u % SPLIT, 1, :], raw[:, u % RAW, :],
                                                  fp(wsp[:, u % SPLIT, 0, :]), ALU.subtract).then_inc(lo_done, 1)
                            dve.wait_ge(group_done, l * NG + i * 4 + G_UP + j + 1)
                            dve.tensor_tensor(e[:, FFN_TAPS - 1:], ps[:, bank_up(j, first), :], scale_main[:, :], ALU.mult)\
                               .then_inc(evac, 1)
                            if half == 0 and not (first and jj == 0):
                                hidden_lo(p - 1)
                            own(evac, l * N_EVAC + i * 4 + G_OUT + j + 1)

                            def w(k):
                                a = VC["conv_ffn"] + k * 2 * NF + half * NF
                                return vec[:, bass.ds(p + a, 1)]

                            if half and not (first and jj == 0):
                                own(f_ready, l * NF + p)
                            taps(cc[:, :], e, w, c_gate if half == 0 else None)
                        dve.wait_ge(tanh_done, l * NF + p + 1)
                        st.mark(dve.scalar_tensor_tensor(th[:, :], th[:, :], 1.0, c_g[:, :], ALU.add, ALU.mult))
                        st.wait()
                        dve.scalar_tensor_tensor(c_v[:, :], th[:, :], 0.5, c_v[:, :], ALU.mult, ALU.mult)\
                           .then_inc(f_done, 1)

                n0 = st.n
                ffn_body(0, first=True)
                per_body = st.n - n0
                ffn_body(1, second=True)
                with dve.Fori(2, NF // 2) as i:
                    st.base, st.n = l * V_STEPS + i * per_body, n0
                    ffn_body(i)
                    assert st.n == n0 + per_body
                st.base, st.n = l * V_STEPS, n0 + per_body * (NF // 2)

                for u in range(U_DOWN + LEAD, NU + LEAD):
                    dve.wait_ge(hi_done, l * NU + u + 1)
                    dve.tensor_tensor(wsp[:, u % SPLIT, 1, :], raw[:, u % RAW, :],
                                      fp(wsp[:, u % SPLIT, 0, :]), ALU.subtract).then_inc(lo_done, 1)
                    if u == U_DOWN + LEAD:
                        hidden_lo(NF - 1)
                updates("post_ffn", KD, lambda k: normed_lo(gain_next[:, k:k + 1], k, k, l + 1))
                assert st.n == V_STEPS, st.n

            for k in range(1, KD, 2):
                dve.wait_ge(ot_done, k + 1)
                dve.tensor_copy(out_tok[:, :, k * P:(k + 1) * P],
                                ps[:, RING[k % len(RING)], :].rearrange("p (c f) -> p c f", f=P))\
                   .then_inc(out_set[1], 1)

        @block.scalar
        def _(act):
            act.preload_act_table_set("exp_and_others")
            act.dma_start(rows[0:HALFROWS, :, :, :],
                          inp["vectors"].rearrange("l (t r) c -> r l t c", t=2)).then_inc(rows_in, 16)
            rope_v = [r.rearrange("s p t -> p s t") for r in rope_tables]
            act.dma_start(rope[:, :, :], rope_v[0]).then_inc(rope_in, 16)
            def square(ev, k, src, l):
                if k == 0 and not (isinstance(l, int) and l == 0):
                    act.wait_ge(stat_done, l * NEV + EVENTS.index(ev))
                elif k >= 2:
                    act.wait_ge(add_done, l * NADD + adds_before(ev) + k - 1)
                act.activation(sq[:, min(k, 1), :], src, ACT.Square).then_inc(sq_done, 1)

            def copy_scale(ev, l):
                act.wait_ge(spread_done, l * NEV + EVENTS.index(ev) + 1)
                act.activation(scale_main[:, :], ps[:, STAT, :], ACT.Copy).then_inc(scale_done, 1)

            def group_ready(g, l):
                act.wait_ge(group_done, l * NG + g + 1)

            def normed_hi(gain, k, n, l):
                act.wait_ge(x_done, l * 2 * KD + n + 1)
                act.activation(xn[:, k, 0, :], x[:, k, :], ACT.Copy, scale=gain).then_inc(xh_done, 1)

            act.wait_ge(gain_set, 1)
            for k in range(KD):
                normed_hi(gain_next[:, k:k + 1], k, k, 0)
                square("pre_mix", k, x[:, k, :], 0)
                if k + 1 in SPLIT_AFTER:
                    split_hi(act, SPLIT_AFTER.index(k + 1), 0, first=True)
            with act.Fori(0, DEPTH) as l:
                act.wait_ge(vec_set, l + 1)
                for u in (3, 4, 5):
                    split_hi(act, u, l)
                copy_scale("pre_mix", l)

                def rot_hi_part(n):
                    act.wait_ge(rot_done, l * 8 + n + 1)
                    if n < 4:
                        dst, e = hid[:, (QM, KM, QM + 1, KM + 1)[n]], rot[:, n % 2, :]
                    else:
                        dst, e = xn[0:MLA_QK, n - 4], ml_rot[0:MLA_QK, n - 4, :]
                    act.activation(dst[:, 0, :], e, ACT.Copy).then_inc(rot_hi, 1)

                def group_a_hi(c):
                    act.wait_ge(sc_val, l * 2 + c + 1)
                    act.activation(hid[:, Y_SLOT["a"] + c, 0, :], sc_w[:, :], ACT.Copy).then_inc(y_hi, 1)

                cf_j = 0
                for g in range(G_MK):
                    if g >= 3:
                        split_hi(act, g + LEAD, l)
                    if g in (0, 2):
                        c = g // 2
                        act.wait_ge(evac, l * N_EVAC + g + 1)
                        act.activation(rot[:, c, :], rot[:, c, :], ACT.Tanh, scale=0.5).then_inc(cf_tanh, 1)
                    if G_QK < g <= G_V:
                        rot_hi_part(g - 1 - G_QK)
                    if G_V < g <= G_V + 2:
                        act.wait_ge(mix_set, l + 1)
                        group_ready(g - 1, l)
                        for j in range(2):
                            c = 2 * (g - 1 - G_V) + j
                            act.activation(vm[:, 0, c, :], ps[:, bank_of(g - 1), j * GW:(j + 1) * GW], ACT.Copy,
                                           scale=rstd_mix[:, c:c + 1]).then_inc(val_hi, 1)
                    for _ in range(CF_SCALAR.get(g, 0)):
                        j, cf_j = cf_j, cf_j + 1
                        if j == 0:
                            act.wait_ge(cf_u_set, l + 1)
                            act.activation(cf_out[:, 1, :], cf_u[:, 1, 0:T], ACT.Identity, scale=col("conv_b", 1),
                                           bias=col("conv_b_bias", 1)).then_inc(cf_prod, 1)
                            continue
                        if j > 2:
                            act.wait_ge(cf_sum, l * (CF_TAPS - 1) + j - 2)
                        act.activation(cf_tmp[:, j % 2, :], cf_u[:, 1, j:j + T], ACT.Copy,
                                       scale=col("conv_b", 2 * j + 1)).then_inc(cf_prod, 1)
                    if g == G_V + 1:
                        act.wait_ge(rot_done, l * 8 + 4)
                        act.dma_start(rope[:, :, :], rope_v[1]).then_inc(rope_in, 16)
                    if g == G_KR + 1:
                        act.wait_ge(kr_done, l + 1)
                        act.activation(kr[DH:MLA_QK, 0, :], rot[DH:MLA_QK, 0, :], ACT.Copy).then_inc(kr_hi, 1)
                    if g == 12:
                        act.wait_ge(evac, l * N_EVAC + G_CKV + 1)
                        square("ckv", 0, lat[:, 3, :], l)
                    if g == 17:
                        act.wait_ge(lat_norm, l * 4 + 1)
                        act.activation(hid[:, CKVN, 0, :], lat[:, 3, :], ACT.Copy, scale=col("mla_kv_norm"))\
                           .then_inc(lat_hi, 1)
                    if g == 16:
                        for j in range(3):
                            act.wait_ge(evac, l * N_EVAC + G_CQ + j + 1)
                            square("cq", j, lat[:, j, :], l)
                    if g == 17:
                        group_a_hi(0)
                    if g == 20:
                        for j in range(3):
                            act.wait_ge(lat_norm, l * 4 + j + 2)
                            act.activation(hid[:, CQN + j, 0, :], lat[:, j, :], ACT.Copy,
                                           scale=col("mla_q_norm", j)).then_inc(lat_hi, 1)
                    if g == 20:
                        for c in range(2):
                            act.wait_ge(cf_cent, l * 2 + c + 1)
                            square("ln", c, cf_out[:, c, :], l)
                group_a_hi(1)

                act.wait_ge(group_done, l * NG + G_MK)
                for h in range(HEADS):
                    group_ready(G_MK + h, l)
                    act.activation(ml_k[h][0:DH, 0, :], ps[0:DH, bank_of(G_MK + h), :], ACT.Copy).then_inc(kn_hi, 1)
                for half in range(2):
                    group_ready(G_MV + half, l)
                    act.activation(vl[:, 0, 2 * half:2 * half + 2, :],
                                   ps[:, bank_of(G_MV + half), :].rearrange("p (c d) -> p c d", c=2),
                                   ACT.Copy).then_inc(val_hi, 1)
                act.wait_ge(kr_lo, l + 1)
                for s in range(2):
                    act.activation(xn[DH:MLA_QK, HEADS:2 * HEADS, s, :],
                                   fp(kr[DH:MLA_QK, s, :]).unsqueeze(1).to_broadcast([MLA_ROPE, HEADS, T]),
                                   ACT.Copy).then_inc(kr_spread, 1)
                rot_hi_part(4)

                for t in range(N_ATT + ATT_TAIL):
                    if TRAIL <= t < N_ATT + TRAIL:
                        s = t - TRAIL
                        h, c = divmod(s, TC)
                        if c == 0 and h >= 2:
                            group_ready(G_PV + h - 2, l)
                        act.wait_ge(pt_done, l * N_ATT + s + 1)
                        act.activation(pt_of(h, c, 0),
                                       ps[:, PT_BANKS[s % 2], 0:(c + 1) * P].rearrange("p (k t) -> p k t", t=P),
                                       ACT.Copy).then_inc(pt_hi, 1)
                    if t < N_ATT:
                        n = (t % TC + 1) * P
                        if t >= NPROB:
                            act.wait_ge(pt_done, l * N_ATT + t - NPROB + 1)
                        if t == 0:
                            act.wait_ge(kr_spread, l * 2 + 2)
                        act.wait_ge(negmax_done, l * N_ATT + t + 1)
                        act.activation(prob[:, t % NPROB, 0:n], sm[:, t % 2, 0:n], ACT.Exp, bias=negmax[:, t:t + 1],
                                       scale=MOBA_SCALE if t < N_ATT // 2 else MLA_SCALE,
                                       accum_out=rowsum[:, t:t + 1]).then_inc(exp_done, 1)
                    if t in (3, 4):
                        c = t - 3
                        act.wait_ge(cf_norm, l * 2 + c + 1)
                        act.activation(cf_out[:, c, :], cf_out[:, c, :], ACT.Identity, scale=col("ln_b_gain", c),
                                       bias=col("ln_b_bias", c)).then_inc(cf_affine, 1)
                        act.wait_ge(cf_affine, l * 2 + c + 1)
                        act.activation(cf_th[:, c, :], cf_out[:, c, :], ACT.Tanh, scale=0.5).then_inc(cf_swish, 1)
                    if t in (6, 7):
                        c = t - 6
                        act.wait_ge(cf_val, l * 2 + c + 1)
                        act.activation(hid[:, Y_SLOT["b"] + c, 0, :], cf_out[:, c, :], ACT.Copy, scale=0.5)\
                           .then_inc(y_hi, 1)
                    if t in (1, 5, 8):
                        rot_hi_part({1: 5, 5: 6, 8: 7}[t])
                    if t in (12, 16, 20):
                        split_hi(act, U_OUT + (t - 12) // 4, l)
                    if t == 8:
                        act.wait_ge(rot_done, l * 8 + 8)
                        act.dma_start(rope[:, :, :], rope_v[0]).then_inc(rope_in, 16)
                    h, r = divmod(t - TRAIL - VALUES_AFTER[2] - 1, TC)
                    if r == 0 and 0 <= h < 2 * HEADS:
                        rr = slice(DH * (h % 2), DH * (h % 2) + DH)
                        group_ready(G_PV + h, l)
                        act.activation(hid[rr, Y_SLOT["c"] + h // 2, 0, :], ps[rr, bank_of(G_PV + h), :], ACT.Copy)\
                           .then_inc(pv_hi, 1)

                for m in range(KD):
                    split_hi(act, U_OUT + m + LEAD, l)
                    group_ready(G_OUT + m, l)
                    bank = bank_of(G_OUT + m)
                    square("post_mix", m, ps[:, bank, :], l)
                    act.activation(y[:, m, 1, :], ps[:, bank, :], ACT.Copy, scale=col("norm_mix_post", m))\
                       .then_inc(y_evac, 1)
                for k in range(KD):
                    normed_hi(col("norm_ffn_pre", k), k, KD + k, l)
                    square("pre_ffn", k, x[:, k, :], l)
                for u in range(U_UP + LEAD, U_UP + LEAD + 3):
                    split_hi(act, u, l)
                copy_scale("pre_ffn", l)

                def hidden_hi(p):
                    act.wait_ge(f_done, l * NF + p + 1)
                    act.activation(hid[:, p, 0, :], c_v[:, :], ACT.Copy).then_inc(f_hi, 1)

                def split_up(i, j):
                    u = U_UP + j + LEAD
                    act.wait_ge(raw_in[u % RAW], l * (NU // RAW * 16) + i * 32 + 16 * (u // RAW + 1))
                    act.wait_ge(group_done, l * NG + i * 4 + G_UP + j)
                    act.activation(wsp[:, u % SPLIT, 0, :], raw[:, u % RAW, :], ACT.Copy).then_inc(hi_done, 1)

                def ffn_body(i, first=False, second=False):
                    for jj in range(2):
                        p = i * 2 + jj
                        if not first and not (second and jj == 0):
                            split_up(i, 2 * jj)
                        if not (first and jj == 0):
                            hidden_hi(p - 1)
                        split_up(i, (3 + jj) if first else 2 * jj + 1)
                        act.wait_ge(c_gate, l * NF + p + 1)
                        act.activation(th[:, :], c_g[:, :], ACT.Tanh, scale=0.5).then_inc(tanh_done, 1)

                ffn_body(0, first=True)
                ffn_body(1, second=True)
                with act.Fori(2, NF // 2) as i:
                    ffn_body(i)
                for n in range(3 * KD):
                    u = U_DOWN + n + LEAD
                    act.wait_ge(raw_in[u % RAW], l * (NU // RAW * 16) + 16 * (u // RAW + 1))
                    s, count, step = released(u - SPLIT)
                    act.wait_ge(s, l * step + count)
                    act.activation(wsp[:, u % SPLIT, 0, :], raw[:, u % RAW, :], ACT.Copy).then_inc(hi_done, 1)
                    if n == 0:
                        hidden_hi(NF - 1)
                    m, part = down_unit(n)
                    if part == 2:
                        group_ready(G_DOWN + m, l)
                        square("post_ffn", m, ps[:, m % 4, :], l)
                        act.activation(y[:, m, 1, :], ps[:, m % 4, :], ACT.Copy, scale=col("norm_ffn_post", m))\
                           .then_inc(y_evac, 1)
                act.wait_ge(gain_set, l + 2)
                for k in range(KD):
                    normed_hi(gain_next[:, k:k + 1], k, k, l + 1)
                    square("pre_mix", k, x[:, k, :], l + 1)

            for k in range(0, KD, 2):
                act.wait_ge(ot_done, k + 1)
                act.activation(out_tok[:, :, k * P:(k + 1) * P],
                               ps[:, RING[k % len(RING)], :].rearrange("p (c f) -> p c f", f=P),
                               ACT.Copy).then_inc(out_set[0], 1)



_WEIGHTS = ["x", "w_in", "w_uq", "w_ukv", "w_out", "w_ffn_up", "w_ffn_down"]
ROPE_THETA = 500000.0


def rope_table(dim, first, period, np):
    half = dim // 2
    inv = (1.0 / (np.float32(ROPE_THETA) ** (np.arange(0, dim, 2, dtype=np.float32) / np.float32(dim))))
    ang = np.arange(T, dtype=np.float32)[:, None] * inv.astype(np.float32)[None, :]
    table = np.zeros((2, P, T), np.float32)
    table[0] = 1.0
    for p0 in range(first, P, period):
        for j in range(dim):
            table[0, p0 + j] = np.cos(ang[:, j % half])
            table[1, p0 + j] = np.sin(ang[:, j % half]) * np.float32(-1.0 if j < half else 1.0)
    return table


def kernel(**inputs):
    import numpy as np
    import concourse.bacc as bacc
    from concourse.bass_utils import run_bass_kernel_spmd

    nc = bacc.Bacc("TRN2", target_bir_lowering=False, num_devices=1)
    arrays = {}

    def dram(name, a):
        arrays[name] = a
        return nc.dram_tensor(name, a.shape, mybir.dt.from_np(a.dtype), kind="ExternalInput").ap()

    inp = {name: dram(f"in_{name}", np.ascontiguousarray(inputs[name])) for name in _WEIGHTS}
    inp["vectors"] = dram("in_vectors", np.concatenate(
        [np.asarray(inputs[name]).reshape(DEPTH, -1, P) for name in [n for n, _, _ in SMALL] + ["conv_ffn"]], axis=1))
    tables = [dram("rope_moba", rope_table(DH // 4, 0, DH, np)), dram("rope_mla", rope_table(MLA_ROPE, DH, P, np))]
    out = nc.dram_tensor("out_x", (1, T, D), mybir.dt.float32, kind="ExternalOutput").ap()
    hybrid_trunk_kernel(nc, inp, tables, out)
    r = run_bass_kernel_spmd(nc, [arrays], core_ids=[0])
    return r.results[0]["out_x"]
```
